# Optimizing a Trainium2 kernel written in Bass

```python
import jax, jax.numpy as jnp
from jax import lax
import numpy as np

D_MODEL = 1024
BATCH = 1
SEQ = 512
DEPTH = 1

RWKV_WIDTH = 512
HEAD_DIM = 64
N_HEADS = RWKV_WIDTH // HEAD_DIM
CONV_WIDTH = D_MODEL - RWKV_WIDTH
CONV_KERNEL = 31
CONV_PAD = CONV_KERNEL // 2
DECAY_LORA = 64
ICLR_LORA = 64
GATE_LORA = 160
N_DIR = 2
D_FF = 2816
LN_EPS = 1e-5
GN_EPS = 64e-5
NORM_EPS = 1e-12
DEEPNORM_ALPHA = (2.0 * DEPTH) ** 0.25
DEEPNORM_BETA = (8.0 * DEPTH) ** -0.25

SHIFT_COLS = 3 * RWKV_WIDTH + N_DIR * DECAY_LORA + N_DIR * ICLR_LORA + GATE_LORA
IN_COLS = SHIFT_COLS + 2 * CONV_WIDTH
RWKV_SPLITS = (RWKV_WIDTH, 2 * RWKV_WIDTH, 3 * RWKV_WIDTH,
               3 * RWKV_WIDTH + N_DIR * DECAY_LORA,
               3 * RWKV_WIDTH + N_DIR * DECAY_LORA + N_DIR * ICLR_LORA)

kernel_name = "hybrid_rwkv7_conformer_conv_deepnorm_encoder"

def layer_norm(x, g, b, eps=LN_EPS):
    xf = x.astype(jnp.float32)
    mu = jnp.mean(xf, axis=-1, keepdims=True)
    var = jnp.mean(jnp.square(xf - mu), axis=-1, keepdims=True)
    return ((xf - mu) * lax.rsqrt(var + eps) * g + b).astype(x.dtype)

def swiglu_ffn(x, w_in, w_out):
    gate, up = jnp.split(x @ w_in, 2, axis=-1)
    return (jax.nn.silu(gate) * up) @ w_out

def centred_shift(p, mu_prev, mu_next):
    zero = jnp.zeros_like(p[:, :1])
    prev = jnp.concatenate([zero, p[:, :-1]], axis=1)
    nxt = jnp.concatenate([p[:, 1:], zero], axis=1)
    return p + mu_prev * (prev - p) + mu_next * (nxt - p)

def heads(z):
    return z.reshape(*z.shape[:-1], N_HEADS, HEAD_DIM)

def wkv7_bidir_scan(r, w, k, v, kk, a):
    def prep(z):
        z = jnp.stack([z[0], jnp.flip(z[1], axis=1)])
        return jnp.moveaxis(z, 2, 0)

    def both(z):
        return prep(jnp.stack([z, z]))

    xs = (both(r), prep(w), prep(k), both(v), both(kk), prep(a))

    def step(S, inp):
        rt, wt, kt, vt, kkt, at = inp
        sa = jnp.einsum('dbhij,dbhj->dbhi', S, -kkt)
        S = (S * wt[..., None, :] + sa[..., :, None] * (kkt * at)[..., None, :]
             + vt[..., :, None] * kt[..., None, :])
        y = jnp.einsum('dbhij,dbhj->dbhi', S, rt)
        return S, y

    b = r.shape[0]
    s0 = jnp.zeros((N_DIR, b, N_HEADS, HEAD_DIM, HEAD_DIM), jnp.float32)
    _, ys = lax.scan(step, s0, xs)
    y = ys[:, 0] + jnp.flip(ys[:, 1], axis=0)
    return jnp.moveaxis(y, 0, 1)

def rwkv7_mixer(ps, w0, w2, a0, a2, g2, k_k, k_a, r_k, lnx_g, lnx_b):
    ps = ps.astype(jnp.float32)
    bsz, t = ps.shape[0], ps.shape[1]
    r, k, v, wd, ad, gd = jnp.split(ps, RWKV_SPLITS, axis=-1)
    wd = wd.reshape(bsz, t, N_DIR, DECAY_LORA)
    ad = ad.reshape(bsz, t, N_DIR, ICLR_LORA)
    lw = jnp.einsum('btdr,drc->dbtc', jnp.tanh(wd), w2) + w0[:, None, None, :]
    decay = jnp.exp(-jnp.exp(-jax.nn.softplus(-lw) - 0.5))
    a = jax.nn.sigmoid(jnp.einsum('btdr,drc->dbtc', ad, a2) + a0[:, None, None, :])
    g = jax.nn.sigmoid(gd) @ g2
    kk = heads(k * k_k)
    kk = kk / jnp.maximum(jnp.linalg.norm(kk, axis=-1, keepdims=True), NORM_EPS)
    kd = k[None] * (1.0 + (a - 1.0) * k_a)
    rh, vh, kdh = heads(r), heads(v), heads(kd)
    y = wkv7_bidir_scan(rh, heads(decay), kdh, vh, kk, heads(a))
    mu = jnp.mean(y, axis=-1, keepdims=True)
    var = jnp.mean(jnp.square(y - mu), axis=-1, keepdims=True)
    yn = ((y - mu) * lax.rsqrt(var + GN_EPS)).reshape(bsz, t, RWKV_WIDTH) * lnx_g + lnx_b
    bonus = jnp.sum(rh[None] * kdh * r_k, axis=(0, -1))[..., None] * vh
    return (yn + bonus.reshape(bsz, t, RWKV_WIDTH)) * g

def conformer_conv(pc, dw, db, ln_g, ln_b):
    u = pc[..., :CONV_WIDTH] * jax.nn.sigmoid(pc[..., CONV_WIDTH:])
    y = lax.conv_general_dilated(u, dw[:, None, :].astype(u.dtype), window_strides=(1,),
                                 padding=[(CONV_PAD, CONV_PAD)],
                                 dimension_numbers=('NWC', 'WIO', 'NWC'),
                                 feature_group_count=CONV_WIDTH) + db
    return jax.nn.silu(layer_norm(y, ln_g, ln_b))

def setup_inputs(seed: int = 0) -> dict:
    key = jax.random.key(seed)
    ks = jax.random.split(key, 32)
    L, D, C = DEPTH, D_MODEL, RWKV_WIDTH
    f32 = jnp.float32

    def nrm(k, shape, scale):
        return jax.random.normal(k, shape, f32) * scale

    col_scale = jnp.ones((IN_COLS,), f32).at[2 * C:3 * C].set(DEEPNORM_BETA)
    return {
        "x": nrm(ks[0], (BATCH, SEQ, D), 1.0),
        "ffn1_w_in": nrm(ks[1], (L, D, 2 * D_FF), D ** -0.5 * DEEPNORM_BETA),
        "ffn1_w_out": nrm(ks[2], (L, D_FF, D), D_FF ** -0.5 * DEEPNORM_BETA),
        "w_in": nrm(ks[3], (L, D, IN_COLS), D ** -0.5) * col_scale,
        "mu_prev": jax.random.uniform(ks[4], (L, SHIFT_COLS), f32, 0.0, 0.4),
        "mu_next": jax.random.uniform(ks[5], (L, SHIFT_COLS), f32, 0.0, 0.4),
        "w0": jax.random.uniform(ks[6], (L, N_DIR, C), f32, -3.0, 1.0),
        "w2": nrm(ks[7], (L, N_DIR, DECAY_LORA, C), 0.1 * DECAY_LORA ** -0.5),
        "a0": nrm(ks[8], (L, N_DIR, C), 0.1),
        "a2": nrm(ks[9], (L, N_DIR, ICLR_LORA, C), 0.5 * ICLR_LORA ** -0.5),
        "g2": nrm(ks[10], (L, GATE_LORA, C), GATE_LORA ** -0.5),
        "k_k": 0.85 + nrm(ks[11], (L, C), 0.05),
        "k_a": 1.0 + nrm(ks[12], (L, C), 0.05),
        "r_k": nrm(ks[13], (L, N_HEADS, HEAD_DIM), 0.1),
        "lnx_g": 1.0 + nrm(ks[14], (L, C), 0.05),
        "lnx_b": nrm(ks[15], (L, C), 0.02),
        "conv_dw": nrm(ks[16], (L, CONV_KERNEL, CONV_WIDTH), CONV_KERNEL ** -0.5),
        "conv_b": nrm(ks[17], (L, CONV_WIDTH), 0.02),
        "conv_ln_g": 1.0 + nrm(ks[18], (L, CONV_WIDTH), 0.05),
        "conv_ln_b": nrm(ks[19], (L, CONV_WIDTH), 0.02),
        "w_out": nrm(ks[20], (L, D, D), D ** -0.5 * DEEPNORM_BETA),
        "ffn2_w_in": nrm(ks[21], (L, D, 2 * D_FF), D ** -0.5 * DEEPNORM_BETA),
        "ffn2_w_out": nrm(ks[22], (L, D_FF, D), D_FF ** -0.5 * DEEPNORM_BETA),
        "ln1_g": 1.0 + nrm(ks[23], (L, D), 0.05),
        "ln1_b": nrm(ks[24], (L, D), 0.02),
        "ln2_g": 1.0 + nrm(ks[25], (L, D), 0.05),
        "ln2_b": nrm(ks[26], (L, D), 0.02),
        "ln3_g": 1.0 + nrm(ks[27], (L, D), 0.05),
        "ln3_b": nrm(ks[28], (L, D), 0.02),
    }

def reference(x, ffn1_w_in, ffn1_w_out, w_in, mu_prev, mu_next, w0, w2, a0, a2, g2,
              k_k, k_a, r_k, lnx_g, lnx_b, conv_dw, conv_b, conv_ln_g, conv_ln_b, w_out,
              ffn2_w_in, ffn2_w_out, ln1_g, ln1_b, ln2_g, ln2_b, ln3_g, ln3_b):
    for l in range(DEPTH):
        x = layer_norm(DEEPNORM_ALPHA * x + 0.5 * swiglu_ffn(x, ffn1_w_in[l], ffn1_w_out[l]),
                       ln1_g[l], ln1_b[l])
        p = x @ w_in[l]
        ps = centred_shift(p[..., :SHIFT_COLS], mu_prev[l], mu_next[l])
        y_rwkv = rwkv7_mixer(ps, w0[l], w2[l], a0[l], a2[l], g2[l], k_k[l], k_a[l],
                             r_k[l], lnx_g[l], lnx_b[l]).astype(x.dtype)
        y_conv = conformer_conv(p[..., SHIFT_COLS:], conv_dw[l], conv_b[l],
                                conv_ln_g[l], conv_ln_b[l])
        mix = jnp.concatenate([y_rwkv, y_conv], axis=-1) @ w_out[l]
        x = layer_norm(DEEPNORM_ALPHA * x + mix, ln2_g[l], ln2_b[l])
        x = layer_norm(DEEPNORM_ALPHA * x + 0.5 * swiglu_ffn(x, ffn2_w_in[l], ffn2_w_out[l]),
                       ln3_g[l], ln3_b[l])
    return x


_drawn_inputs = setup_inputs


def setup_inputs(seed=0):
    import zlib

    import numpy as np

    out = dict(_drawn_inputs(seed))
    spreads = {}
    factors = {'w2': 8.0,
     'a0': 7.607,
     'k_k': 40.363,
     'k_a': 5.566,
     'lnx_g': 6.515,
     'lnx_b': 31.796,
     'conv_b': 7.473,
     'conv_ln_g': 4.959,
     'conv_ln_b': 23.633,
     'ln2_b': 2.805,
     'ln3_b': 2.741}
    for name, (base, spread) in spreads.items():
        noise = np.random.default_rng([zlib.crc32(name.encode()), seed]).standard_normal(out[name].shape)
        drawn = base * np.exp(spread * noise) if base else spread * noise
        out[name] = __import__('jax').numpy.asarray(drawn.astype(out[name].dtype))
    for name, factor in factors.items():
        out[name] = (out[name] * factor).astype(out[name].dtype)
    return out
```

```python
from contextlib import ExitStack
import math

import concourse.bass as bass
from concourse import mybir

F32 = mybir.dt.float32
F32R = mybir.dt.float32r
U8 = mybir.dt.uint8
ALU = mybir.AluOpType
ACT = mybir.ActivationFunctionType

P = 128
SEQ = 512
D_MODEL = 1024
D_FF = 2816
WIDTH = 512
HEAD = 64
TAPS = 31
PAD = TAPS // 2
KT = D_MODEL // P
FT = D_FF // P
JT = WIDTH // P
CHUNK = 128
NC = SEQ // CHUNK
MID = CHUNK // 2 - 1
LEVELS = 7
ALPHA = 2.0 ** 0.25
LN_EPS = 1e-5
GN_EPS = 64e-5
NORM_EPS = 1e-12
KAPPA = math.exp(-0.5)

PROJ = [(w, j) for j in range(JT) for w in ("conv_gate", "conv_value")]
PROJ += [("wd", 0), ("ad", 0), ("gd", 0), ("gd", 1)]
PROJ += [("k", j) for j in range(JT)] + [("r", j) for j in range(JT)] + [("v", j) for j in range(JT)]
PROJ_BANKS = 4
FFN1_IN = 0
FFN1_OUT = FFN1_IN + 2 * FT
PROJ_IN = FFN1_OUT + FT
MIX_OUT = PROJ_IN + len(PROJ)
FFN2_IN = MIX_OUT + KT
FFN2_OUT = FFN2_IN + 2 * FT
N_ITEMS = FFN2_OUT + FT


def param_columns():
    at, col = {}, 0
    for name, n in (("ln1_g", KT), ("ln1_b", KT), ("ln2_g", KT), ("ln2_b", KT), ("ln3_g", KT), ("ln3_b", KT),
                    ("mu_prev", 16), ("mu_next", 16), ("w0", 2 * JT), ("a0", 2 * JT), ("k_k", JT), ("k_a", JT),
                    ("r_k", JT), ("lnx_g", JT), ("lnx_b", JT), ("conv_dw", TAPS * JT), ("conv_b", JT),
                    ("conv_ln_g", JT), ("conv_ln_b", JT)):
        at[name] = col
        col += n
    return at, col


PAR, N_PAR = param_columns()
MU = {("r", j): j for j in range(4)} | {("k", j): 4 + j for j in range(4)} | {("v", j): 8 + j for j in range(4)}
MU |= {("wd", 0): 12, ("ad", 0): 13, ("gd", 0): 14, ("gd", 1): 15}


def encoder_block(nc, x_t, weights, params, lora, gate_tail, ident_c, head_ones_c, tri_c, level_c, out_t):
    spill = nc.dram_tensor("x1_spill", (P, KT * SEQ), F32, kind="Internal").ap()
    with ExitStack() as ctx:
        def sb(name, cols, dt=F32):
            return ctx.enter_context(nc.sbuf_tensor(name, [P, cols], dt))

        def sem(name):
            return ctx.enter_context(nc.semaphore(name))

        par = sb("par", N_PAR)
        own = sb("own", 16 + JT)
        ident = sb("ident", P)
        ones = sb("ones", P)
        head_ones = sb("head_ones", P)
        tri = sb("tri", 2 * 512)
        level = sb("level", 2 * LEVELS * P, U8)

        eps = [sb(f"eps{n}", 1) for n in range(4)]
        h_reset = sb("h_reset", SEQ)

        base = (nc.sbuf_base + 63) // 64 * 64

        def at(name, offset, cols, dt=F32):
            return nc.alloc_sbuf_tensor_at(name, [P, cols], dt, offset=base + offset)

        raw = [at(f"w_raw{s}", 4096 * s, 1024) for s in range(2)]
        w_hi = [at(f"w_hi{s}", 8192 + 4096 * s, 1024, F32R) for s in range(2)]
        w_lo = [at(f"w_lo{s}", 16384 + 4096 * s, 1024, F32R) for s in range(2)]
        x_hi = at("x_hi", 28672, KT * SEQ, F32R)
        x_lo = at("x_lo", 45056, KT * SEQ, F32R)
        x32 = at("x32", 61440, KT * SEQ)
        h_hi = at("h_hi", 77824, FT * SEQ, F32R)
        h_lo = at("h_lo", 122880, FT * SEQ, F32R)
        sig = at("sig", 167936, 2 * SEQ)
        h_raw = at("h_raw", 172032, 2 * SEQ)
        y_ln = at("y_ln", 77824, KT * SEQ)
        sq_ln = at("sq_ln", 94208, KT * SEQ)
        std = at("std", 176128, SEQ)
        rstd = at("rstd", 178176, SEQ)
        level_f = at("level_f", 180224, 2 * LEVELS * P)
        k_t = at("k_t", 94208, JT * SEQ)
        r_t = at("r_t", 102400, JT * SEQ)
        v_t = at("v_t", 110592, JT * SEQ)
        kk_t = at("kk_t", 118784, JT * SEQ)
        ULEN = SEQ + 2 * PAD
        u_t = at("u_t", 126976, JT * ULEN)
        conv_t = at("conv_t", 135680, JT * SEQ)
        wag_t = at("wag_t", 143872, 4 * SEQ)
        lora_s = at("lora_s", 152064, 4 * 512)
        bonus_t = at("bonus_t", 160256, JT * SEQ)
        gate_t = at("gate_t", 168448, JT * SEQ)
        tmp = at("tmp", 176640, 10 * SEQ)
        e_t = at("e_t", 197120, 2 * SEQ)
        fac = at("fac", 201216, 2 * JT * (NC - 1))
        qr = at("qr", 28672, 2 * JT * 2 * SEQ)
        b_m = at("b_m", 61440, 2 * JT * SEQ)
        k_m = at("k_m", 77824, 2 * JT * SEQ)
        a_t = at("a_t", 94208, 2 * 2 * 4 * 512)
        v_tok = at("v_tok", 126976, NC * WIDTH)
        y_t = at("y_t", 143872, JT * SEQ)
        inv = at("inv", 152064, 2 * 2 * 4 * P)
        x_i = at("x_i", 176640, 2 * 4 * P)
        y_i = at("y_i", 180736, 2 * 4 * P)
        b_tok = at("b_tok", 184832, 4 * P)
        k_tok = at("k_tok", 186880, 4 * P)
        w_c = at("w_c", 188928, 8 * HEAD)
        u_c = at("u_c", 190976, 8 * HEAD)
        s_new = at("s_new", 193024, 4 * P)
        state = at("state", 197120, 8 * P)
        t_i = at("t_i", 0, LEVELS * 2 * 4 * P)
        assert base + 201312 <= nc.sbuf_usable_end, (base, nc.sbuf_usable_end)

        ps = [ctx.enter_context(nc.psum_tensor(f"bank{i}", [P, 512], F32)) for i in range(8)]

        def ch(t, j, n=1):
            return t[:, j * SEQ:(j + n) * SEQ]

        def col(name, j=0):
            return par[:, PAR[name] + j:PAR[name] + j + 1]

        consts_loaded = sem("consts_loaded")
        x_loaded = sem("x_loaded")
        lora_loaded = sem("lora_loaded")
        raw_landed = [sem(f"raw_landed{s}") for s in range(2)]
        hi_ready = sem("hi_ready")
        lo_ready = sem("lo_ready")
        weights_used = sem("weights_used")
        pairs_free = sem("pairs_free")
        sig_ready = sem("sig_ready")
        gated = sem("gated")
        h_high = sem("h_high")
        h_ready = sem("h_ready")
        x_high = sem("x_high")
        x_low = sem("x_low")
        ln_in = sem("ln_in")
        ln_sum = sem("ln_sum")
        ln_centered = sem("ln_centered")
        ln_squared = sem("ln_squared")
        ln_var = sem("ln_var")
        ln_std = sem("ln_std")
        ln_rstd = sem("ln_rstd")
        ln_norm = sem("ln_norm")
        ln_out = sem("ln_out")
        ones_set = sem("ones_set")
        eps_set = sem("eps_set")
        own_set = sem("own_set")
        pads_set = sem("pads_set")
        presets = sem("presets")
        spilled = sem("spilled")
        reloaded = sem("reloaded")
        proj_free = [sem(f"proj_free{b}") for b in range(PROJ_BANKS)]
        proj_part = sem("proj_part")
        vec = sem("vec")
        act_own = sem("act_own")
        tile_done = sem("tile_done")
        conv_done = sem("conv_done")
        cn_sum, cn_cent, cn_sq, cn_var, cn_std, cn_norm, cn_z, cn_sig, conv_out = (
            sem(n) for n in ("cn_sum", "cn_cent", "cn_sq", "cn_var", "cn_std", "cn_norm", "cn_z", "cn_sig", "conv_out"))
        kk_in, kk_sq, kk_ss, kk_norm, kk_ready = (sem(n) for n in ("kk_in", "kk_sq", "kk_ss", "kk_norm", "kk_ready"))
        act_in, lora_mm, lora_act, gate_mm, gate_out = (
            sem(n) for n in ("act_in", "lora_mm", "lora_act", "gate_mm", "gate_out"))
        cum_ready, exp_ready, exp_used, mult_ready, prep_done, fac_in, fac_ready = (
            sem(n) for n in ("cum_ready", "exp_ready", "exp_used", "mult_ready", "prep_done", "fac_in", "fac_ready"))
        bonus_in, bonus_mm, bonus_out, vtok_mm, vtok_out = (
            sem(n) for n in ("bonus_in", "bonus_mm", "bonus_out", "vtok_mm", "vtok_out"))
        prod_mm, ring_free, prod_out = sem("prod_mm"), [sem("ring_free0"), sem("ring_free1")], sem("prod_out")
        lx_mm, t_ready, xn_mm, x_ready, yn_mm, y_ready = (
            [sem(f"{n}{d}") for d in range(2)] for n in ("lx_mm", "t_ready", "xn_mm", "x_ready", "yn_mm", "y_ready"))
        tok_mm, tok_out, w_mm, w_out_s, u_mm, u_out, y_mm, y_out, s_mm, s_sum, s_out = (
            sem(n) for n in ("tok_mm", "tok_out", "w_mm", "w_out_s", "u_mm", "u_out", "y_mm", "y_out", "s_mm",
                             "s_sum", "s_out"))
        gn_sum, gn_cent, gn_sq, gn_var, gn_std, gn_norm, gn_z, mix_high, mix_low, mix_in = (
            sem(n) for n in ("gn_sum", "gn_cent", "gn_sq", "gn_var", "gn_std", "gn_norm", "gn_z", "mix_high",
                             "mix_low", "mix_in"))
        stored = sem("stored")
        block = ctx.enter_context(nc.Block())

        turns = [(n, half) for n in range(NC) for half in range(2)]
        schedule = []
        for i in range(len(turns) + 1):
            prepare = [("products", i)] + [("level", i, m) for m in range(LEVELS)] if i < len(turns) else []
            run = [("tokens", i - 1), ("w", i - 1), ("u", i - 1), ("y", i - 1), ("state", i - 1)] if i else []
            while prepare or run:
                schedule += prepare[:1] + run[:1]
                prepare, run = prepare[1:], run[1:]

        def chunk(n, d):
            return n if d == 0 else NC - 1 - n

        def unit(half, d, u):
            return (half * 2 + d) * 4 + u

        def prod(half, d, u, what):
            c0 = unit(half, d, u) * 512 + {"qb": 0, "rb": 128, "qk": 256, "rk": 384}[what]
            return a_t[:, c0:c0 + 128]

        @block.sync
        def _(sp):
            sp.dma_start(x32[:, :], x_t).then_inc(x_loaded, 16)
            for s in range(2):
                sp.dma_start(raw[s][:, :], weights[s]).then_inc(raw_landed[s], 16)
            sp.dma_start(par[:, :], params).then_inc(consts_loaded, 16)
            sp.dma_start(ident[:, :], ident_c).then_inc(consts_loaded, 16)
            sp.dma_start(head_ones[:, :], head_ones_c).then_inc(consts_loaded, 16)
            sp.dma_start(tri[:, :], tri_c).then_inc(consts_loaded, 16)
            sp.dma_start(level_f[:, :], level_c).then_inc(consts_loaded, 16)

            def stream(first, last):
                with sp.Fori(first // 2, last // 2) as t:
                    for s in range(2):
                        g = t * 2
                        sp.wait_ge(hi_ready, g + (s - 1))
                        sp.wait_ge(lo_ready, g + (s - 1))
                        sp.dma_start(raw[s][:, :], weights[bass.ds(g + s, 1), :, :].rearrange("a p n -> (a p) n"))\
                            .then_inc(raw_landed[s], 16)

            stream(2, MIX_OUT)
            sp.wait_ge(y_ready[0], len(turns) * LEVELS)
            sp.wait_ge(y_ready[1], len(turns) * LEVELS)
            stream(MIX_OUT, N_ITEMS)
            for k in range(KT):
                sp.wait_ge(ln_out, 2 * KT + k + 1)
                sp.dma_start(out_t[:, k * SEQ:(k + 1) * SEQ], ch(x32, k)).then_inc(stored, 16)
            sp.wait_ge(stored, 16 * KT)

        @block.gpsimd
        def _(pool):
            pool.memset(ones[:, :], 1.0).then_inc(ones_set, 1)
            pool.wait_ge(ln_out, KT)
            pool.dma_start(spill, x32[:, :]).then_inc(spilled, 16)
            pool.wait_ge(weights_used, 2 + PROJ_IN)
            for j in range(JT):
                pool.memset(u_t[:, j * ULEN:j * ULEN + PAD], 0.0).then_inc(pads_set, 1)
                pool.memset(u_t[:, (j + 1) * ULEN - PAD:(j + 1) * ULEN], 0.0).then_inc(pads_set, 1)
            pool.dma_start(lora_s[:, 0:1536], lora).then_inc(lora_loaded, 16)
            pool.dma_start(lora_s[0:32, 1536:2048], gate_tail).then_inc(lora_loaded, 16)
            pool.wait_ge(weights_used, 2 + MIX_OUT)
            pool.wait_ge(consts_loaded, 80)
            for i in range(LEVELS * 2):
                pool.tensor_copy(t_i[:, i * 512:(i + 1) * 512].rearrange("p (u s) -> p u s", u=4),
                                 ident[:, :].rearrange("p (a s) -> p a s", a=1).to_broadcast([P, 4, P]))\
                    .then_inc(presets, 1)
            pool.wait_ge(y_mm, len(turns))
            pool.wait_ge(spilled, 16)
            pool.dma_start(x32[:, :], spill).then_inc(reloaded, 16)
            pool.wait_ge(reloaded, 16)

        @block.tensor
        def _(pe):
            pe.sem_inc(weights_used, 2)
            pe.sem_inc(pairs_free, 2)
            for b in range(PROJ_BANKS):
                pe.sem_inc(proj_free[b], 1)

            def three(bank, s, k, high, low, start, stop):
                wh, wl = w_hi[s][:, k * P:(k + 1) * P], w_lo[s][:, k * P:(k + 1) * P]
                pe.matmul(bank[:, :], wh, high, start=start, stop=False)
                pe.matmul(bank[:, :], wh, low, start=False, stop=False)
                return pe.matmul(bank[:, :], wl, high, start=False, stop=stop)

            def up_tile(g, s, bank):
                pe.wait_ge(hi_ready, g + 1)
                pe.wait_ge(lo_ready, g + 1)
                for k in range(KT):
                    last = three(bank, s, k, ch(x_hi, k), ch(x_lo, k), k == 0, k == KT - 1)
                last.then_inc(weights_used, 1)

            def down_tile(g, s, f, high, low, first, last_one, order=range(KT)):
                pe.wait_ge(hi_ready, g + 1)
                pe.wait_ge(lo_ready, g + 1)
                for d in order:
                    last = three(ps[d], s, d, high[:, bass.ds(f * SEQ, SEQ)], low[:, bass.ds(f * SEQ, SEQ)],
                                 first, last_one)
                last.then_inc(weights_used, 1)

            def swiglu(in0, out0, e):
                pe.wait_ge(x_high, KT * (1 + 2 * e))
                pe.wait_ge(x_low, KT * (1 + 2 * e))
                with pe.Fori(0, FT // 2) as i:
                    for s in range(2):
                        pe.wait_ge(pairs_free, i * 2 + (s + 1 + FT * e))
                        for part in range(2):
                            up_tile(i * 4 + (in0 + 2 * s + part), part, ps[2 * s + part])
                pe.wait_ge(h_ready, FT * (e + 1))
                down_tile(out0, 0, 0, h_hi, h_lo, True, False)
                with pe.Fori(0, FT // 2 - 1) as i:
                    for s in (1, 0):
                        down_tile(i * 2 + (out0 + 2 - s), s, i * 2 + (2 - s), h_hi, h_lo, False, False)
                down_tile(out0 + FT - 1, 1, FT - 1, h_hi, h_lo, False, True)

            def layer_sums(n):
                for k in range(KT):
                    pe.wait_ge(ln_in, KT * n + k + 1)
                    last = pe.matmul(ps[0][:, :], ones[:, :], ch(y_ln, k), start=k == 0, stop=k == KT - 1)
                last.then_inc(ln_sum, 1)
                for k in range(KT):
                    pe.wait_ge(ln_squared, KT * n + k + 1)
                    last = pe.matmul(ps[1][:, :], ones[:, :], ch(sq_ln, k), start=k == 0, stop=k == KT - 1)
                last.then_inc(ln_var, 1)

            pe.wait_ge(ones_set, 1)
            pe.wait_ge(consts_loaded, 80)
            swiglu(FFN1_IN, FFN1_OUT, 0)
            layer_sums(0)

            pe.wait_ge(x_high, KT * 2)
            pe.wait_ge(x_low, KT * 2)
            with pe.Fori(0, len(PROJ) // PROJ_BANKS) as i:
                for b in range(PROJ_BANKS):
                    pe.wait_ge(proj_free[b], i + 1)
                    up_tile(i * 4 + (PROJ_IN + b), b % 2, ps[b])

            for j in range(JT):
                pe.wait_ge(kk_sq, j + 1)
                pe.matmul(ps[4 + j][:, :], head_ones[:, :], ch(tmp, j), start=True, stop=True).then_inc(kk_ss, 1)
            pe.wait_ge(lora_loaded, 32)
            pe.wait_ge(act_in, 3)
            for b in range(PROJ_BANKS):
                pe.wait_ge(proj_free[b], len(PROJ) // PROJ_BANKS + 1)
            for j in range(JT):
                pe.wait_ge(gate_out, max(j - 1, 1)) if j >= 2 else None
                b = ps[j % 2]
                pe.matmul(b[:, :], lora_s[:, 1024 + j * P:1024 + (j + 1) * P], ch(wag_t, 2), start=True, stop=False)
                pe.matmul(b[:, :], lora_s[0:32, 1536 + j * P:1536 + (j + 1) * P], wag_t[0:32, 3 * SEQ:4 * SEQ],
                          start=False, stop=True).then_inc(gate_mm, 1)
            for j in range(JT):
                pe.wait_ge(conv_done, j + 1)
                last = pe.matmul(ps[2][:, :], ones[:, :], ch(conv_t, j), start=j == 0, stop=j == JT - 1)
            last.then_inc(cn_sum, 1)
            for j in range(JT):
                pe.wait_ge(cn_sq, j + 1)
                last = pe.matmul(ps[3][:, :], ones[:, :], ch(tmp, 4 + j), start=j == 0, stop=j == JT - 1)
            last.then_inc(cn_var, 1)
            pe.wait_ge(cn_std, 1)
            pe.wait_ge(kk_norm, JT)
            pe.wait_ge(gate_out, JT)
            for j in range(JT):
                for d in range(2):
                    for what in range(2):
                        rows = slice(64 * d, 64 * d + 64)
                        i = 4 * j + 2 * d + what
                        if j >= 1:
                            pe.wait_ge(lora_act, i - 3)
                        pe.matmul(ps[i % 4][:, :], lora_s[rows, 512 * what + j * P:512 * what + (j + 1) * P],
                                  wag_t[rows, what * SEQ:(what + 1) * SEQ], start=True, stop=True)\
                            .then_inc(lora_mm, 1)
            for j in range(JT):
                for c in range(NC):
                    last = pe.transpose(ps[4 + c][:, j * P:(j + 1) * P],
                                        v_t[:, j * SEQ + c * CHUNK:j * SEQ + (c + 1) * CHUNK], ident[:, :])
            last.then_inc(vtok_mm, 1)
            pe.wait_ge(lora_act, 16)
            for j in range(JT):
                pe.wait_ge(bonus_in, j + 1)
                pe.matmul(ps[j][:, :], head_ones[:, :], ch(bonus_t, j), start=True, stop=True).then_inc(bonus_mm, 1)
            pe.wait_ge(bonus_out, JT)
            pe.wait_ge(vtok_out, NC)
            pe.wait_ge(prep_done, 2 * JT)
            pe.wait_ge(fac_ready, 1)

            rings = [0]
            head_rows = [slice(0, 64), slice(64, 128)]

            def ring():
                b, use = rings[0] % 2, rings[0] // 2
                rings[0] += 1
                if use:
                    pe.wait_ge(ring_free[b], use)
                return ps[b]

            def products(i):
                n, half = turns[i]
                for d in range(2):
                    for u in range(4):
                        j, rows, c = 2 * half + u // 2, head_rows[u % 2], chunk(n, d)
                        bank = ring()
                        c0 = ((d * JT + j) * NC + c) * 2 * CHUNK
                        t0 = (d * JT + j) * SEQ + c * CHUNK
                        q_and_r = qr[rows, c0:c0 + 2 * CHUNK]
                        pe.matmul(bank[:, 0:256], b_m[rows, t0:t0 + CHUNK], q_and_r, start=True, stop=True)
                        pe.matmul(bank[:, 256:512], k_m[rows, t0:t0 + CHUNK], q_and_r, start=True, stop=True)\
                            .then_inc(prod_mm, 1)

            def level_step(i, m):
                n, half = turns[i]
                done = i * LEVELS + m
                for d in range(2):
                    px = ps[2 + d]
                    if m == 0:
                        pe.wait_ge(prod_out, 8 * i + 4 * d + 4)
                        if i:
                            pe.wait_ge(x_ready[d], (LEVELS - 2) * i)
                            pe.wait_ge(t_ready[d], done)
                    else:
                        if m >= 2:
                            pe.wait_ge(x_ready[d], i * (LEVELS - 2) + m - 1)
                    for u in range(4):
                        o = px[:, u * P:(u + 1) * P]
                        if m == 0:
                            last = pe.transpose(o, prod(half, d, u, "qb"), ident[:, :])
                        else:
                            x_now = t_i if m == 1 else x_i
                            last = pe.matmul(o, prod(half, d, u, "qb"), x_now[:, (4 * d + u) * P:(4 * d + u + 1) * P],
                                             start=True, stop=True)
                    last.then_inc(lx_mm[d], 1)
                for d in range(2):
                    pe.wait_ge(t_ready[d], done + 1)
                    if done:
                        pe.wait_ge(y_ready[d], done)
                    px, py = ps[2 + d], ps[4 + d]

                    def t_of(u):
                        c0 = ((m * 2 + d) * 4 + u) * P
                        return t_i[:, c0:c0 + P]

                    y_now = [y_i[:, (4 * d + u) * P:(4 * d + u + 1) * P] for u in range(4)]
                    if 1 <= m < LEVELS - 1:
                        for u in range(4):
                            last = pe.matmul(px[:, u * P:(u + 1) * P], y_now[u], t_of(u), start=True, stop=True)
                        last.then_inc(xn_mm[d], 1)
                    for u in range(4):
                        o = py[:, u * P:(u + 1) * P]
                        if m == 0:
                            last = pe.transpose(o, t_of(u), ident[:, :])
                        else:
                            last = pe.matmul(o, t_of(u), y_now[u], start=True, stop=True)
                    last.then_inc(yn_mm[d], 1)

            def tokens(i):
                n, half = turns[i]
                if n == NC - 1:
                    return
                for t in (b_m, k_m):
                    bank = ring()
                    for d in range(2):
                        for jj in range(2):
                            t0 = (d * JT + 2 * half + jj) * SEQ + chunk(n, d) * CHUNK
                            last = pe.transpose(bank[:, (2 * d + jj) * P:(2 * d + jj + 1) * P],
                                                t[:, t0:t0 + CHUNK], ident[:, :])
                    last.then_inc(tok_mm, 1)

            pairs = [(d, jj) for d in range(2) for jj in range(2)]

            def pair_at(d, jj):
                return slice((2 * d + jj) * P, (2 * d + jj + 1) * P)

            def state_of(half, d, jj):
                return state[:, (4 * half + 2 * d + jj) * P:(4 * half + 2 * d + jj + 1) * P]

            def qr_of(i, d, jj, w):
                n, half = turns[i]
                c0 = (((d * JT + 2 * half + jj) * NC + chunk(n, d)) * 2 + w) * CHUNK
                return qr[:, c0:c0 + CHUNK]

            def head_at(d, u):
                return slice((4 * d + u) * HEAD, (4 * d + u + 1) * HEAD)

            def v_of(i, d, u, n_heads=1):
                n, half = turns[i]
                c0 = chunk(n, d) * WIDTH + (4 * half + u) * HEAD
                return v_tok[:, c0:c0 + n_heads * HEAD]

            def run_w(i):
                n, half = turns[i]
                if i:
                    pe.wait_ge(u_out, i)
                if i >= 2 and n:
                    pe.wait_ge(s_out, 4 * (i - 1))
                for d, jj in pairs:
                    if n:
                        pe.matmul(ps[6][:, pair_at(d, jj)], qr_of(i, d, jj, 0), state_of(half, d, jj),
                                  start=True, stop=True)
                    for u in (2 * jj, 2 * jj + 1):
                        last = pe.matmul(ps[6][:, head_at(d, u)], prod(half, d, u, "qk"), v_of(i, d, u),
                                         start=n == 0, stop=True, skip_group_check=True)
                last.then_inc(w_mm, 1)

            def run_u(i):
                n, half = turns[i]
                pe.wait_ge(w_out_s, i + 1)
                for d in range(2):
                    pe.wait_ge(y_ready[d], LEVELS * (i + 1))
                for d in range(2):
                    for u in range(4):
                        c0 = unit(half, d, u) * P
                        last = pe.matmul(ps[6][:, head_at(d, u)], inv[:, c0:c0 + P], w_c[:, head_at(d, u)],
                                         start=True, stop=True)
                last.then_inc(u_mm, 1)

            def run_y(i):
                n, half = turns[i]
                pe.wait_ge(u_out, i + 1)
                if i:
                    pe.wait_ge(s_sum, i) if turns[i - 1][0] < NC - 1 else pe.wait_ge(y_out, 2 * i)
                for d, jj in pairs:
                    if n:
                        pe.matmul(ps[7][:, pair_at(d, jj)], state_of(half, d, jj), qr_of(i, d, jj, 1),
                                  start=True, stop=True)
                    for u in (2 * jj, 2 * jj + 1):
                        o = ps[7][head_rows[u % 2], pair_at(d, jj)]
                        pe.matmul(o, u_c[:, head_at(d, u)], prod(half, d, u, "rb"), start=n == 0, stop=False,
                                  skip_group_check=True)
                        last = pe.matmul(o, v_of(i, d, u), prod(half, d, u, "rk"), start=False, stop=True,
                                         skip_group_check=True)
                last.then_inc(y_mm, 1)

            def run_state(i):
                n, half = turns[i]
                if n == NC - 1:
                    return
                pe.wait_ge(tok_out, 2 * (i + 1))
                pe.wait_ge(y_out, 2 * (i + 1))
                for d, jj in pairs:
                    o, t = ps[7][:, pair_at(d, jj)], pair_at(d, jj)
                    pe.matmul(o, b_tok[:, t], u_c[:, t], start=True, stop=False)
                    last = pe.matmul(o, k_tok[:, t], v_of(i, d, 2 * jj, 2), start=False, stop=True)
                last.then_inc(s_mm, 1)

            steps = {"products": products, "level": level_step, "tokens": tokens, "w": run_w, "u": run_u,
                     "y": run_y, "state": run_state}
            pe.wait_ge(presets, 2 * LEVELS)
            for what, *which in schedule:
                steps[what](*which)

            pe.wait_ge(y_out, 2 * len(turns))
            for j in range(JT):
                pe.matmul(ps[j][:, :], head_ones[:, :], ch(y_t, j), start=True, stop=True).then_inc(gn_sum, 1)
            for j in range(JT):
                pe.wait_ge(gn_sq, j + 1)
                pe.matmul(ps[4 + j][:, :], head_ones[:, :], ch(tmp, 4 + j), start=True, stop=True).then_inc(gn_var, 1)

            pe.wait_ge(gn_std, JT)
            for k in range(KT):
                pe.wait_ge(mix_high, KT)
                pe.wait_ge(mix_low, KT)
                down_tile(MIX_OUT + k, k % 2, k, x_hi, x_lo, k == 0, k == KT - 1)
            layer_sums(1)

            swiglu(FFN2_IN, FFN2_OUT, 1)
            layer_sums(2)

        @block.scalar
        def _(act):
            own_steps = [0]

            def step(ins):
                own_steps[0] += 1
                ins.then_inc(act_own, 1)
                act.wait_ge(act_own, own_steps[0])

            def high(g, s, turn):
                act.wait_ge(raw_landed[s], turn * 16 + 16)
                act.wait_ge(weights_used, g + 1)
                act.activation(w_hi[s][:, :], raw[s][:, :], ACT.Copy).then_inc(hi_ready, 1)

            def swiglu(in0, out0, e, last):
                with act.Fori(0, FT // 2) as i:
                    for s in range(2):
                        g = i * 4 + (in0 + 2 * s)
                        high(g + 2, 0, i * 2 + (in0 // 2 + s + 1))
                        act.wait_ge(weights_used, g + 3)
                        act.wait_ge(pairs_free, i * 2 + (s + 1 + FT * e))
                        act.activation(ch(sig, s), ps[2 * s][:, :], ACT.Sigmoid).then_inc(sig_ready, 1)
                        high(g + 3, 1, i * 2 + (in0 // 2 + s + 1))
                with act.Fori(0, FT // 2 - last) as i:
                    for s in range(2):
                        high(i * 2 + (out0 + 2 + s), s, i + (out0 // 2 + 1))

            def norm(n):
                for k in range(KT):
                    act.wait_ge(ln_centered, KT * n + k + 1)
                    act.activation(ch(sq_ln, k), ch(y_ln, k), ACT.Square).then_inc(ln_squared, 1)
                act.wait_ge(ln_var, n + 1)
                act.activation(std[:, :], ps[1][:, :], ACT.Sqrt, scale=1.0 / D_MODEL, bias=eps[n][:, :])\
                    .then_inc(ln_std, 1)
                for k in range(KT):
                    act.wait_ge(ln_norm, KT * n + k + 1)
                    gain = dict(scale=col(f"ln{n + 1}_g", k), bias=col(f"ln{n + 1}_b", k))
                    act.activation(ch(x32, k), ch(y_ln, k), ACT.Identity, **gain).then_inc(ln_out, 1)
                    if n < 2:
                        act.activation(ch(x_hi, k), ch(y_ln, k), ACT.Identity, **gain).then_inc(x_high, 1)

            high(0, 0, 0)
            high(1, 1, 0)
            act.wait_ge(x_loaded, 16)
            for k in range(KT):
                act.activation(ch(x_hi, k), ch(x32, k), ACT.Copy).then_inc(x_high, 1)
            act.wait_ge(consts_loaded, 80)
            act.wait_ge(eps_set, 3)
            swiglu(FFN1_IN, FFN1_OUT, 0, 0)
            norm(0)

            for q, (what, j) in enumerate(PROJ):
                g = PROJ_IN + q
                if g + 2 < MIX_OUT:
                    high(g + 2, q % 2, (g + 2) // 2)
                act.wait_ge(weights_used, g + 3)
                bank = ps[q % PROJ_BANKS]
                if what == "conv_gate":
                    if j >= 2:
                        act.wait_ge(tile_done, j - 1)
                    act.activation(ch(tmp, j % 2), bank[:, :], ACT.Sigmoid).then_inc(proj_free[q % PROJ_BANKS], 1)
                elif what != "conv_value":
                    dst = {"wd": (wag_t, 0), "ad": (wag_t, 1), "gd": (wag_t, 2 + j), "k": (k_t, j), "r": (r_t, j),
                           "v": (v_t, j)}[what]
                    m = MU[what, j]
                    if q == 2 * JT:
                        act.wait_ge(own_set, 2)
                    act.activation(ch(*dst), bank[:, :], ACT.Identity, scale=own[:, m:m + 1]).then_inc(proj_part, 1)

            for j in range(JT):
                act.wait_ge(kk_in, j + 1)
                act.activation(ch(tmp, j), ch(kk_t, j), ACT.Square).then_inc(kk_sq, 1)
            act.activation(ch(wag_t, 0), ch(wag_t, 0), ACT.Tanh).then_inc(act_in, 1)
            act.activation(ch(wag_t, 2), ch(wag_t, 2), ACT.Sigmoid).then_inc(act_in, 1)
            act.activation(ch(wag_t, 3), ch(wag_t, 3), ACT.Sigmoid).then_inc(act_in, 1)
            for j in range(JT):
                act.wait_ge(kk_ss, j + 1)
                act.activation(ch(tmp, j), ps[4 + j][:, :], ACT.Sqrt).then_inc(kk_norm, 1)
            for j in range(JT):
                act.wait_ge(gate_mm, j + 1)
                act.activation(ch(gate_t, j), ps[j % 2][:, :], ACT.Copy).then_inc(gate_out, 1)
            for j in range(JT):
                act.wait_ge(cn_cent, j + 1)
                act.activation(ch(tmp, 4 + j), ch(conv_t, j), ACT.Square).then_inc(cn_sq, 1)
            act.wait_ge(cn_var, 1)
            act.activation(ch(tmp, 8), ps[3][:, :], ACT.Sqrt, scale=1.0 / WIDTH, bias=eps[1][:, :]).then_inc(cn_std, 1)
            for j in range(JT):
                act.wait_ge(cn_norm, j + 1)
                act.activation(ch(conv_t, j), ch(conv_t, j), ACT.Identity, scale=col("conv_ln_g", j),
                               bias=col("conv_ln_b", j)).then_inc(cn_z, 1)
            act.wait_ge(cn_z, JT)
            for j in range(JT):
                act.activation(ch(tmp, 4 + j), ch(conv_t, j), ACT.Sigmoid).then_inc(cn_sig, 1)
            act.wait_ge(conv_out, JT)
            act.wait_ge(kk_ready, 1)
            exps = [0]

            def decay(src, sign):
                i = exps[0]
                exps[0] += 1
                if i >= 2:
                    act.wait_ge(exp_used, i - 1)
                act.activation(ch(e_t, i % 2), src, ACT.Exp, scale=sign * KAPPA).then_inc(exp_ready, 1)

            for j in range(JT):
                if j:
                    act.wait_ge(prep_done, 2 * j)
                for d in range(2):
                    act.wait_ge(lora_mm, 4 * j + 2 * d + 1)
                    act.activation(ch(tmp, 5 * d), ps[2 * d][:, :], ACT.Sigmoid, bias=col("w0", d * JT + j))\
                        .then_inc(lora_act, 1)
                    act.wait_ge(lora_mm, 4 * j + 2 * d + 2)
                    act.activation(ch(tmp, 5 * d + 1), ps[2 * d + 1][:, :], ACT.Sigmoid, bias=col("a0", d * JT + j))\
                        .then_inc(lora_act, 1)
                    act.wait_ge(lora_act, 4 * j + 2 * d + 2)
                    act.activation(ch(tmp, 5 * d + 2), ch(tmp, 5 * d + 1), ACT.Identity, scale=col("k_a", j),
                                   bias=own[:, 16 + j:17 + j]).then_inc(mult_ready, 1)
                for d in range(2):
                    act.wait_ge(cum_ready, 2 * j + d + 1)
                    past, before = ch(tmp, 5 * d + 4), ch(tmp, 5 * d)
                    for src, sign in ([(past, 1), (before, -1), (past, -1)] if d == 0 else
                                      [(before, -1), (past, 1), (before, 1)]):
                        decay(src, sign)
            act.wait_ge(fac_in, 2 * JT)
            act.activation(fac[:, :], fac[:, :], ACT.Exp, scale=-KAPPA).then_inc(fac_ready, 1)
            act.wait_ge(vtok_mm, 1)
            for c in range(NC):
                act.activation(v_tok[:, c * WIDTH:(c + 1) * WIDTH], ps[4 + c][:, :], ACT.Copy).then_inc(vtok_out, 1)

            rings = [0]

            def products(i):
                rings[0] += 8

            def level_step(i, m):
                n, half = turns[i]
                done = i * LEVELS + m
                for d in range(2):
                    if 1 <= m < LEVELS - 1:
                        act.wait_ge(xn_mm[d], i * (LEVELS - 2) + m)
                        act.activation(x_i[:, d * 512:(d + 1) * 512], ps[2 + d][:, :], ACT.Copy).then_inc(x_ready[d], 1)
                    act.wait_ge(yn_mm[d], done + 1)
                    dst = y_i[:, d * 512:(d + 1) * 512] if m < LEVELS - 1 else \
                        inv[:, unit(half, d, 0) * P:(unit(half, d, 0) + 4) * P]
                    act.activation(dst, ps[4 + d][:, :], ACT.Copy).then_inc(y_ready[d], 1)

            def tokens(i):
                if turns[i][0] == NC - 1:
                    return
                for t, dst in enumerate((b_tok, k_tok)):
                    act.wait_ge(tok_mm, 2 * i + t + 1)
                    if i:
                        act.wait_ge(s_mm, i)
                    b = rings[0] % 2
                    rings[0] += 1
                    act.activation(dst[:, :], ps[b][:, :], ACT.Copy).then_inc(tok_out, 1)
                    act.wait_ge(tok_out, 2 * i + t + 1)
                    act.sem_inc(ring_free[b], 1)

            def run_w(i):
                act.wait_ge(w_mm, i + 1)
                act.activation(w_c[:, :], ps[6][:, :], ACT.Copy).then_inc(w_out_s, 1)

            def run_u(i):
                act.wait_ge(u_mm, i + 1)
                act.activation(u_c[:, :], ps[6][:, :], ACT.Copy).then_inc(u_out, 1)

            def nothing(i):
                pass

            steps = {"products": products, "level": level_step, "tokens": tokens, "w": run_w, "u": run_u,
                     "y": nothing, "state": nothing}
            for what, *which in schedule:
                steps[what](*which)

            for j in range(JT):
                act.wait_ge(gn_cent, j + 1)
                act.activation(ch(tmp, 4 + j), ch(y_t, j), ACT.Square).then_inc(gn_sq, 1)
            for j in range(JT):
                act.wait_ge(gn_var, j + 1)
                act.activation(ch(tmp, j), ps[4 + j][:, :], ACT.Sqrt, scale=1.0 / HEAD, bias=eps[3][:, :])\
                    .then_inc(gn_std, 1)
            high(MIX_OUT, 0, MIX_OUT // 2)
            high(MIX_OUT + 1, 1, MIX_OUT // 2)
            for j in range(JT):
                act.activation(ch(x_hi, JT + j), ch(conv_t, j), ACT.Copy).then_inc(mix_high, 1)
            for j in range(JT):
                act.wait_ge(gn_norm, j + 1)
                act.activation(ch(y_t, j), ch(y_t, j), ACT.Identity, scale=col("lnx_g", j), bias=col("lnx_b", j))\
                    .then_inc(gn_z, 1)
            for j in range(JT):
                act.wait_ge(mix_in, j + 1)
                act.activation(ch(x_hi, j), ch(y_t, j), ACT.Copy).then_inc(mix_high, 1)
            for k in range(KT):
                g = MIX_OUT + 2 + k
                high(g, k % 2, g // 2)
            norm(1)
            swiglu(FFN2_IN, FFN2_OUT, 1, 1)
            norm(2)

        @block.vector
        def _(dve):
            own_steps = [0]

            def step(ins):
                own_steps[0] += 1
                ins.then_inc(vec, 1)
                dve.wait_ge(vec, own_steps[0])

            def low(g, s):
                dve.wait_ge(hi_ready, g + 1)
                dve.tensor_tensor(w_lo[s][:, :], raw[s][:, :], w_hi[s][:, :].bitcast(F32), ALU.subtract)\
                    .then_inc(lo_ready, 1)

            def swiglu(in0, out0, e, last):
                with dve.Fori(0, FT // 2) as i:
                    for s in range(2):
                        g = i * 4 + (in0 + 2 * s)
                        pair = i * 2 + (s + FT * e)
                        low(g + 2, 0)
                        dve.wait_ge(sig_ready, pair + 1)
                        dve.tensor_tensor(ch(h_raw, s), ps[2 * s][:, :], ch(sig, s), ALU.mult).then_inc(gated, 1)
                        low(g + 3, 1)
                        dve.wait_ge(weights_used, g + 4)
                        dve.wait_ge(gated, pair + 1)
                        dve.tensor_tensor(ch(h_raw, s), ps[2 * s + 1][:, :], ch(h_raw, s), ALU.mult)\
                            .then_inc(pairs_free, 1)
                        dve.wait_ge(pairs_free, pair + 3)
                        f = bass.ds(i * (2 * SEQ) + s * SEQ, SEQ)
                        dve.tensor_copy(h_hi[:, f], ch(h_raw, s)).then_inc(h_high, 1)
                        dve.wait_ge(h_high, pair + 1)
                        dve.tensor_tensor(h_lo[:, f], ch(h_raw, s), h_hi[:, f].bitcast(F32), ALU.subtract)\
                            .then_inc(h_ready, 1)
                with dve.Fori(0, FT // 2 - last) as i:
                    for s in range(2):
                        low(i * 2 + (out0 + 2 + s), s)

            def norm(n, items_done, residual):
                dve.wait_ge(weights_used, 2 + items_done)
                for k in range(KT):
                    dve.scalar_tensor_tensor(ch(y_ln, k), ch(x32, k), residual, ps[k][:, :], ALU.mult, ALU.add)\
                        .then_inc(ln_in, 1)
                dve.wait_ge(ln_sum, n + 1)
                for k in range(KT):
                    dve.scalar_tensor_tensor(ch(y_ln, k), ps[0][:, :], -1.0 / D_MODEL, ch(y_ln, k), ALU.mult, ALU.add)\
                        .then_inc(ln_centered, 1)
                dve.wait_ge(ln_std, n + 1)
                dve.reciprocal(rstd[:, :], std[:, :]).then_inc(ln_rstd, 1)
                dve.wait_ge(ln_rstd, n + 1)
                for k in range(KT):
                    dve.tensor_tensor(ch(y_ln, k), ch(y_ln, k), rstd[:, :], ALU.mult).then_inc(ln_norm, 1)
                if n < 2:
                    for k in range(KT):
                        dve.wait_ge(x_high, KT * (n + 1) + k + 1)
                        dve.tensor_tensor(ch(x_lo, k), ch(x32, k), ch(x_hi, k).bitcast(F32), ALU.subtract)\
                            .then_inc(x_low, 1)

            for n, value in enumerate((4 * LN_EPS, LN_EPS, 4 * LN_EPS, GN_EPS)):
                dve.memset(eps[n][:, :], value).then_inc(eps_set, 1)
            step(dve.memset(h_reset[:, :], 1.0))
            step(dve.memset(h_reset[:, :].rearrange("p (c t) -> p c t", c=NC)[:, :, 0:1], 0.0))
            low(0, 0)
            low(1, 1)
            dve.wait_ge(x_loaded, 16)
            for k in range(KT):
                dve.wait_ge(x_high, k + 1)
                dve.tensor_tensor(ch(x_lo, k), ch(x32, k), ch(x_hi, k).bitcast(F32), ALU.subtract).then_inc(x_low, 1)
            dve.wait_ge(consts_loaded, 80)
            step(dve.tensor_copy(level[:, :], level_f[:, :]))
            p0, n0 = PAR["mu_prev"], PAR["mu_next"]
            step(dve.tensor_tensor(own[:, 0:16], par[:, p0:p0 + 16], par[:, n0:n0 + 16], ALU.add))
            dve.tensor_scalar(own[:, 0:16], own[:, 0:16], -1.0, 1.0, ALU.mult, ALU.add).then_inc(own_set, 1)
            dve.tensor_scalar(own[:, 16:16 + JT], par[:, PAR["k_a"]:PAR["k_a"] + JT], -1.0, 1.0, ALU.mult, ALU.add)\
                .then_inc(own_set, 1)

            swiglu(FFN1_IN, FFN1_OUT, 0, 0)
            norm(0, PROJ_IN, 2 * ALPHA)

            taps = [(j, k) for j in range(JT) for k in range(TAPS)]

            def tap(j, k):
                window = u_t[:, j * ULEN + k:j * ULEN + k + SEQ]
                weight = par[:, PAR["conv_dw"] + k * JT + j:PAR["conv_dw"] + k * JT + j + 1]
                if k == 0:
                    step(dve.tensor_scalar(ch(conv_t, j), window, weight, col("conv_b", j), ALU.mult, ALU.add))
                elif k < TAPS - 1:
                    step(dve.scalar_tensor_tensor(ch(conv_t, j), window, weight, ch(conv_t, j), ALU.mult, ALU.add))
                else:
                    dve.scalar_tensor_tensor(ch(conv_t, j), window, weight, ch(conv_t, j), ALU.mult, ALU.add)\
                        .then_inc(conv_done, 1)

            parts = 0
            dve.wait_ge(pads_set, 2 * JT)
            for q, (what, j) in enumerate(PROJ):
                g = PROJ_IN + q
                if g + 2 < MIX_OUT:
                    low(g + 2, q % 2)
                bank, free = ps[q % PROJ_BANKS], proj_free[q % PROJ_BANKS]
                if what == "conv_value":
                    dve.wait_ge(weights_used, g + 3)
                    dve.wait_ge(proj_free[(q - 1) % PROJ_BANKS], 2 + q // PROJ_BANKS)
                    step(dve.tensor_tensor(u_t[:, j * ULEN + PAD:j * ULEN + PAD + SEQ], bank[:, :], ch(tmp, j % 2),
                                           ALU.mult))
                    dve.sem_inc(free, 1)
                    dve.sem_inc(tile_done, 1)
                elif what != "conv_gate":
                    parts += 1
                    dst, i = {"wd": (wag_t, 0), "ad": (wag_t, 1), "gd": (wag_t, 2 + j), "k": (k_t, j), "r": (r_t, j),
                              "v": (v_t, j)}[what]
                    m, c0 = MU[what, j], i * SEQ
                    dve.wait_ge(proj_part, parts)
                    later, earlier = dst[:, c0 + 1:c0 + SEQ], dst[:, c0:c0 + SEQ - 1]
                    step(dve.scalar_tensor_tensor(later, bank[:, 0:SEQ - 1], col("mu_prev", m), later,
                                                  ALU.mult, ALU.add))
                    step(dve.scalar_tensor_tensor(earlier, bank[:, 1:SEQ], col("mu_next", m), earlier,
                                                  ALU.mult, ALU.add))
                    dve.sem_inc(free, 1)
                    dve.sem_inc(tile_done, 1)
                    if what == "k":
                        dve.tensor_scalar(ch(kk_t, j), ch(k_t, j), col("k_k", j), None, ALU.mult).then_inc(kk_in, 1)
                if q >= 2 * JT:
                    for _ in range(8):
                        if taps:
                            tap(*taps.pop(0))

            dve.wait_ge(kk_norm, JT)
            step(dve.tensor_scalar(ch(tmp, 0, 4), ch(tmp, 0, 4), NORM_EPS, None, ALU.max))
            step(dve.reciprocal(ch(tmp, 0, 4), ch(tmp, 0, 4)))
            dve.tensor_tensor(kk_t[:, :], kk_t[:, :], ch(tmp, 0, 4), ALU.mult).then_inc(kk_ready, 1)
            dve.wait_ge(cn_sum, 1)
            for j in range(JT):
                dve.scalar_tensor_tensor(ch(conv_t, j), ps[2][:, :], -1.0 / WIDTH, ch(conv_t, j), ALU.mult, ALU.add)\
                    .then_inc(cn_cent, 1)
            dve.wait_ge(cn_std, 1)
            step(dve.reciprocal(ch(tmp, 9), ch(tmp, 8)))
            for j in range(JT):
                dve.tensor_tensor(ch(conv_t, j), ch(conv_t, j), ch(tmp, 9), ALU.mult).then_inc(cn_norm, 1)
            for j in range(JT):
                dve.wait_ge(cn_sig, j + 1)
                dve.tensor_tensor(ch(conv_t, j), ch(conv_t, j), ch(tmp, 4 + j), ALU.mult).then_inc(conv_out, 1)

            reset = h_reset[:, :]
            exps = 0
            dve.wait_ge(kk_ready, 1)
            for j in range(JT):
                for d in range(2):
                    rate, a, kd, cum, past = (ch(tmp, 5 * d + i) for i in range(5))
                    c_view = cum.rearrange("p (c t) -> p c t", c=NC)
                    p_view = past.rearrange("p (c t) -> p c t", c=NC)
                    dve.wait_ge(mult_ready, 2 * j + d + 1)
                    step(dve.tensor_tensor_scan(cum, reset, rate, 0.0, ALU.mult, ALU.add))
                    step(dve.tensor_tensor(p_view, c_view, c_view[:, :, MID:MID + 1].to_broadcast([P, NC, CHUNK]),
                                           ALU.subtract))
                    dve.tensor_tensor(rate, past, rate, ALU.subtract).then_inc(cum_ready, 1)
                    f0 = (d * JT + j) * (NC - 1)
                    dve.tensor_tensor(fac[:, f0:f0 + NC - 1].rearrange("p (c a) -> p c a", a=1),
                                      p_view[:, 0:NC - 1, CHUNK - 1:CHUNK], c_view[:, 1:NC, MID:MID + 1],
                                      ALU.add).then_inc(fac_in, 1)
                    step(dve.tensor_tensor(kd, kd, ch(k_t, j), ALU.mult))
                    if d == 0:
                        dve.tensor_copy(ch(bonus_t, j), kd)
                    else:
                        dve.tensor_tensor(ch(bonus_t, j), ch(bonus_t, j), kd, ALU.add)
                    step(dve.tensor_tensor(a, a, ch(kk_t, j), ALU.mult))
                for d in range(2):
                    rate, a, kd, cum, past = (ch(tmp, 5 * d + i) for i in range(5))
                    slot = (d * JT + j) * SEQ
                    q_view = qr[:, 2 * slot:2 * slot + 2 * SEQ].rearrange("p (c w t) -> p c w t", c=NC, w=2)
                    e_view = [ch(e_t, s).rearrange("p (c t) -> p c t", c=NC) for s in range(2)]
                    dve.wait_ge(exp_ready, exps + 1)
                    dve.tensor_tensor(b_m[:, slot:slot + SEQ], a, ch(e_t, exps % 2), ALU.mult)
                    dve.tensor_tensor(k_m[:, slot:slot + SEQ], kd, ch(e_t, exps % 2), ALU.mult).then_inc(exp_used, 1)
                    dve.wait_ge(exp_ready, exps + 2)
                    dve.scalar_tensor_tensor(q_view[:, :, 0, :], ch(kk_t, j).rearrange("p (c t) -> p c t", c=NC), -1.0,
                                             e_view[(exps + 1) % 2], ALU.mult, ALU.mult).then_inc(exp_used, 1)
                    dve.wait_ge(exp_ready, exps + 3)
                    step(dve.tensor_tensor(q_view[:, :, 1, :], ch(r_t, j).rearrange("p (c t) -> p c t", c=NC),
                                           e_view[(exps + 2) % 2], ALU.mult))
                    dve.sem_inc(exp_used, 1)
                    dve.sem_inc(prep_done, 1)
                    exps += 3
                dve.scalar_tensor_tensor(ch(bonus_t, j), ch(bonus_t, j), col("r_k", j), ch(r_t, j), ALU.mult, ALU.mult)\
                    .then_inc(bonus_in, 1)
            for j in range(JT):
                dve.wait_ge(bonus_mm, j + 1)
                dve.tensor_tensor(ch(bonus_t, j), ps[j][:, :], ch(v_t, j), ALU.mult).then_inc(bonus_out, 1)

            rings = [0]

            def products(i):
                n, half = turns[i]
                for d in range(2):
                    for u in range(4):
                        b = rings[0] % 2
                        rings[0] += 1
                        dve.wait_ge(prod_mm, 8 * i + 4 * d + u + 1)
                        if i == 0 and d == 0 and u == 0:
                            dve.wait_ge(vtok_mm, 1)
                        c0 = unit(half, d, u) * 512
                        dve.tensor_tensor(a_t[:, c0:c0 + 512], ps[b][:, :], tri[:, d * 512:(d + 1) * 512], ALU.mult)\
                            .then_inc(prod_out, 1)
                        dve.wait_ge(prod_out, 8 * i + 4 * d + u + 1)
                        dve.sem_inc(ring_free[b], 1)

            def level_step(i, m):
                for d in range(2):
                    dve.wait_ge(lx_mm[d], i * LEVELS + m + 1)
                    c0 = (m * 2 + d) * 512
                    l0 = (d * LEVELS + m) * P
                    if i == 0 and m == 0 and d == 0:
                        dve.wait_ge(presets, 2 * LEVELS)
                    dve.copy_predicated(t_i[:, c0:c0 + 512].rearrange("p (u s) -> p u s", u=4),
                                        level[:, l0:l0 + P].rearrange("p (a s) -> p a s", a=1).to_broadcast([P, 4, P]),
                                        ps[2 + d][:, :].rearrange("p (u s) -> p u s", u=4)).then_inc(t_ready[d], 1)

            def tokens(i):
                if turns[i][0] < NC - 1:
                    rings[0] += 2

            def run_y(i):
                n, half = turns[i]
                dve.wait_ge(y_mm, i + 1)
                for d in range(2):
                    dst = y_t[:, 2 * half * SEQ:(2 * half + 2) * SEQ].rearrange("p (j c t) -> p j c t", j=2, c=NC)[
                        :, :, chunk(n, d), :]
                    src = ps[7][:, 2 * d * CHUNK:(2 * d + 2) * CHUNK].rearrange("p (j t) -> p j t", j=2)
                    if n < NC // 2:
                        dve.tensor_copy(dst, src).then_inc(y_out, 1)
                    else:
                        dve.tensor_tensor(dst, src, dst, ALU.add).then_inc(y_out, 1)

            def run_state(i):
                n, half = turns[i]
                if n == NC - 1:
                    return
                dve.wait_ge(s_mm, i + 1)
                now = state[:, half * 4 * P:(half + 1) * 4 * P]
                if n:
                    dve.tensor_tensor(s_new[:, :], ps[7][:, :], now, ALU.add).then_inc(s_sum, 1)
                else:
                    dve.tensor_copy(s_new[:, :], ps[7][:, :]).then_inc(s_sum, 1)
                dve.wait_ge(s_sum, i + 1)
                for d in range(2):
                    for jj in range(2):
                        f = (d * JT + 2 * half + jj) * (NC - 1) + (n if d == 0 else NC - 2 - n)
                        c0 = (2 * d + jj) * P
                        dve.scalar_tensor_tensor(now[:, c0:c0 + P], s_new[:, c0:c0 + P], fac[:, f:f + 1],
                                                 head_ones[:, :], ALU.mult, ALU.mult).then_inc(s_out, 1)

            def nothing(i):
                pass

            steps = {"products": products, "level": level_step, "tokens": tokens, "w": nothing, "u": nothing,
                     "y": run_y, "state": run_state}
            for what, *which in schedule:
                steps[what](*which)

            for j in range(JT):
                dve.wait_ge(gn_sum, j + 1)
                dve.scalar_tensor_tensor(ch(y_t, j), ps[j][:, :], -1.0 / HEAD, ch(y_t, j), ALU.mult, ALU.add)\
                    .then_inc(gn_cent, 1)
            dve.wait_ge(gn_std, JT)
            step(dve.reciprocal(ch(tmp, 0, 4), ch(tmp, 0, 4)))
            for j in range(JT):
                dve.tensor_tensor(ch(y_t, j), ch(y_t, j), ch(tmp, j), ALU.mult).then_inc(gn_norm, 1)
            low(MIX_OUT, 0)
            low(MIX_OUT + 1, 1)
            for j in range(JT):
                dve.wait_ge(mix_high, j + 1)
                dve.tensor_tensor(ch(x_lo, JT + j), ch(conv_t, j), ch(x_hi, JT + j).bitcast(F32), ALU.subtract)\
                    .then_inc(mix_low, 1)
            for j in range(JT):
                dve.wait_ge(gn_z, j + 1)
                step(dve.tensor_tensor(ch(y_t, j), ch(y_t, j), ch(bonus_t, j), ALU.add))
                dve.tensor_tensor(ch(y_t, j), ch(y_t, j), ch(gate_t, j), ALU.mult).then_inc(mix_in, 1)
            for j in range(JT):
                dve.wait_ge(mix_high, JT + j + 1)
                dve.tensor_tensor(ch(x_lo, j), ch(y_t, j), ch(x_hi, j).bitcast(F32), ALU.subtract).then_inc(mix_low, 1)
            for k in range(KT):
                low(MIX_OUT + 2 + k, k % 2)
            dve.wait_ge(reloaded, 16)
            norm(1, FFN2_IN, ALPHA)
            swiglu(FFN2_IN, FFN2_OUT, 1, 1)
            norm(2, N_ITEMS, 2 * ALPHA)


def kernel(**inputs):
    import numpy as np
    import concourse.bacc as bacc
    from concourse.bass_utils import run_bass_kernel_spmd

    a = {k: np.ascontiguousarray(v) for k, v in inputs.items()}
    f32 = np.float32

    def columns(v):
        v = v.reshape(-1)
        n = -(-v.size // P)
        out = np.zeros((n * P,), v.dtype)
        out[:v.size] = v
        return out.reshape(n, P).T

    def in_tile(w):
        full = np.zeros((D_MODEL, P), w.dtype)
        full[:, :w.shape[1]] = w
        return full.reshape(KT, P, P).transpose(1, 0, 2).reshape(P, KT * P)

    w_in = a["w_in"][0]
    shift = 3 * WIDTH + 4 * 64 + 160
    starts = {"r": 0, "k": WIDTH, "v": 2 * WIDTH, "wd": 3 * WIDTH, "ad": 3 * WIDTH + 128, "gd": 3 * WIDTH + 256,
              "conv_value": shift, "conv_gate": shift + WIDTH}
    tiles = []

    def ffn(w1, w2):
        for f in range(FT):
            tiles.append(in_tile(w1[:, f * P:(f + 1) * P]))
            tiles.append(in_tile(w1[:, D_FF + f * P:D_FF + (f + 1) * P]))
        for f in range(FT):
            tiles.append(w2[f * P:(f + 1) * P, :])

    ffn(a["ffn1_w_in"][0], a["ffn1_w_out"][0])
    for what, j in PROJ:
        c0 = starts[what] + j * P
        c1 = min(c0 + P, shift) if what == "gd" else c0 + P
        tiles.append(in_tile(w_in[:, c0:c1]))
    for k in range(KT):
        tiles.append(a["w_out"][0][k * P:(k + 1) * P, :])
    ffn(a["ffn2_w_in"][0], a["ffn2_w_out"][0])
    weights = np.stack(tiles)

    order = sorted(PAR, key=PAR.get)
    params = np.ascontiguousarray(np.concatenate([columns(a[name][0]) for name in order], axis=1))
    lora = np.ascontiguousarray(np.concatenate(
        [a["w2"][0].reshape(128, WIDTH), a["a2"][0].reshape(128, WIDTH), a["g2"][0, :128]], axis=1))
    gate_tail = np.ascontiguousarray(a["g2"][0, 128:])
    x_t = np.ascontiguousarray(a["x"][0].T.reshape(KT, P, SEQ).transpose(1, 0, 2).reshape(P, KT * SEQ))

    src, dst = np.arange(CHUNK)[:, None], np.arange(CHUNK)[None, :]
    tri = []
    for strict, whole in ((dst > src, dst >= src), (dst < src, dst <= src)):
        tri += [strict, whole, strict, whole]
    tri = np.concatenate(tri, axis=1).astype(f32)
    level = []
    for d in range(2):
        for m in range(LEVELS):
            row, colm = (src, dst) if d == 0 else (dst, src)
            level.append((row >> (m + 1) == colm >> (m + 1)) & ((row >> m) % 2 == 1) & ((colm >> m) % 2 == 0))
    level = np.concatenate(level, axis=1).astype(f32)
    arrays = {
        "x_t": x_t, "weights": weights, "params": params, "lora": lora, "gate_tail": gate_tail,
        "ident_c": np.eye(P, dtype=f32), "head_ones_c": np.kron(np.eye(2, dtype=f32), np.ones((64, 64), f32)),
        "tri_c": tri, "level_c": level,
    }
    nc = bacc.Bacc("TRN2", target_bir_lowering=False, num_devices=1)
    aps = {n: nc.dram_tensor(n + "_in", v.shape, mybir.dt.from_np(v.dtype), kind="ExternalInput").ap()
           for n, v in arrays.items()}
    out_t = nc.dram_tensor("out_t", (P, KT * SEQ), F32, kind="ExternalOutput").ap()
    encoder_block(nc, out_t=out_t, **aps)
    got = run_bass_kernel_spmd(nc, [{n + "_in": v for n, v in arrays.items()}], core_ids=[0])
    y = got.results[0]["out_t"].reshape(P, KT, SEQ)
    return y.transpose(1, 0, 2).reshape(D_MODEL, SEQ).T[None]
```

```python
from contextlib import ExitStack
import math

import concourse.bass as bass
from concourse import mybir

F32 = mybir.dt.float32
F32R = mybir.dt.float32r
U8 = mybir.dt.uint8
ALU = mybir.AluOpType
ACT = mybir.ActivationFunctionType

P = 128
SEQ = 512
D_MODEL = 1024
D_FF = 2816
WIDTH = 512
HEAD = 64
TAPS = 31
PAD = TAPS // 2
KT = D_MODEL // P
FT = D_FF // P
JT = WIDTH // P
CHUNK = 128
NC = SEQ // CHUNK
MID = CHUNK // 2 - 1
LEVELS = 7
ALPHA = 2.0 ** 0.25
LN_EPS = 1e-5
GN_EPS = 64e-5
NORM_EPS = 1e-12
KAPPA = math.exp(-0.5)

PROJ = [("wd", 0), ("ad", 0), ("gd", 0), ("gd", 1)]
PROJ += [("k", j) for j in range(JT)] + [("r", j) for j in range(JT)] + [("v", j) for j in range(JT)]
PROJ += [(w, j) for j in range(JT) for w in ("conv_gate", "conv_value")]
PROJ_BANKS = 4
FFN1_IN = 0
FFN1_OUT = FFN1_IN + 2 * FT
PROJ_IN = FFN1_OUT + FT
MIX_OUT = PROJ_IN + len(PROJ)
FFN2_IN = MIX_OUT + KT
FFN2_OUT = FFN2_IN + 2 * FT
N_ITEMS = FFN2_OUT + FT


def param_columns():
    at, col = {}, 0
    for name, n in (("ln1_g", KT), ("ln1_b", KT), ("ln2_g", KT), ("ln2_b", KT), ("ln3_g", KT), ("ln3_b", KT),
                    ("mu_prev", 16), ("mu_next", 16), ("w0", 2 * JT), ("a0", 2 * JT), ("k_k", JT), ("k_a", JT),
                    ("r_k", JT), ("lnx_g", JT), ("lnx_b", JT), ("conv_dw", TAPS * JT), ("conv_b", JT),
                    ("conv_ln_g", JT), ("conv_ln_b", JT)):
        at[name] = col
        col += n
    return at, col


PAR, N_PAR = param_columns()
MU = {("r", j): j for j in range(4)} | {("k", j): 4 + j for j in range(4)} | {("v", j): 8 + j for j in range(4)}
MU |= {("wd", 0): 12, ("ad", 0): 13, ("gd", 0): 14, ("gd", 1): 15}


def encoder_block(nc, x_t, weights, params, lora, gate_tail, ident_c, head_ones_c, tri_c, level_c, out_t):
    spill = nc.dram_tensor("x1_spill", (P, KT * SEQ), F32, kind="Internal").ap()
    with ExitStack() as ctx:
        def sb(name, cols, dt=F32):
            return ctx.enter_context(nc.sbuf_tensor(name, [P, cols], dt))

        def sem(name):
            return ctx.enter_context(nc.semaphore(name))

        par = sb("par", N_PAR)
        own = sb("own", 16 + JT)
        ident = sb("ident", P)
        ones = sb("ones", P)
        head_ones = sb("head_ones", P)
        tri = sb("tri", 2 * 512)
        level = sb("level", 2 * LEVELS * P, U8)

        ident_r = sb("ident_r", P, F32R)
        two_r = sb("two_r", P, F32R)
        minus_r = sb("minus_r", P, F32R)
        eps = [sb(f"eps{n}", 1) for n in range(4)]
        h_reset = sb("h_reset", SEQ, mybir.dt.bfloat16)

        base = (nc.sbuf_base + 63) // 64 * 64

        def at(name, offset, cols, dt=F32):
            return nc.alloc_sbuf_tensor_at(name, [P, cols], dt, offset=base + offset)

        raw = [at(f"w_raw{s}", 4096 * s, 1024) for s in range(2)]
        w_hi = [at(f"w_hi{s}", 8192 + 4096 * s, 1024, F32R) for s in range(2)]
        w_lo = [at(f"w_lo{s}", 16384 + 4096 * s, 1024, F32R) for s in range(2)]
        x_hi = at("x_hi", 24576, KT * SEQ, F32R)
        x_lo = at("x_lo", 40960, KT * SEQ, F32R)
        x32 = at("x32", 57344, KT * SEQ)
        h_hi = at("h_hi", 73728, FT * SEQ, F32R)
        h_lo = at("h_lo", 118784, FT * SEQ, F32R)
        sig = at("sig", 163840, 2 * SEQ)
        h_raw = at("h_raw", 167936, 2 * SEQ)
        y_ln = at("y_ln", 73728, KT * SEQ)
        sq_ln = at("sq_ln", 90112, KT * SEQ)
        x_back = at("x_back", 114688, KT * SEQ)
        std = at("std", 197120, SEQ)
        rstd = at("rstd", 199168, SEQ)
        level_f = at("level_f", 180736, 2 * LEVELS * P)
        ULEN = SEQ + 2 * PAD
        k_t = at("k_t", 57344, JT * SEQ)
        r_t = at("r_t", 65536, JT * SEQ)
        kk_t = at("kk_t", 73728, JT * SEQ)
        qr = at("qr", 81920, 2 * JT * 2 * SEQ)
        b_m = at("b_m", 114688, 2 * JT * SEQ)
        k_m = at("k_m", 131072, 2 * JT * SEQ)
        v_t = at("v_t", 147456, JT * SEQ)
        u_t = at("u_t", 155648, JT * ULEN)
        wag_t = at("wag_t", 164352, 4 * SEQ)
        lora_s = at("lora_s", 172544, 4 * 512)
        tmp = at("tmp", 180736, 10 * SEQ)
        fac = at("fac", 201216, 2 * JT * (NC - 1))
        tt_i = at("tt_i", 8192, 2 * 4 * P, F32R)
        at_r = at("at_r", 12288, 2 * 4 * P, F32R)
        x_i = at("x_i", 16384, 2 * 4 * P, F32R)
        y_i = at("y_i", 20480, 2 * 4 * P, F32R)
        a_t = at("a_t", 24576, 2 * 2 * 4 * 512)
        inv = at("inv", 57344, 2 * 2 * 4 * P)
        y_t = at("y_t", 65536, JT * SEQ)
        e_i = at("e_i", 73728, 2 * 4 * P)
        b_tok = at("b_tok", 77824, 4 * P)
        k_tok = at("k_tok", 79872, 4 * P)
        state = at("state", 164352, 8 * P)
        s_new = at("s_new", 172544, 4 * P)
        v_tok = at("v_tok", 180736, NC * WIDTH)
        conv_t = at("conv_t", 188928, JT * SEQ)
        w_c = at("w_c", 197120, 8 * HEAD)
        u_c = at("u_c", 199168, 8 * HEAD)
        cn_t = at("cn_t", 8192, JT * SEQ)
        cn_std = at("cn_std_t", 16384, 2 * SEQ)
        gate_t = at("gate_t", 73728, JT * SEQ)
        gn_sq_t = at("gn_sq_t", 81920, JT * SEQ)
        gn_std_t = at("gn_std_t", 90112, JT * SEQ)
        assert base + 201312 <= nc.sbuf_usable_end, (base, nc.sbuf_usable_end)

        ps = [ctx.enter_context(nc.psum_tensor(f"bank{i}", [P, 512], F32)) for i in range(8)]

        def ch(t, j, n=1):
            return t[:, j * SEQ:(j + n) * SEQ]

        def col(name, j=0):
            return par[:, PAR[name] + j:PAR[name] + j + 1]

        consts_loaded = sem("consts_loaded")
        x_loaded = [sem(f"x_loaded{k}") for k in range(KT // 2)]
        lora_loaded = sem("lora_loaded")
        raw_landed = [sem(f"raw_landed{s}") for s in range(2)]
        hi_ready = sem("hi_ready")
        lo_ready = sem("lo_ready")
        weights_used = sem("weights_used")
        pairs_free = sem("pairs_free")
        sig_ready = sem("sig_ready")
        gated = sem("gated")
        h_high = sem("h_high")
        h_ready = sem("h_ready")
        x_high = sem("x_high")
        x_low = sem("x_low")
        ln_in = sem("ln_in")
        ln_sum = sem("ln_sum")
        ln_centered = sem("ln_centered")
        ln_squared = sem("ln_squared")
        ln_var = sem("ln_var")
        ln_std = sem("ln_std")
        ln_rstd = sem("ln_rstd")
        ln_norm = sem("ln_norm")
        ln_out = sem("ln_out")
        ones_set = sem("ones_set")
        eps_set = sem("eps_set")
        own_set = sem("own_set")
        diag_set = sem("diag_set")
        sums_done = sem("sums_done")
        pads_set = sem("pads_set")
        spilled = sem("spilled")
        reloaded = sem("reloaded")
        proj_free = [sem(f"proj_free{b}") for b in range(PROJ_BANKS)]
        proj_part = sem("proj_part")
        vec = sem("vec")
        act_own = sem("act_own")
        tile_done = sem("tile_done")
        conv_done = sem("conv_done")
        cn_sum, cn_cent, cn_sq, cn_var, cn_root, cn_norm, cn_z, cn_sig, conv_out = (
            sem(n) for n in ("cn_sum", "cn_cent", "cn_sq", "cn_var", "cn_root", "cn_norm", "cn_z", "cn_sig", "conv_out"))
        kk_in, kk_sq, kk_ss, kk_norm, kk_ready = (sem(n) for n in ("kk_in", "kk_sq", "kk_ss", "kk_norm", "kk_ready"))
        act_in, lora_mm, lora_act, gate_mm, gate_out = (
            sem(n) for n in ("act_in", "lora_mm", "lora_act", "gate_mm", "gate_out"))
        cum_ready, exp_ready, exp_used, mult_ready, prep_done, fac_in, fac_ready = (
            sem(n) for n in ("cum_ready", "exp_ready", "exp_used", "mult_ready", "prep_done", "fac_in", "fac_ready"))
        bonus_in, bonus_mm, bonus_out, vtok_mm, vtok_out = (
            sem(n) for n in ("bonus_in", "bonus_mm", "bonus_out", "vtok_mm", "vtok_out"))
        prod_mm, ring_free, prod_out = sem("prod_mm"), [sem("ring_free0"), sem("ring_free1")], sem("prod_out")
        at_ready, nw_mm, e_ready, in_mm, inv_ready = (
            [sem(f"{n}{d}") for d in range(2)] for n in ("at_ready", "nw_mm", "e_ready", "in_mm", "inv_ready"))
        lx_mm, t_ready, xn_mm, x_ready, yn_mm, y_ready = (
            [sem(f"{n}{d}") for d in range(2)] for n in ("lx_mm", "t_ready", "xn_mm", "x_ready", "yn_mm", "y_ready"))
        tok_mm, tok_out, w_mm, w_out_s, u_mm, u_out, y_mm, y_out, s_mm, s_sum, s_out = (
            sem(n) for n in ("tok_mm", "tok_out", "w_mm", "w_out_s", "u_mm", "u_out", "y_mm", "y_out", "s_mm",
                             "s_sum", "s_out"))
        gn_sum, gn_cent, gn_sq, gn_var, gn_std, gn_norm, gn_z, mix_high, mix_low, mix_in = (
            sem(n) for n in ("gn_sum", "gn_cent", "gn_sq", "gn_var", "gn_std", "gn_norm", "gn_z", "mix_high",
                             "mix_low", "mix_in"))
        stored = sem("stored")
        block = ctx.enter_context(nc.Block())

        turns = [(n, half) for n in range(NC) for half in range(2)]
        schedule = []
        for i in range(len(turns) + 1):
            prepare = [("products", i)] + [("level", i, m) for m in range(LEVELS)] + [("newton", i)] if i < len(turns) else []
            run = [("tokens", i - 1), ("w", i - 1), ("u", i - 1), ("y", i - 1), ("state", i - 1)] if i else []
            if i == len(turns):
                run = run[:2] + [("conv_sum",)] + run[2:4] + [("conv_var",)]
            while prepare or run:
                schedule += prepare[:1] + run[:1]
                prepare, run = prepare[1:], run[1:]

        def e_buf(i):
            return ch(tmp, (3, 8)[i % 2])

        def chunk(n, d):
            return n if d == 0 else NC - 1 - n

        def unit(half, d, u):
            return (half * 2 + d) * 4 + u

        def prod(half, d, u, what):
            c0 = unit(half, d, u) * 512 + {"qb": 0, "rb": 128, "qk": 256, "rk": 384}[what]
            return a_t[:, c0:c0 + 128]

        @block.sync
        def _(sp):
            sp.dma_start(raw[0][:, :], weights[0]).then_inc(raw_landed[0], 16)
            for k in range(0, KT, 2):
                sp.dma_start(ch(x32, k, 2), x_t[:, k * SEQ:(k + 2) * SEQ]).then_inc(x_loaded[k // 2], 16)
            sp.dma_start(raw[1][:, :], weights[1]).then_inc(raw_landed[1], 16)
            sp.dma_start(par[:, :], params).then_inc(consts_loaded, 16)
            sp.dma_start(ident[:, :], ident_c).then_inc(consts_loaded, 16)
            sp.dma_start(head_ones[:, :], head_ones_c).then_inc(consts_loaded, 16)
            sp.dma_start(tri[:, :], tri_c).then_inc(consts_loaded, 16)
            sp.dma_start(level_f[:, :], level_c).then_inc(consts_loaded, 16)

            with sp.Fori(1, N_ITEMS // 2) as t:
                for s in range(2):
                    g = t * 2
                    sp.wait_ge(hi_ready, g + (s - 1))
                    sp.wait_ge(lo_ready, g + (s - 1))
                    sp.dma_start(raw[s][:, :], weights[bass.ds(g + s, 1), :, :].rearrange("a p n -> (a p) n"))\
                        .then_inc(raw_landed[s], 16)
            for k in range(KT):
                sp.wait_ge(ln_out, 2 * KT + k + 1)
                sp.dma_start(out_t[:, k * SEQ:(k + 1) * SEQ], ch(x32, k)).then_inc(stored, 16)
            sp.wait_ge(stored, 16 * KT)

        @block.gpsimd
        def _(pool):
            pool.memset(ones[:, :], 1.0).then_inc(ones_set, 1)
            pool.wait_ge(ln_out, KT)
            pool.dma_start(spill, x32[:, :]).then_inc(spilled, 16)
            pool.wait_ge(weights_used, 2 + PROJ_IN)
            for j in range(JT):
                pool.memset(u_t[:, j * ULEN:j * ULEN + PAD], 0.0).then_inc(pads_set, 1)
                pool.memset(u_t[:, (j + 1) * ULEN - PAD:(j + 1) * ULEN], 0.0).then_inc(pads_set, 1)
            pool.dma_start(lora_s[:, 0:1536], lora).then_inc(lora_loaded, 16)
            pool.dma_start(lora_s[0:32, 1536:2048], gate_tail).then_inc(lora_loaded, 16)
            pool.wait_ge(y_mm, len(turns))
            pool.wait_ge(spilled, 16)
            pool.dma_start(x_back[:, :], spill).then_inc(reloaded, 16)
            pool.wait_ge(reloaded, 16)

        @block.tensor
        def _(pe):
            pe.sem_inc(weights_used, 2)
            pe.sem_inc(pairs_free, 2)
            for b in range(PROJ_BANKS):
                pe.sem_inc(proj_free[b], 1)

            def three(bank, s, k, high, low, start, stop):
                wh, wl = w_hi[s][:, k * P:(k + 1) * P], w_lo[s][:, k * P:(k + 1) * P]
                pe.matmul(bank[:, :], wh, high, start=start, stop=False)
                pe.matmul(bank[:, :], wh, low, start=False, stop=False)
                return pe.matmul(bank[:, :], wl, high, start=False, stop=stop)

            def up_tile(g, s, bank, n_x):
                pe.wait_ge(hi_ready, g + 1)
                pe.wait_ge(lo_ready, g + 1)
                for k in range(KT):
                    pe.wait_ge(x_low, KT * n_x + k + 1)
                    last = three(bank, s, k, ch(x_hi, k), ch(x_lo, k), k == 0, k == KT - 1)
                last.then_inc(weights_used, 1)

            def down_tile(g, s, f, high, low, first, last_one):
                pe.wait_ge(hi_ready, g + 1)
                pe.wait_ge(lo_ready, g + 1)
                for d in range(KT):
                    last = three(ps[d], s, d, high[:, bass.ds(f * SEQ, SEQ)], low[:, bass.ds(f * SEQ, SEQ)],
                                 first, last_one)
                    if last_one and d < KT - 1:
                        last.then_inc(sums_done, 1)
                last.then_inc(weights_used, 1)

            def swiglu(in0, out0, e):
                with pe.Fori(0, FT // 2) as i:
                    for s in range(2):
                        pe.wait_ge(pairs_free, i * 2 + (s + 1 + FT * e))
                        for part in range(2):
                            up_tile(i * 4 + (in0 + 2 * s + part), part, ps[2 * s + part], 2 * e)
                pe.wait_ge(h_ready, FT * (e + 1))
                down_tile(out0, 0, 0, h_hi, h_lo, True, False)
                with pe.Fori(0, FT // 2 - 1) as i:
                    for s in (1, 0):
                        down_tile(i * 2 + (out0 + 2 - s), s, i * 2 + (2 - s), h_hi, h_lo, False, False)
                down_tile(out0 + FT - 1, 1, FT - 1, h_hi, h_lo, False, True)

            def layer_sums(n):
                for k in range(KT):
                    pe.wait_ge(ln_in, KT * n + k + 1)
                    last = pe.matmul(ps[0][:, :], ones[:, :], ch(y_ln, k), start=k == 0, stop=k == KT - 1)
                last.then_inc(ln_sum, 1)
                for k in range(KT):
                    pe.wait_ge(ln_squared, KT * n + k + 1)
                    last = pe.matmul(ps[1][:, :], ones[:, :], ch(sq_ln, k), start=k == 0, stop=k == KT - 1)
                last.then_inc(ln_var, 1)

            swiglu(FFN1_IN, FFN1_OUT, 0)
            pe.wait_ge(ones_set, 1)
            pe.wait_ge(consts_loaded, 80)
            layer_sums(0)

            def kk_sums():
                for j in range(JT):
                    pe.wait_ge(kk_sq, j + 1)
                    pe.matmul(ps[4 + j][:, :], head_ones[:, :], ch(tmp, j), start=True, stop=True)\
                        .then_inc(kk_ss, 1)

            def lora(j):
                if j == 0:
                    pe.wait_ge(lora_loaded, 32)
                    pe.wait_ge(tile_done, 2)
                    pe.wait_ge(act_in, 1)
                    pe.wait_ge(kk_norm, JT)
                for d in range(2):
                    for what in range(2):
                        rows = slice(64 * d, 64 * d + 64)
                        i = 4 * j + 2 * d + what
                        if j >= 1:
                            pe.wait_ge(lora_act, i - 3)
                        pe.matmul(ps[4 + i % 4][:, :], lora_s[rows, 512 * what + j * P:512 * what + (j + 1) * P],
                                  wag_t[rows, what * SEQ:(what + 1) * SEQ], start=True, stop=True)\
                            .then_inc(lora_mm, 1)

            between = {9: [kk_sums], 11: [lambda: lora(0)], 13: [lambda: lora(1)], 15: [lambda: lora(2)],
                       17: [lambda: lora(3)]}
            for q in range(len(PROJ)):
                b = q % PROJ_BANKS
                pe.wait_ge(proj_free[b], q // PROJ_BANKS + 1)
                up_tile(PROJ_IN + q, q % 2, ps[b], 1)
                for more in between.get(q, []):
                    more()

            pe.wait_ge(lora_act, 16)
            pe.wait_ge(tile_done, 16)
            for j in range(JT):
                if j >= 2:
                    pe.wait_ge(vtok_out, j - 1)
                for c in range(NC):
                    last = pe.transpose(ps[6 + j % 2][:, c * P:(c + 1) * P],
                                        v_t[:, j * SEQ + c * CHUNK:j * SEQ + (c + 1) * CHUNK], ident[:, :])
                last.then_inc(vtok_mm, 1)
            for j in range(JT):
                pe.wait_ge(vtok_out, j + 3) if j < 2 else pe.wait_ge(bonus_out, j - 1)
                pe.wait_ge(bonus_in, j + 1)
                pe.matmul(ps[6 + j % 2][:, :], head_ones[:, :], ch(k_t, j), start=True, stop=True)\
                    .then_inc(bonus_mm, 1)
            pe.wait_ge(prep_done, 2 * JT)
            pe.wait_ge(diag_set, 3)
            for b in range(PROJ_BANKS):
                pe.wait_ge(proj_free[b], len(PROJ) // PROJ_BANKS + 1)

            rings = [0]
            head_rows = [slice(0, 64), slice(64, 128)]

            def ring():
                b, use = rings[0] % 2, rings[0] // 2
                rings[0] += 1
                if use:
                    pe.wait_ge(ring_free[b], use)
                return ps[b]

            def products(i):
                n, half = turns[i]
                for d in range(2):
                    for u in range(4):
                        j, rows, c = 2 * half + u // 2, head_rows[u % 2], chunk(n, d)
                        bank = ring()
                        c0 = ((d * JT + j) * NC + c) * 2 * CHUNK
                        t0 = (d * JT + j) * SEQ + c * CHUNK
                        q_and_r = qr[rows, c0:c0 + 2 * CHUNK]
                        pe.matmul(bank[:, 0:256], b_m[rows, t0:t0 + CHUNK], q_and_r, start=True, stop=True)
                        pe.matmul(bank[:, 256:512], k_m[rows, t0:t0 + CHUNK], q_and_r, start=True, stop=True)\
                            .then_inc(prod_mm, 1)

            def rows_of(t, d):
                return t[:, d * 4 * P:(d + 1) * 4 * P]

            def tile_of(t, d, u):
                return t[:, (4 * d + u) * P:(4 * d + u + 1) * P]

            eyes, two_eyes = (t[:, :].rearrange("p (a s) -> p a s", a=1).to_broadcast([P, 4, P])
                              for t in (ident_r, two_r))

            def level_step(i, m):
                n, half = turns[i]
                done = i * LEVELS + m
                for d in range(2):
                    px = ps[2 + d]
                    if m == 0:
                        pe.wait_ge(at_ready[d], i + 1)
                        if i:
                            pe.wait_ge(e_ready[d], i)
                    else:
                        pe.wait_ge(y_ready[d], done)
                        if m >= 2:
                            pe.wait_ge(x_ready[d], i * (LEVELS - 1) + m - 1)
                    pe.matmul(px[:, :].rearrange("p (u s) -> p u s", u=4), ident_r[:, :], eyes, start=True, stop=True)
                    for u in range(4):
                        x_now = ident_r[:, :] if m == 0 else tile_of(tt_i if m == 1 else x_i, d, u)
                        last = pe.matmul(px[:, u * P:(u + 1) * P], tile_of(at_r, d, u), x_now, start=False, stop=True,
                                         skip_group_check=True)
                    last.then_inc(lx_mm[d], 1)
                for d in range(2):
                    pe.wait_ge(t_ready[d], done + 1)
                    px, py = ps[2 + d], ps[4 + d]
                    if m == 0 and i:
                        pe.wait_ge(inv_ready[d], i)
                    y_now = [ident_r[:, :] if m == 0 else tile_of(y_i, d, u) for u in range(4)]
                    if m:
                        for u in range(4):
                            last = pe.matmul(px[:, u * P:(u + 1) * P], y_now[u], tile_of(tt_i, d, u),
                                             start=True, stop=True)
                        last.then_inc(xn_mm[d], 1)
                    for u in range(4):
                        last = pe.matmul(py[:, u * P:(u + 1) * P], tile_of(tt_i, d, u), y_now[u],
                                         start=True, stop=True)
                    last.then_inc(yn_mm[d], 1)

            def newton(i):
                n, half = turns[i]
                for d in range(2):
                    px = ps[2 + d]
                    pe.wait_ge(x_ready[d], (i + 1) * (LEVELS - 1))
                    pe.matmul(px[:, :].rearrange("p (u s) -> p u s", u=4), ident_r[:, :], two_eyes,
                              start=True, stop=True)
                    pe.matmul(px[:, :], minus_r[:, :], rows_of(x_i, d), start=False, stop=True, skip_group_check=True)
                    for u in range(4):
                        last = pe.matmul(px[:, u * P:(u + 1) * P], prod(half, d, u, "qb"),
                                         tile_of(x_i, d, u).bitcast(F32), start=False, stop=True,
                                         skip_group_check=True)
                    last.then_inc(nw_mm[d], 1)
                for d in range(2):
                    py = ps[4 + d]
                    pe.wait_ge(y_ready[d], (i + 1) * LEVELS)
                    pe.wait_ge(e_ready[d], i + 1)
                    for u in range(4):
                        last = pe.matmul(py[:, u * P:(u + 1) * P], tile_of(e_i, d, u),
                                         tile_of(y_i, d, u).bitcast(F32), start=True, stop=True)
                    last.then_inc(in_mm[d], 1)

            def tokens(i):
                n, half = turns[i]
                if n == NC - 1:
                    return
                for t in (b_m, k_m):
                    bank = ring()
                    for d in range(2):
                        for jj in range(2):
                            t0 = (d * JT + 2 * half + jj) * SEQ + chunk(n, d) * CHUNK
                            last = pe.transpose(bank[:, (2 * d + jj) * P:(2 * d + jj + 1) * P],
                                                t[:, t0:t0 + CHUNK], ident[:, :])
                    last.then_inc(tok_mm, 1)

            pairs = [(d, jj) for d in range(2) for jj in range(2)]

            def pair_at(d, jj):
                return slice((2 * d + jj) * P, (2 * d + jj + 1) * P)

            def state_of(half, d, jj):
                return state[:, (4 * half + 2 * d + jj) * P:(4 * half + 2 * d + jj + 1) * P]

            def qr_of(i, d, jj, w):
                n, half = turns[i]
                c0 = (((d * JT + 2 * half + jj) * NC + chunk(n, d)) * 2 + w) * CHUNK
                return qr[:, c0:c0 + CHUNK]

            def head_at(d, u):
                return slice((4 * d + u) * HEAD, (4 * d + u + 1) * HEAD)

            def v_of(i, d, u, n_heads=1):
                n, half = turns[i]
                c0 = chunk(n, d) * WIDTH + (4 * half + u) * HEAD
                return v_tok[:, c0:c0 + n_heads * HEAD]

            def run_w(i):
                n, half = turns[i]
                if i:
                    pe.wait_ge(u_out, i)
                else:
                    pe.wait_ge(vtok_out, JT)
                    pe.wait_ge(bonus_out, JT)
                if i >= 2 and n:
                    pe.wait_ge(s_out, 4 * (i - 1))
                for d, jj in pairs:
                    if n:
                        pe.matmul(ps[6][:, pair_at(d, jj)], qr_of(i, d, jj, 0), state_of(half, d, jj),
                                  start=True, stop=True)
                    for u in (2 * jj, 2 * jj + 1):
                        last = pe.matmul(ps[6][:, head_at(d, u)], prod(half, d, u, "qk"), v_of(i, d, u),
                                         start=n == 0, stop=True, skip_group_check=True)
                last.then_inc(w_mm, 1)

            def run_u(i):
                n, half = turns[i]
                pe.wait_ge(w_out_s, i + 1)
                for d in range(2):
                    pe.wait_ge(inv_ready[d], i + 1)
                for d in range(2):
                    for u in range(4):
                        c0 = unit(half, d, u) * P
                        last = pe.matmul(ps[6][:, head_at(d, u)], inv[:, c0:c0 + P], w_c[:, head_at(d, u)],
                                         start=True, stop=True)
                last.then_inc(u_mm, 1)

            def run_y(i):
                n, half = turns[i]
                pe.wait_ge(u_out, i + 1)
                if i:
                    pe.wait_ge(s_sum, i) if turns[i - 1][0] < NC - 1 else pe.wait_ge(y_out, 2 * i)
                for d, jj in pairs:
                    if n:
                        pe.matmul(ps[7][:, pair_at(d, jj)], state_of(half, d, jj), qr_of(i, d, jj, 1),
                                  start=True, stop=True)
                    for u in (2 * jj, 2 * jj + 1):
                        o = ps[7][head_rows[u % 2], pair_at(d, jj)]
                        pe.matmul(o, u_c[:, head_at(d, u)], prod(half, d, u, "rb"), start=n == 0, stop=False,
                                  skip_group_check=True)
                        last = pe.matmul(o, v_of(i, d, u), prod(half, d, u, "rk"), start=False, stop=True,
                                         skip_group_check=True)
                last.then_inc(y_mm, 1)

            def run_state(i):
                n, half = turns[i]
                if n == NC - 1:
                    return
                pe.wait_ge(tok_out, 2 * (i + 1))
                pe.wait_ge(y_out, 2 * (i + 1))
                for d, jj in pairs:
                    o, t = ps[7][:, pair_at(d, jj)], pair_at(d, jj)
                    pe.matmul(o, b_tok[:, t], u_c[:, t], start=True, stop=False)
                    last = pe.matmul(o, k_tok[:, t], v_of(i, d, 2 * jj, 2), start=False, stop=True)
                last.then_inc(s_mm, 1)

            def conv_sum():
                for j in range(JT):
                    pe.wait_ge(conv_done, j + 1)
                    last = pe.matmul(ps[2][:, :], ones[:, :], ch(conv_t, j), start=j == 0, stop=j == JT - 1)
                last.then_inc(cn_sum, 1)

            def conv_var():
                for j in range(JT):
                    pe.wait_ge(cn_sq, j + 1)
                    last = pe.matmul(ps[3][:, :], ones[:, :], ch(cn_t, j), start=j == 0, stop=j == JT - 1)
                last.then_inc(cn_var, 1)

            steps = {"products": products, "level": level_step, "newton": newton, "tokens": tokens, "w": run_w,
                     "u": run_u, "y": run_y, "state": run_state, "conv_sum": conv_sum, "conv_var": conv_var}
            for what, *which in schedule:
                steps[what](*which)

            pe.wait_ge(y_out, 2 * len(turns))
            pe.wait_ge(cn_root, 1)
            for j in range(JT):
                pe.matmul(ps[j][:, :], head_ones[:, :], ch(y_t, j), start=True, stop=True).then_inc(gn_sum, 1)
            for j in range(JT):
                if j >= 2:
                    pe.wait_ge(gate_out, j - 1)
                b = ps[6 + j % 2]
                pe.matmul(b[:, :], lora_s[:, 1024 + j * P:1024 + (j + 1) * P], ch(wag_t, 2), start=True, stop=False)
                pe.matmul(b[:, :], lora_s[0:32, 1536 + j * P:1536 + (j + 1) * P], wag_t[0:32, 3 * SEQ:4 * SEQ],
                          start=False, stop=True).then_inc(gate_mm, 1)
            for j in range(JT):
                pe.wait_ge(gn_sq, j + 1)
                b = ps[(4, 5, 0, 1)[j]]
                pe.matmul(b[:, :], head_ones[:, :], ch(gn_sq_t, j), start=True, stop=True).then_inc(gn_var, 1)

            pe.wait_ge(gn_std, JT)
            pe.wait_ge(gate_out, JT)
            for i in range(KT):
                pe.wait_ge(mix_low, i + 1)
                down_tile(MIX_OUT + i, i % 2, (i + JT) % KT, x_hi, x_lo, i == 0, i == KT - 1)
            layer_sums(1)

            swiglu(FFN2_IN, FFN2_OUT, 1)
            layer_sums(2)

        @block.scalar
        def _(act):
            def high(g, s, turn):
                act.wait_ge(raw_landed[s], turn * 16 + 16)
                act.wait_ge(weights_used, g + 1)
                act.activation(w_hi[s][:, :], raw[s][:, :], ACT.Copy).then_inc(hi_ready, 1)

            def swiglu(in0, out0, e, last):
                with act.Fori(0, FT // 2) as i:
                    for s in range(2):
                        g = i * 4 + (in0 + 2 * s)
                        high(g + 2, 0, i * 2 + (in0 // 2 + s + 1))
                        act.wait_ge(weights_used, g + 3)
                        act.wait_ge(pairs_free, i * 2 + (s + 1 + FT * e))
                        act.activation(ch(sig, s), ps[2 * s][:, :], ACT.Sigmoid).then_inc(sig_ready, 1)
                        high(g + 3, 1, i * 2 + (in0 // 2 + s + 1))
                with act.Fori(0, FT // 2 - last) as i:
                    for s in range(2):
                        high(i * 2 + (out0 + 2 + s), s, i + (out0 // 2 + 1))

            def norm(n):
                for k in range(KT):
                    act.wait_ge(ln_centered, KT * n + k + 1)
                    act.activation(ch(sq_ln, k), ch(y_ln, k), ACT.Square).then_inc(ln_squared, 1)
                act.wait_ge(ln_var, n + 1)
                act.activation(std[:, :], ps[1][:, :], ACT.Sqrt, scale=1.0 / D_MODEL, bias=eps[n][:, :])\
                    .then_inc(ln_std, 1)
                for k in range(KT):
                    act.wait_ge(ln_norm, KT * n + k + 1)
                    gain = dict(scale=col(f"ln{n + 1}_g", k), bias=col(f"ln{n + 1}_b", k))
                    act.activation(ch(x32, k), ch(y_ln, k), ACT.Identity, **gain).then_inc(ln_out, 1)
                    if n < 2:
                        act.activation(ch(x_hi, k), ch(y_ln, k), ACT.Identity, **gain).then_inc(x_high, 1)

            high(0, 0, 0)
            for k in range(KT):
                act.wait_ge(x_loaded[k // 2], 16)
                act.activation(ch(x_hi, k), ch(x32, k), ACT.Copy).then_inc(x_high, 1)
            high(1, 1, 0)
            act.wait_ge(consts_loaded, 80)
            act.wait_ge(eps_set, 4)
            swiglu(FFN1_IN, FFN1_OUT, 0, 0)
            norm(0)

            def wag_functions():
                act.wait_ge(tile_done, 4)
                act.activation(ch(wag_t, 0), ch(wag_t, 0), ACT.Tanh).then_inc(act_in, 1)
                act.activation(ch(wag_t, 2, 2), ch(wag_t, 2, 2), ACT.Sigmoid).then_inc(act_in, 1)

            def kk_squares():
                for j in range(JT):
                    act.wait_ge(kk_in, j + 1)
                    act.activation(ch(tmp, j), ch(kk_t, j), ACT.Square).then_inc(kk_sq, 1)

            def kk_roots():
                for j in range(JT):
                    act.wait_ge(kk_ss, j + 1)
                    act.activation(ch(tmp, j), ps[4 + j][:, :], ACT.Sqrt).then_inc(kk_norm, 1)

            def rates(j):
                if j:
                    act.wait_ge(prep_done, 2 * j)
                else:
                    act.wait_ge(kk_ready, 1)
                for d in range(2):
                    act.wait_ge(lora_mm, 4 * j + 2 * d + 1)
                    act.activation(ch(tmp, 5 * d), ps[4 + 2 * d][:, :], ACT.Sigmoid, bias=col("w0", d * JT + j))\
                        .then_inc(lora_act, 1)
                    act.wait_ge(lora_mm, 4 * j + 2 * d + 2)
                    act.activation(ch(tmp, 5 * d + 1), ps[5 + 2 * d][:, :], ACT.Sigmoid, bias=col("a0", d * JT + j))\
                        .then_inc(lora_act, 1)
                    act.wait_ge(lora_act, 4 * j + 2 * d + 2)
                    act.activation(ch(tmp, 5 * d + 2), ch(tmp, 5 * d + 1), ACT.Identity, scale=col("k_a", j),
                                   bias=own[:, 16 + j:17 + j]).then_inc(mult_ready, 1)

            def decays(j):
                act.wait_ge(cum_ready, 2 * j + 2)
                for d in range(2):
                    past, before = ch(tmp, 5 * d + 4), ch(tmp, 5 * d)
                    sources = [(past, 1), (before, -1), (past, -1)] if d == 0 else \
                              [(before, -1), (past, 1), (before, 1)]
                    for w, (src, sign) in enumerate(sources):
                        i = 6 * j + 3 * d + w
                        if i >= 2:
                            act.wait_ge(exp_used, i - 1)
                        act.activation(e_buf(i), src, ACT.Exp, scale=sign * KAPPA).then_inc(exp_ready, 1)

            between = {4: [wag_functions], 8: [kk_squares], 10: [kk_roots]}
            for j in range(JT):
                between[12 + 2 * j] = [lambda j=j: rates(j)]
                between[13 + 2 * j] = [lambda j=j: decays(j)]
            act.wait_ge(own_set, 2)
            parts = 0
            for q, (what, j) in enumerate(PROJ):
                g = PROJ_IN + q
                high(g + 2, q % 2, (g + 2) // 2) if g + 2 < MIX_OUT else None
                act.wait_ge(weights_used, g + 3)
                bank = ps[q % PROJ_BANKS]
                if what == "conv_gate":
                    act.activation(u_t[:, j * ULEN + PAD:j * ULEN + PAD + SEQ], bank[:, :], ACT.Sigmoid)\
                        .then_inc(proj_free[q % PROJ_BANKS], 1)
                elif what != "conv_value":
                    if what == "k" and j == 0:
                        act.wait_ge(spilled, 16)
                    dst = {"wd": (wag_t, 0), "ad": (wag_t, 1), "gd": (wag_t, 2 + j), "k": (k_t, j), "r": (r_t, j),
                           "v": (v_t, j)}[what]
                    m = MU[what, j]
                    act.activation(ch(*dst), bank[:, :], ACT.Identity, scale=own[:, m:m + 1]).then_inc(proj_part, 1)
                for more in between.get(q, []):
                    more()
            act.wait_ge(fac_in, 2 * JT)
            act.activation(fac[:, :], fac[:, :], ACT.Exp, scale=-KAPPA).then_inc(fac_ready, 1)
            act.wait_ge(prep_done, 2 * JT)
            for j in range(JT):
                act.wait_ge(vtok_mm, j + 1)
                act.activation(v_tok[:, :].rearrange("p (c w) -> p c w", c=NC)[:, :, j * P:(j + 1) * P],
                               ps[6 + j % 2][:, :].rearrange("p (c w) -> p c w", c=NC), ACT.Copy).then_inc(vtok_out, 1)

            rings = [0]

            def products(i):
                n, half = turns[i]
                rings[0] += 8
                for d in range(2):
                    act.wait_ge(prod_out, 8 * i + 4 * d + 4)
                    c0 = unit(half, d, 0) * 512
                    act.activation(at_r[:, d * 512:(d + 1) * 512].rearrange("p (u s) -> p u s", u=4),
                                   a_t[:, c0:c0 + 4 * 512].rearrange("p (u w) -> p u w", u=4)[:, :, 0:P],
                                   ACT.Copy).then_inc(at_ready[d], 1)

            def level_step(i, m):
                for d in range(2):
                    if m:
                        act.wait_ge(xn_mm[d], i * (LEVELS - 1) + m)
                        act.activation(x_i[:, d * 512:(d + 1) * 512], ps[2 + d][:, :], ACT.Copy).then_inc(x_ready[d], 1)
                    act.wait_ge(yn_mm[d], i * LEVELS + m + 1)
                    act.activation(y_i[:, d * 512:(d + 1) * 512], ps[4 + d][:, :], ACT.Copy).then_inc(y_ready[d], 1)

            def newton(i):
                n, half = turns[i]
                for d in range(2):
                    act.wait_ge(nw_mm[d], i + 1)
                    act.activation(e_i[:, d * 512:(d + 1) * 512], ps[2 + d][:, :], ACT.Copy).then_inc(e_ready[d], 1)
                for d in range(2):
                    act.wait_ge(in_mm[d], i + 1)
                    c0 = unit(half, d, 0) * P
                    act.activation(inv[:, c0:c0 + 4 * P], ps[4 + d][:, :], ACT.Copy).then_inc(inv_ready[d], 1)

            def tokens(i):
                if turns[i][0] == NC - 1:
                    return
                for t, dst in enumerate((b_tok, k_tok)):
                    act.wait_ge(tok_mm, 2 * i + t + 1)
                    if i:
                        act.wait_ge(s_mm, i)
                    b = rings[0] % 2
                    rings[0] += 1
                    act.activation(dst[:, :], ps[b][:, :], ACT.Copy).then_inc(tok_out, 1)
                    act.wait_ge(tok_out, 2 * i + t + 1)
                    act.sem_inc(ring_free[b], 1)

            def run_w(i):
                act.wait_ge(w_mm, i + 1)
                act.activation(w_c[:, :], ps[6][:, :], ACT.Copy).then_inc(w_out_s, 1)

            def run_u(i):
                act.wait_ge(u_mm, i + 1)
                act.activation(u_c[:, :], ps[6][:, :], ACT.Copy).then_inc(u_out, 1)

            def nothing(i):
                pass

            def conv_sum():
                for j in range(JT):
                    act.wait_ge(cn_cent, j + 1)
                    act.activation(ch(cn_t, j), ch(conv_t, j), ACT.Square).then_inc(cn_sq, 1)

            def conv_var():
                act.wait_ge(cn_var, 1)
                act.activation(ch(cn_std, 0), ps[3][:, :], ACT.Sqrt, scale=1.0 / WIDTH, bias=eps[1][:, :])\
                    .then_inc(cn_root, 1)

            steps = {"products": products, "level": level_step, "newton": newton, "tokens": tokens, "w": run_w,
                     "u": run_u, "y": nothing, "state": nothing, "conv_sum": conv_sum, "conv_var": conv_var}
            for what, *which in schedule:
                steps[what](*which)

            for j in range(JT):
                act.wait_ge(gn_cent, j + 1)
                act.activation(ch(gn_sq_t, j), ch(y_t, j), ACT.Square).then_inc(gn_sq, 1)
            for j in range(JT):
                act.wait_ge(gate_mm, j + 1)
                act.activation(ch(gate_t, j), ps[6 + j % 2][:, :], ACT.Copy).then_inc(gate_out, 1)
            for j in range(JT):
                act.wait_ge(gn_var, j + 1)
                act.activation(ch(gn_std_t, j), ps[(4, 5, 0, 1)[j]][:, :], ACT.Sqrt, scale=1.0 / HEAD,
                               bias=eps[3][:, :]).then_inc(gn_std, 1)
            for j in range(JT):
                act.wait_ge(cn_norm, j + 1)
                act.activation(ch(conv_t, j), ch(conv_t, j), ACT.Identity, scale=col("conv_ln_g", j),
                               bias=col("conv_ln_b", j)).then_inc(cn_z, 1)
            for j in range(JT):
                act.wait_ge(cn_z, j + 1)
                act.activation(ch(cn_t, j), ch(conv_t, j), ACT.Sigmoid).then_inc(cn_sig, 1)
            act.wait_ge(conv_out, JT)
            high(MIX_OUT, 0, MIX_OUT // 2)
            high(MIX_OUT + 1, 1, MIX_OUT // 2)
            for j in range(JT):
                act.activation(ch(x_hi, JT + j), ch(conv_t, j), ACT.Copy).then_inc(mix_high, 1)
            for j in range(JT):
                act.wait_ge(gn_norm, j + 1)
                act.activation(ch(y_t, j), ch(y_t, j), ACT.Identity, scale=col("lnx_g", j), bias=col("lnx_b", j))\
                    .then_inc(gn_z, 1)
            for j in range(JT):
                act.wait_ge(mix_in, j + 1)
                act.activation(ch(x_hi, j), ch(y_t, j), ACT.Copy).then_inc(mix_high, 1)
            for k in range(KT):
                g = MIX_OUT + 2 + k
                high(g, k % 2, g // 2)
            norm(1)
            swiglu(FFN2_IN, FFN2_OUT, 1, 1)
            norm(2)

        @block.vector
        def _(dve):
            own_steps = [0]

            def step(ins):
                own_steps[0] += 1
                ins.then_inc(vec, 1)
                dve.wait_ge(vec, own_steps[0])

            def low(g, s):
                dve.wait_ge(hi_ready, g + 1)
                dve.tensor_tensor(w_lo[s][:, :], raw[s][:, :], w_hi[s][:, :].bitcast(F32), ALU.subtract)\
                    .then_inc(lo_ready, 1)

            def swiglu(in0, out0, e, last):
                with dve.Fori(0, FT // 2) as i:
                    for s in range(2):
                        g = i * 4 + (in0 + 2 * s)
                        pair = i * 2 + (s + FT * e)
                        low(g + 2, 0)
                        dve.wait_ge(sig_ready, pair + 1)
                        dve.tensor_tensor(ch(h_raw, s), ps[2 * s][:, :], ch(sig, s), ALU.mult).then_inc(gated, 1)
                        low(g + 3, 1)
                        dve.wait_ge(weights_used, g + 4)
                        dve.wait_ge(gated, pair + 1)
                        dve.tensor_tensor(ch(h_raw, s), ps[2 * s + 1][:, :], ch(h_raw, s), ALU.mult)\
                            .then_inc(pairs_free, 1)
                        dve.wait_ge(pairs_free, pair + 3)
                        f = bass.ds(i * (2 * SEQ) + s * SEQ, SEQ)
                        dve.tensor_copy(h_hi[:, f], ch(h_raw, s)).then_inc(h_high, 1)
                        dve.wait_ge(h_high, pair + 1)
                        dve.tensor_tensor(h_lo[:, f], ch(h_raw, s), h_hi[:, f].bitcast(F32), ALU.subtract)\
                            .then_inc(h_ready, 1)
                with dve.Fori(0, FT // 2 - last) as i:
                    for s in range(2):
                        low(i * 2 + (out0 + 2 + s), s)

            def norm(n, items_done, x, residual):
                for k in range(KT):
                    dve.wait_ge(sums_done, (KT - 1) * n + k + 1) if k < KT - 1 else \
                        dve.wait_ge(weights_used, 2 + items_done)
                    dve.scalar_tensor_tensor(ch(y_ln, k), ch(x, k), residual, ps[k][:, :], ALU.mult, ALU.add)\
                        .then_inc(ln_in, 1)
                dve.wait_ge(ln_sum, n + 1)
                for k in range(KT):
                    dve.scalar_tensor_tensor(ch(y_ln, k), ps[0][:, :], -1.0 / D_MODEL, ch(y_ln, k), ALU.mult, ALU.add)\
                        .then_inc(ln_centered, 1)
                dve.wait_ge(ln_std, n + 1)
                dve.reciprocal(rstd[:, :], std[:, :]).then_inc(ln_rstd, 1)
                dve.wait_ge(ln_rstd, n + 1)
                for k in range(KT + 2):
                    if k < KT:
                        dve.tensor_tensor(ch(y_ln, k), ch(y_ln, k), rstd[:, :], ALU.mult).then_inc(ln_norm, 1)
                    if n < 2 and k >= 2:
                        dve.wait_ge(x_high, KT * (n + 1) + k - 1)
                        dve.tensor_tensor(ch(x_lo, k - 2), ch(x32, k - 2), ch(x_hi, k - 2).bitcast(F32), ALU.subtract)\
                            .then_inc(x_low, 1)

            for n, value in enumerate((4 * LN_EPS, LN_EPS, 4 * LN_EPS, GN_EPS)):
                dve.memset(eps[n][:, :], value).then_inc(eps_set, 1)
            step(dve.memset(h_reset[:, :], 1.0))
            step(dve.memset(h_reset[:, :].rearrange("p (c t) -> p c t", c=NC)[:, :, 0:1], 0.0))
            low(0, 0)
            for k in range(KT):
                dve.wait_ge(x_high, k + 1)
                dve.tensor_tensor(ch(x_lo, k), ch(x32, k), ch(x_hi, k).bitcast(F32), ALU.subtract).then_inc(x_low, 1)
            low(1, 1)
            dve.wait_ge(consts_loaded, 80)
            step(dve.tensor_copy(level[:, :], level_f[:, :]))
            dve.tensor_copy(ident_r[:, :], ident[:, :]).then_inc(diag_set, 1)
            dve.tensor_scalar(two_r[:, :], ident[:, :], 2.0, None, ALU.mult).then_inc(diag_set, 1)
            dve.tensor_scalar(minus_r[:, :], ident[:, :], -1.0, None, ALU.mult).then_inc(diag_set, 1)
            p0, n0 = PAR["mu_prev"], PAR["mu_next"]
            step(dve.tensor_tensor(own[:, 0:16], par[:, p0:p0 + 16], par[:, n0:n0 + 16], ALU.add))
            dve.tensor_scalar(own[:, 0:16], own[:, 0:16], -1.0, 1.0, ALU.mult, ALU.add).then_inc(own_set, 1)
            dve.tensor_scalar(own[:, 16:16 + JT], par[:, PAR["k_a"]:PAR["k_a"] + JT], -1.0, 1.0, ALU.mult, ALU.add)\
                .then_inc(own_set, 1)

            swiglu(FFN1_IN, FFN1_OUT, 0, 0)
            norm(0, PROJ_IN, x32, 2 * ALPHA)

            taps = [(j, k) for j in range(JT) for k in range(TAPS)]

            def tap(j, k):
                window = u_t[:, j * ULEN + k:j * ULEN + k + SEQ]
                weight = par[:, PAR["conv_dw"] + k * JT + j:PAR["conv_dw"] + k * JT + j + 1]
                if k == 0:
                    step(dve.tensor_scalar(ch(conv_t, j), window, weight, col("conv_b", j), ALU.mult, ALU.add))
                elif k < TAPS - 1:
                    step(dve.scalar_tensor_tensor(ch(conv_t, j), window, weight, ch(conv_t, j), ALU.mult, ALU.add))
                else:
                    dve.scalar_tensor_tensor(ch(conv_t, j), window, weight, ch(conv_t, j), ALU.mult, ALU.add)\
                        .then_inc(conv_done, 1)

            def kk_normalized():
                dve.wait_ge(kk_norm, JT)
                step(dve.tensor_scalar(ch(tmp, 0, 4), ch(tmp, 0, 4), NORM_EPS, None, ALU.max))
                step(dve.reciprocal(ch(tmp, 0, 4), ch(tmp, 0, 4)))
                dve.tensor_tensor(kk_t[:, :], kk_t[:, :], ch(tmp, 0, 4), ALU.mult).then_inc(kk_ready, 1)
                dve.wait_ge(kk_ready, 1)

            def sums(j):
                for d in range(2):
                    rate, a, kd, cum, past = (ch(tmp, 5 * d + i) for i in range(5))
                    c_view = cum.rearrange("p (c t) -> p c t", c=NC)
                    p_view = past.rearrange("p (c t) -> p c t", c=NC)
                    dve.wait_ge(mult_ready, 2 * j + d + 1)
                    step(dve.tensor_tensor_scan(cum, h_reset[:, :], rate, 0.0, ALU.mult, ALU.add))
                    step(dve.tensor_tensor(p_view, c_view, c_view[:, :, MID:MID + 1].to_broadcast([P, NC, CHUNK]),
                                           ALU.subtract))
                    f0 = (d * JT + j) * (NC - 1)
                    dve.tensor_tensor(fac[:, f0:f0 + NC - 1].rearrange("p (c a) -> p c a", a=1),
                                      p_view[:, 0:NC - 1, CHUNK - 1:CHUNK], c_view[:, 1:NC, MID:MID + 1],
                                      ALU.add).then_inc(fac_in, 1)
                    dve.tensor_tensor(rate, past, rate, ALU.subtract).then_inc(cum_ready, 1)
                    step(dve.tensor_tensor(kd, kd, ch(k_t, j), ALU.mult))
                    step(dve.tensor_tensor(a, a, ch(kk_t, j), ALU.mult))

            def operands(j):
                for d in range(2):
                    a, kd = ch(tmp, 5 * d + 1), ch(tmp, 5 * d + 2)
                    slot = (d * JT + j) * SEQ
                    q_view = qr[:, 2 * slot:2 * slot + 2 * SEQ].rearrange("p (c w t) -> p c w t", c=NC, w=2)
                    i = 6 * j + 3 * d
                    dve.wait_ge(exp_ready, i + 1)
                    dve.tensor_tensor(b_m[:, slot:slot + SEQ], a, e_buf(i), ALU.mult)
                    dve.tensor_tensor(k_m[:, slot:slot + SEQ], kd, e_buf(i), ALU.mult).then_inc(exp_used, 1)
                    dve.wait_ge(exp_ready, i + 2)
                    dve.scalar_tensor_tensor(q_view[:, :, 0, :], ch(kk_t, j).rearrange("p (c t) -> p c t", c=NC), -1.0,
                                             e_buf(i + 1).rearrange("p (c t) -> p c t", c=NC), ALU.mult, ALU.mult)\
                        .then_inc(exp_used, 1)
                    dve.wait_ge(exp_ready, i + 3)
                    dve.tensor_tensor(q_view[:, :, 1, :], ch(r_t, j).rearrange("p (c t) -> p c t", c=NC),
                                      e_buf(i + 2).rearrange("p (c t) -> p c t", c=NC), ALU.mult)\
                        .then_inc(exp_used, 1)
                    dve.wait_ge(exp_used, i + 3)
                    if d:
                        step(dve.tensor_tensor(ch(k_t, j), ch(tmp, 2), kd, ALU.add))
                        dve.scalar_tensor_tensor(ch(k_t, j), ch(k_t, j), col("r_k", j), ch(r_t, j),
                                                 ALU.mult, ALU.mult).then_inc(bonus_in, 1)
                        dve.wait_ge(bonus_in, j + 1)
                    dve.sem_inc(prep_done, 1)

            between = {11: [kk_normalized]}
            for j in range(JT):
                between[12 + 2 * j] = [lambda j=j: sums(j)]
                between[13 + 2 * j] = [lambda j=j: operands(j)]
            parts = 0
            dve.wait_ge(pads_set, 2 * JT)
            for q, (what, j) in enumerate(PROJ):
                g = PROJ_IN + q
                low(g + 2, q % 2) if g + 2 < MIX_OUT else None
                bank, free = ps[q % PROJ_BANKS], proj_free[q % PROJ_BANKS]
                if what == "conv_value":
                    dve.wait_ge(weights_used, g + 3)
                    dve.wait_ge(proj_free[(q - 1) % PROJ_BANKS], 2 + q // PROJ_BANKS)
                    u = u_t[:, j * ULEN + PAD:j * ULEN + PAD + SEQ]
                    step(dve.tensor_tensor(u, bank[:, :], u, ALU.mult))
                    dve.sem_inc(free, 1)
                    dve.sem_inc(tile_done, 1)
                elif what != "conv_gate":
                    parts += 1
                    dst, i = {"wd": (wag_t, 0), "ad": (wag_t, 1), "gd": (wag_t, 2 + j), "k": (k_t, j), "r": (r_t, j),
                              "v": (v_t, j)}[what]
                    m, c0 = MU[what, j], i * SEQ
                    dve.wait_ge(proj_part, parts)
                    later, earlier = dst[:, c0 + 1:c0 + SEQ], dst[:, c0:c0 + SEQ - 1]
                    step(dve.scalar_tensor_tensor(later, bank[:, 0:SEQ - 1], col("mu_prev", m), later,
                                                  ALU.mult, ALU.add))
                    step(dve.scalar_tensor_tensor(earlier, bank[:, 1:SEQ], col("mu_next", m), earlier,
                                                  ALU.mult, ALU.add))
                    dve.sem_inc(free, 1)
                    dve.sem_inc(tile_done, 1)
                    if what == "k":
                        dve.tensor_scalar(ch(kk_t, j), ch(k_t, j), col("k_k", j), None, ALU.mult).then_inc(kk_in, 1)
                for more in between.get(q, []):
                    more()
            for j in range(JT):
                dve.wait_ge(bonus_mm, j + 1)
                dve.tensor_tensor(ch(v_t, j), ps[6 + j % 2][:, :], ch(v_t, j), ALU.mult).then_inc(bonus_out, 1)

            rings = [0]

            def products(i):
                n, half = turns[i]
                for d in range(2):
                    for u in range(4):
                        b = rings[0] % 2
                        rings[0] += 1
                        dve.wait_ge(prod_mm, 8 * i + 4 * d + u + 1)
                        c0 = unit(half, d, u) * 512
                        dve.tensor_tensor(a_t[:, c0:c0 + 512], ps[b][:, :], tri[:, d * 512:(d + 1) * 512], ALU.mult)\
                            .then_inc(prod_out, 1)
                        dve.wait_ge(prod_out, 8 * i + 4 * d + u + 1)
                        dve.sem_inc(ring_free[b], 1)

            def some_taps():
                for _ in range(2):
                    if taps:
                        tap(*taps.pop(0))

            def level_step(i, m):
                for d in range(2):
                    dve.wait_ge(lx_mm[d], i * LEVELS + m + 1)
                    l0 = (d * LEVELS + m) * P
                    dve.tensor_tensor(tt_i[:, d * 512:(d + 1) * 512].rearrange("p (u s) -> p u s", u=4),
                                      ps[2 + d][:, :].rearrange("p (u s) -> p u s", u=4),
                                      level[:, l0:l0 + P].rearrange("p (a s) -> p a s", a=1).to_broadcast([P, 4, P]),
                                      ALU.mult).then_inc(t_ready[d], 1)
                some_taps()

            def newton(i):
                some_taps()

            def tokens(i):
                if turns[i][0] < NC - 1:
                    rings[0] += 2

            def run_y(i):
                n, half = turns[i]
                dve.wait_ge(y_mm, i + 1)
                for d in range(2):
                    dst = y_t[:, 2 * half * SEQ:(2 * half + 2) * SEQ].rearrange("p (j c t) -> p j c t", j=2, c=NC)[
                        :, :, chunk(n, d), :]
                    src = ps[7][:, 2 * d * CHUNK:(2 * d + 2) * CHUNK].rearrange("p (j t) -> p j t", j=2)
                    if n < NC // 2:
                        dve.tensor_copy(dst, src).then_inc(y_out, 1)
                    else:
                        dve.tensor_tensor(dst, src, dst, ALU.add).then_inc(y_out, 1)

            def run_state(i):
                n, half = turns[i]
                if n == NC - 1:
                    return
                dve.wait_ge(s_mm, i + 1)
                now = state[:, half * 4 * P:(half + 1) * 4 * P]
                if n:
                    dve.tensor_tensor(s_new[:, :], ps[7][:, :], now, ALU.add).then_inc(s_sum, 1)
                else:
                    dve.tensor_copy(s_new[:, :], ps[7][:, :]).then_inc(s_sum, 1)
                dve.wait_ge(s_sum, i + 1)
                for d in range(2):
                    for jj in range(2):
                        f = (d * JT + 2 * half + jj) * (NC - 1) + (n if d == 0 else NC - 2 - n)
                        c0 = (2 * d + jj) * P
                        dve.scalar_tensor_tensor(now[:, c0:c0 + P], s_new[:, c0:c0 + P], fac[:, f:f + 1],
                                                 head_ones[:, :], ALU.mult, ALU.mult).then_inc(s_out, 1)

            def nothing(i):
                pass

            def conv_sum():
                dve.wait_ge(cn_sum, 1)
                for j in range(JT):
                    dve.scalar_tensor_tensor(ch(conv_t, j), ps[2][:, :], -1.0 / WIDTH, ch(conv_t, j),
                                             ALU.mult, ALU.add).then_inc(cn_cent, 1)

            def conv_var():
                dve.wait_ge(cn_root, 1)
                step(dve.reciprocal(ch(cn_std, 1), ch(cn_std, 0)))
                for j in range(JT):
                    dve.tensor_tensor(ch(conv_t, j), ch(conv_t, j), ch(cn_std, 1), ALU.mult).then_inc(cn_norm, 1)

            steps = {"products": products, "level": level_step, "newton": newton, "tokens": tokens, "w": nothing,
                     "u": nothing, "y": run_y, "state": run_state, "conv_sum": conv_sum, "conv_var": conv_var}
            for what, *which in schedule:
                steps[what](*which)

            for j in range(JT):
                dve.wait_ge(gn_sum, j + 1)
                dve.scalar_tensor_tensor(ch(y_t, j), ps[j][:, :], -1.0 / HEAD, ch(y_t, j), ALU.mult, ALU.add)\
                    .then_inc(gn_cent, 1)
            dve.wait_ge(gn_std, JT)
            step(dve.reciprocal(gn_std_t[:, :], gn_std_t[:, :]))
            for j in range(JT):
                dve.tensor_tensor(ch(y_t, j), ch(y_t, j), ch(gn_std_t, j), ALU.mult).then_inc(gn_norm, 1)
            for j in range(JT):
                dve.wait_ge(cn_sig, j + 1)
                dve.tensor_tensor(ch(conv_t, j), ch(conv_t, j), ch(cn_t, j), ALU.mult).then_inc(conv_out, 1)
            low(MIX_OUT, 0)
            low(MIX_OUT + 1, 1)
            for j in range(JT):
                dve.wait_ge(mix_high, j + 1)
                dve.tensor_tensor(ch(x_lo, JT + j), ch(conv_t, j), ch(x_hi, JT + j).bitcast(F32), ALU.subtract)\
                    .then_inc(mix_low, 1)
            for j in range(JT):
                dve.wait_ge(gn_z, j + 1)
                step(dve.tensor_tensor(ch(y_t, j), ch(y_t, j), ch(v_t, j), ALU.add))
                dve.tensor_tensor(ch(y_t, j), ch(y_t, j), ch(gate_t, j), ALU.mult).then_inc(mix_in, 1)
            for j in range(JT):
                dve.wait_ge(mix_high, JT + j + 1)
                dve.tensor_tensor(ch(x_lo, j), ch(y_t, j), ch(x_hi, j).bitcast(F32), ALU.subtract).then_inc(mix_low, 1)
            for k in range(KT):
                low(MIX_OUT + 2 + k, k % 2)
            dve.wait_ge(reloaded, 16)
            norm(1, FFN2_IN, x_back, ALPHA)
            swiglu(FFN2_IN, FFN2_OUT, 1, 1)
            norm(2, N_ITEMS, x32, 2 * ALPHA)


def kernel(**inputs):
    import numpy as np
    import concourse.bacc as bacc
    from concourse.bass_utils import run_bass_kernel_spmd

    a = {k: np.ascontiguousarray(v) for k, v in inputs.items()}
    f32 = np.float32

    def columns(v):
        v = v.reshape(-1)
        n = -(-v.size // P)
        out = np.zeros((n * P,), v.dtype)
        out[:v.size] = v
        return out.reshape(n, P).T

    def in_tile(w):
        full = np.zeros((D_MODEL, P), w.dtype)
        full[:, :w.shape[1]] = w
        return full.reshape(KT, P, P).transpose(1, 0, 2).reshape(P, KT * P)

    w_in = a["w_in"][0]
    shift = 3 * WIDTH + 4 * 64 + 160
    starts = {"r": 0, "k": WIDTH, "v": 2 * WIDTH, "wd": 3 * WIDTH, "ad": 3 * WIDTH + 128, "gd": 3 * WIDTH + 256,
              "conv_value": shift, "conv_gate": shift + WIDTH}
    tiles = []

    def ffn(w1, w2):
        for f in range(FT):
            tiles.append(in_tile(w1[:, f * P:(f + 1) * P]))
            tiles.append(in_tile(w1[:, D_FF + f * P:D_FF + (f + 1) * P]))
        for f in range(FT):
            tiles.append(w2[f * P:(f + 1) * P, :])

    ffn(a["ffn1_w_in"][0], a["ffn1_w_out"][0])
    for what, j in PROJ:
        c0 = starts[what] + j * P
        c1 = min(c0 + P, shift) if what == "gd" else c0 + P
        tiles.append(in_tile(w_in[:, c0:c1]))
    for i in range(KT):
        k = (i + JT) % KT
        tiles.append(a["w_out"][0][k * P:(k + 1) * P, :])
    ffn(a["ffn2_w_in"][0], a["ffn2_w_out"][0])
    weights = np.stack(tiles)

    order = sorted(PAR, key=PAR.get)
    params = np.ascontiguousarray(np.concatenate([columns(a[name][0]) for name in order], axis=1))
    lora = np.ascontiguousarray(np.concatenate(
        [a["w2"][0].reshape(128, WIDTH), a["a2"][0].reshape(128, WIDTH), a["g2"][0, :128]], axis=1))
    gate_tail = np.ascontiguousarray(a["g2"][0, 128:])
    x_t = np.ascontiguousarray(a["x"][0].T.reshape(KT, P, SEQ).transpose(1, 0, 2).reshape(P, KT * SEQ))

    src, dst = np.arange(CHUNK)[:, None], np.arange(CHUNK)[None, :]
    tri = []
    for strict, whole in ((dst > src, dst >= src), (dst < src, dst <= src)):
        tri += [strict, whole, strict, whole]
    tri = np.concatenate(tri, axis=1).astype(f32)
    level = []
    for d in range(2):
        for m in range(LEVELS):
            row, colm = (src, dst) if d == 0 else (dst, src)
            level.append((src == dst) | (row >> (m + 1) == colm >> (m + 1)) & ((row >> m) % 2 == 1) & ((colm >> m) % 2 == 0))
    level = np.concatenate(level, axis=1).astype(f32)
    arrays = {
        "x_t": x_t, "weights": weights, "params": params, "lora": lora, "gate_tail": gate_tail,
        "ident_c": np.eye(P, dtype=f32), "head_ones_c": np.kron(np.eye(2, dtype=f32), np.ones((64, 64), f32)),
        "tri_c": tri, "level_c": level,
    }
    nc = bacc.Bacc("TRN2", target_bir_lowering=False, num_devices=1)
    aps = {n: nc.dram_tensor(n + "_in", v.shape, mybir.dt.from_np(v.dtype), kind="ExternalInput").ap()
           for n, v in arrays.items()}
    out_t = nc.dram_tensor("out_t", (P, KT * SEQ), F32, kind="ExternalOutput").ap()
    encoder_block(nc, out_t=out_t, **aps)
    got = run_bass_kernel_spmd(nc, [{n + "_in": v for n, v in arrays.items()}], core_ids=[0])
    y = got.results[0]["out_t"].reshape(P, KT, SEQ)
    return y.transpose(1, 0, 2).reshape(D_MODEL, SEQ).T[None]
```

```python
from contextlib import ExitStack
import math

import concourse.bass as bass
from concourse import mybir

F32 = mybir.dt.float32
F32R = mybir.dt.float32r
F16 = mybir.dt.float16
U8 = mybir.dt.uint8
ALU = mybir.AluOpType
ACT = mybir.ActivationFunctionType

P = 128
SEQ = 512
D_MODEL = 1024
D_FF = 2816
WIDTH = 512
HEAD = 64
TAPS = 31
PAD = TAPS // 2
KT = D_MODEL // P
FT = D_FF // P
JT = WIDTH // P
CHUNK = 128
NC = SEQ // CHUNK
MID = CHUNK // 2 - 1
LEVELS = 7
ALPHA = 2.0 ** 0.25
LN_EPS = 1e-5
GN_EPS = 64e-5
NORM_EPS = 1e-12
KAPPA = math.exp(-0.5)

PROJ = [("wd", 0), ("ad", 0)] + [("k", j) for j in range(JT)] + [("gd", 0), ("gd", 1)]
PROJ += [("r", j) for j in range(JT)] + [("v", j) for j in range(JT)]
PROJ += [(w, j) for j in range(JT) for w in ("conv_gate", "conv_value")]
PROJ_BANKS = 4
FIRST_K = PROJ.index(("k", 0))
RATES_AT = (9, 12, 15, 19)
LAST_PART_AT = (11, 14, 18, 22)
FFN1_IN = 0
FFN1_OUT = FFN1_IN + 2 * FT
PROJ_IN = FFN1_OUT + FT
MIX_OUT = PROJ_IN + len(PROJ)
FFN2_IN = MIX_OUT + KT
FFN2_OUT = FFN2_IN + 2 * FT
N_ITEMS = FFN2_OUT + FT


def param_columns():
    at, col = {}, 0
    for name, n in (("ln1_g", KT), ("ln1_b", KT), ("ln2_g", KT), ("ln2_b", KT), ("ln3_g", KT), ("ln3_b", KT),
                    ("mu_prev", 16), ("mu_next", 16), ("w0", 2 * JT), ("a0", 2 * JT), ("k_k", JT), ("k_a", JT),
                    ("r_k", JT), ("lnx_g", JT), ("lnx_b", JT), ("conv_dw", TAPS * JT), ("conv_b", JT),
                    ("conv_ln_g", JT), ("conv_ln_b", JT)):
        at[name] = col
        col += n
    return at, col


PAR, N_PAR = param_columns()
MU = {("r", j): j for j in range(4)} | {("k", j): 4 + j for j in range(4)} | {("v", j): 8 + j for j in range(4)}
MU |= {("wd", 0): 12, ("ad", 0): 13, ("gd", 0): 14, ("gd", 1): 15}


def encoder_block(nc, x_t, weights, params, lora, gate_tail, ident_c, head_ones_c, tri_c, level_c, out_t):
    spill = nc.dram_tensor("x1_spill", (P, KT * SEQ), F32, kind="Internal").ap()
    with ExitStack() as ctx:
        def sb(name, cols, dt=F32):
            return ctx.enter_context(nc.sbuf_tensor(name, [P, cols], dt))

        def sem(name):
            return ctx.enter_context(nc.semaphore(name))

        par = sb("par", N_PAR)
        own = sb("own", 16 + JT)
        ident = sb("ident", P)
        ones = sb("ones", P)
        head_ones = sb("head_ones", P)
        tri = sb("tri", 2 * 512)
        level = sb("level", 2 * LEVELS * P, U8)

        ident_h = sb("ident_h", P, F16)
        minus_h = sb("minus_h", P, F16)
        eps = [sb(f"eps{n}", 1) for n in range(4)]
        h_reset = sb("h_reset", SEQ, mybir.dt.bfloat16)

        base = (nc.sbuf_base + 63) // 64 * 64

        def at(name, offset, cols, dt=F32):
            return nc.alloc_sbuf_tensor_at(name, [P, cols], dt, offset=base + offset)

        raw = [at(f"w_raw{s}", 4096 * s, 1024) for s in range(2)]
        w_hi = [at(f"w_hi{s}", 8192 + 4096 * s, 1024, F32R) for s in range(2)]
        w_lo = [at(f"w_lo{s}", 16384 + 4096 * s, 1024, F32R) for s in range(2)]
        x_hi = at("x_hi", 24576, KT * SEQ, F32R)
        x_lo = at("x_lo", 40960, KT * SEQ, F32R)
        x32 = at("x32", 57344, KT * SEQ)
        h_hi = at("h_hi", 73728, FT * SEQ, F32R)
        h_lo = at("h_lo", 118784, FT * SEQ, F32R)
        sig = at("sig", 163840, 2 * SEQ)
        h_raw = at("h_raw", 167936, 2 * SEQ)
        y_ln = at("y_ln", 73728, KT * SEQ)
        sq_ln = at("sq_ln", 90112, KT * SEQ)
        x_back = at("x_back", 114688, KT * SEQ)
        std = at("std", 197120, SEQ)
        rstd = at("rstd", 199168, SEQ)
        level_f = at("level_f", 180736, 2 * LEVELS * P)
        ULEN = SEQ + 2 * PAD
        k_t = at("k_t", 57344, JT * SEQ)
        r_t = at("r_t", 65536, JT * SEQ)
        kk_t = at("kk_t", 73728, JT * SEQ)
        qr = at("qr", 81920, 2 * JT * 2 * SEQ)
        b_m = at("b_m", 114688, 2 * JT * SEQ)
        k_m = at("k_m", 131072, 2 * JT * SEQ)
        v_t = at("v_t", 147456, JT * SEQ)
        u_t = at("u_t", 155648, JT * ULEN)
        wag_t = at("wag_t", 164352, 4 * SEQ)
        lora_s = at("lora_s", 172544, 4 * 512)
        tmp = at("tmp", 180736, 10 * SEQ)
        fac = at("fac", 201216, 2 * JT * (NC - 1))
        tt_i = at("tt_i", 8192, 2 * 4 * P, F16)
        at_r = at("at_r", 10240, 2 * 4 * P, F16)
        x_i = at("x_i", 12288, 2 * 4 * P, F16)
        y_i = at("y_i", 14336, 2 * 4 * P, F16)
        r_i = at("r_i", 16384, 2 * 4 * P, F16)
        x_f = at("x_f", 20480, 2 * 4 * P)
        a_t = at("a_t", 24576, 2 * 2 * 4 * 512)
        inv = at("inv", 57344, 2 * 2 * 4 * P)
        y_t = at("y_t", 65536, JT * SEQ)
        b_tok = at("b_tok", 77824, 4 * P)
        k_tok = at("k_tok", 79872, 4 * P)
        state = at("state", 164352, 8 * P)
        s_new = at("s_new", 172544, 4 * P)
        tapped = at("tapped", 174592, SEQ)
        v_tok = at("v_tok", 180736, NC * WIDTH)
        conv_t = at("conv_t", 188928, JT * SEQ)
        w_c = at("w_c", 197120, 8 * HEAD)
        u_c = at("u_c", 199168, 8 * HEAD)
        cn_std = at("cn_std_t", 131072, 2 * SEQ)
        cn_t = at("cn_t", 135168, JT * SEQ)
        conv_lo = at("conv_lo", 188928, JT * SEQ, F32R)
        gate_t = at("gate_t", 155648, JT * SEQ)
        gn_sq_t = at("gn_sq_t", 81920, JT * SEQ)
        gn_std_t = at("gn_std_t", 98304, JT * SEQ)
        assert base + 201312 <= nc.sbuf_usable_end, (base, nc.sbuf_usable_end)

        ps = [ctx.enter_context(nc.psum_tensor(f"bank{i}", [P, 512], F32)) for i in range(8)]

        def ch(t, j, n=1):
            return t[:, j * SEQ:(j + n) * SEQ]

        def col(name, j=0):
            return par[:, PAR[name] + j:PAR[name] + j + 1]

        consts_loaded = sem("consts_loaded")
        x_loaded = [sem(f"x_loaded{k}") for k in range(KT // 2)]
        lora_loaded = sem("lora_loaded")
        raw_landed = [sem(f"raw_landed{s}") for s in range(2)]
        hi_ready = sem("hi_ready")
        lo_ready = sem("lo_ready")
        weights_used = sem("weights_used")
        pairs_free = sem("pairs_free")
        sig_ready = sem("sig_ready")
        gated = sem("gated")
        h_high = sem("h_high")
        h_ready = sem("h_ready")
        x_high = sem("x_high")
        x_low = sem("x_low")
        ln_in = sem("ln_in")
        ln_sum = sem("ln_sum")
        ln_centered = sem("ln_centered")
        ln_squared = sem("ln_squared")
        ln_var = sem("ln_var")
        ln_std = sem("ln_std")
        ln_rstd = sem("ln_rstd")
        ln_norm = sem("ln_norm")
        ln_out = sem("ln_out")
        ones_set = sem("ones_set")
        eps_set = sem("eps_set")
        own_set = sem("own_set")
        diag_set = sem("diag_set")
        sums_done = sem("sums_done")
        pads_set = sem("pads_set")
        rated = sem("rated")
        pool_taps = sem("pool_taps")
        spilled = sem("spilled")
        reloaded = sem("reloaded")
        proj_free = [sem(f"proj_free{b}") for b in range(PROJ_BANKS)]
        proj_part = sem("proj_part")
        vec = sem("vec")
        tile_done = sem("tile_done")
        conv_done = sem("conv_done")
        cn_sum, cn_cent, cn_sq, cn_var, cn_root, cn_norm, cn_z, cn_sig, conv_out = (
            sem(n) for n in ("cn_sum", "cn_cent", "cn_sq", "cn_var", "cn_root", "cn_norm", "cn_z", "cn_sig",
                             "conv_out"))
        kk_in, kk_sq, kk_ss, kk_norm, kk_ready = (sem(n) for n in ("kk_in", "kk_sq", "kk_ss", "kk_norm", "kk_ready"))
        act_in, lora_mm, lora_act, gate_mm, gate_out = (
            sem(n) for n in ("act_in", "lora_mm", "lora_act", "gate_mm", "gate_out"))
        cum_ready, exp_ready, mult_ready, prep_done, fac_in, fac_ready = (
            sem(n) for n in ("cum_ready", "exp_ready", "mult_ready", "prep_done", "fac_in", "fac_ready"))
        bonus_in, bonus_mm, bonus_out, vtok_mm, vtok_out = (
            sem(n) for n in ("bonus_in", "bonus_mm", "bonus_out", "vtok_mm", "vtok_out"))
        prod_mm, ring_free, prod_out = sem("prod_mm"), [sem("ring_free0"), sem("ring_free1")], sem("prod_out")
        at_ready, xf_ready, nw_mm, r_ready, z_mm, in_mm, inv_ready = (
            [sem(f"{n}{d}") for d in range(2)]
            for n in ("at_ready", "xf_ready", "nw_mm", "r_ready", "z_mm", "in_mm", "inv_ready"))
        lx_mm, t_ready, xn_mm, x_ready, yn_mm, y_ready = (
            [sem(f"{n}{d}") for d in range(2)] for n in ("lx_mm", "t_ready", "xn_mm", "x_ready", "yn_mm", "y_ready"))
        tok_mm, tok_out, w_mm, w_out_s, u_mm, u_out, y_mm, y_out, s_mm, s_sum, s_out = (
            sem(n) for n in ("tok_mm", "tok_out", "w_mm", "w_out_s", "u_mm", "u_out", "y_mm", "y_out", "s_mm",
                             "s_sum", "s_out"))
        gn_sum, gn_cent, gn_sq, gn_var, gn_std, gn_norm, gn_z, mix_high, mix_low, mix_in = (
            sem(n) for n in ("gn_sum", "gn_cent", "gn_sq", "gn_var", "gn_std", "gn_norm", "gn_z", "mix_high",
                             "mix_low", "mix_in"))
        stored = sem("stored")
        block = ctx.enter_context(nc.Block())

        turns = [(n, half) for n in range(NC) for half in range(2)]
        schedule = [("product", 0, p) for p in range(8)] + [("operand", 0, d) for d in range(2)]
        for i in range(len(turns) + 1):
            stages = [(what, i, m) for m in range(LEVELS) for what in ("ax", "xy")] + [("residual", i), ("second", i),
                                                                                      ("inverse", i)]
            fill = [("w", i - 1), ("u", i - 1), ("tokens", i - 1)] + [("y", i - 1, p) for p in range(4)] \
                if i else [("values", j) for j in range(JT)] + [("bonus", j) for j in range(JT - 1)]
            ahead = [("product", i + 1, p) for p in range(8)] if i + 1 < len(turns) else [("nothing",)] * 8
            fill += ahead[:2] + [("state", i - 1) if i else ("bonus", JT - 1)] + ahead[2:] + [("nothing",)]
            if i == len(turns) - 1:
                side = [[("conv_sum",)], [], [("conv_var",)], [], [("conv_root", 0), ("conv_root", 1)],
                        [("conv_root", 2), ("conv_root", 3)], []]
                side = [[f] + more for f, more in zip(fill, side)]
                side += [[("conv_norm", j), ("gate", j)] for j in range(JT)]
                side += [[("head_sum", 0), ("head_sum", 1)], [("head_var", 0)], [("head_var", 1), ("conv_swish",)],
                         [("head_root", 0), ("conv_high", 0)], [("conv_high", 1), ("head_root", 1)],
                         [("conv_high", 2), ("conv_high", 3)]]
                for before, stage in zip(side, stages):
                    schedule += before + [stage]
            elif i == len(turns):
                schedule += [("w", i - 1), ("head_gate", 0), ("conv_low",), ("u", i - 1), ("head_gate", 1),
                             ("mix_weights", 0)]
                schedule += fill[3:7] + [("mix_weights", 1)]
                schedule += [(what, j) for what in ("head_sum", "head_var") for j in (2, 3)]
                schedule += [("head_split", 0), ("head_split", 1), ("head_root", 2), ("mix_weights", 2),
                             ("head_gate", 2), ("head_split", 2), ("head_root", 3), ("mix_weights", 3),
                             ("head_gate", 3), ("head_split", 3)]
                schedule += [("mix_weights", k) for k in range(4, KT + 2)]
            else:
                for before, stage in zip(fill, stages):
                    schedule += [before, stage]
                    if stage == ("ax", i, LEVELS - 1):
                        schedule += [("operand", i + 1, 0)]
                    if stage[0] == "inverse":
                        schedule += [("operand", i + 1, 1)]

        ring_use, uses = {}, 0
        for what, *which in schedule:
            count = {"product": 1, "conv_sum": 1, "conv_var": 1, "gate": 1, "head_sum": 1, "head_var": 1}.get(what, 0)
            if what == "tokens" and turns[which[0]][0] < NC - 1:
                count = 2
            for k in range(count):
                ring_use[(what, *which, k)] = (uses % 2, uses // 2)
                uses += 1

        def power(w):
            return ch(tmp, (3, 0, 4, 8, 9, 5)[w])

        def tap_weight(j, k):
            return par[:, PAR["conv_dw"] + k * JT + j:PAR["conv_dw"] + k * JT + j + 1]

        def chunk(n, d):
            return n if d == 0 else NC - 1 - n

        def unit(half, d, u):
            return (half * 2 + d) * 4 + u

        def prod(half, d, u, what):
            c0 = unit(half, d, u) * 512 + {"qb": 0, "rb": 128, "qk": 256, "rk": 384}[what]
            return a_t[:, c0:c0 + 128]

        @block.sync
        def _(sp):
            for k in range(0, KT, 2):
                if k < 4:
                    sp.dma_start(raw[k // 2][:, :], weights[k // 2]).then_inc(raw_landed[k // 2], 16)
                sp.dma_start(ch(x32, k, 2), x_t[:, k * SEQ:(k + 2) * SEQ]).then_inc(x_loaded[k // 2], 16)
            sp.dma_start(par[:, :], params).then_inc(consts_loaded, 16)
            sp.dma_start(ident[:, :], ident_c).then_inc(consts_loaded, 16)
            sp.dma_start(head_ones[:, :], head_ones_c).then_inc(consts_loaded, 16)
            sp.dma_start(tri[:, :], tri_c).then_inc(consts_loaded, 16)
            sp.dma_start(level_f[:, :], level_c).then_inc(consts_loaded, 16)

            with sp.Fori(1, N_ITEMS // 2) as t:
                for s in range(2):
                    g = t * 2
                    sp.wait_ge(hi_ready, g + (s - 1))
                    sp.wait_ge(lo_ready, g + (s - 1))
                    sp.dma_start(raw[s][:, :], weights[bass.ds(g + s, 1), :, :].rearrange("a p n -> (a p) n"))\
                        .then_inc(raw_landed[s], 16)
            for k in range(KT):
                sp.wait_ge(ln_out, 2 * KT + k + 1)
                sp.dma_start(out_t[:, k * SEQ:(k + 1) * SEQ], ch(x32, k)).then_inc(stored, 16)
            sp.wait_ge(stored, 16 * KT)

        @block.gpsimd
        def _(pool):
            pool.memset(ones[:, :], 1.0).then_inc(ones_set, 1)
            pool.wait_ge(ln_out, KT)
            pool.dma_start(spill, x32[:, :]).then_inc(spilled, 16)
            pool.wait_ge(weights_used, 2 + PROJ_IN)
            for j in range(JT):
                pool.memset(u_t[:, j * ULEN:j * ULEN + PAD], 0.0).then_inc(pads_set, 1)
                pool.memset(u_t[:, (j + 1) * ULEN - PAD:(j + 1) * ULEN], 0.0).then_inc(pads_set, 1)
            pool.dma_start(lora_s[:, 0:1536], lora).then_inc(lora_loaded, 16)
            pool.dma_start(lora_s[0:32, 1536:2048], gate_tail).then_inc(lora_loaded, 16)
            pool.wait_ge(kk_ready, JT)
            for j in range(JT):
                for d in range(2):
                    a, kd = ch(tmp, 5 * d + 1), ch(tmp, 5 * d + 2)
                    pool.wait_ge(mult_ready, 2 * j + d + 1)
                    pool.tensor_tensor(kd, kd, ch(k_t, j), ALU.mult).then_inc(rated, 1)
                    pool.tensor_tensor(a, a, ch(kk_t, j), ALU.mult).then_inc(rated, 1)
            pool.wait_ge(prep_done, 2 * JT)
            pool.wait_ge(tile_done, 16 + JT)
            j = JT - 1
            for k in range(TAPS):
                window, weight = u_t[:, j * ULEN + k:j * ULEN + k + SEQ], tap_weight(j, k)
                if k:
                    pool.wait_ge(pool_taps, 2 * k - 1)
                out = ch(conv_t, j) if k == 0 else tapped[:, :]
                pool.tensor_scalar(out, window, weight, col("conv_b", j) if k == 0 else 0.0, ALU.mult, ALU.add)\
                    .then_inc(pool_taps, 1)
                if k:
                    pool.wait_ge(pool_taps, 2 * k)
                    pool.tensor_tensor(ch(conv_t, j), ch(conv_t, j), tapped[:, :], ALU.add).then_inc(pool_taps, 1)
            pool.wait_ge(y_mm, len(turns))
            pool.wait_ge(spilled, 16)
            pool.dma_start(x_back[:, :], spill).then_inc(reloaded, 16)
            pool.wait_ge(reloaded, 16)

        @block.tensor
        def _(pe):
            pe.sem_inc(weights_used, 2)
            pe.sem_inc(pairs_free, 2)
            for b in range(PROJ_BANKS):
                pe.sem_inc(proj_free[b], 1)

            def three(bank, s, k, high, low, start, stop):
                wh, wl = w_hi[s][:, k * P:(k + 1) * P], w_lo[s][:, k * P:(k + 1) * P]
                pe.matmul(bank[:, :], wh, high, start=start, stop=False)
                pe.matmul(bank[:, :], wh, low, start=False, stop=False)
                return pe.matmul(bank[:, :], wl, high, start=False, stop=stop)

            def up_pair(g, bank0, bank1, n_x):
                lag = 3
                for i in range(KT + lag):
                    if i in (0, lag):
                        pe.wait_ge(hi_ready, g + 1 + i // lag)
                        pe.wait_ge(lo_ready, g + 1 + i // lag)
                    for s, k, bank in ((0, i, bank0), (1, i - lag, bank1)):
                        if 0 <= k < KT:
                            if s == 0:
                                pe.wait_ge(x_low, KT * n_x + k + 1)
                            last = three(bank, s, k, ch(x_hi, k), ch(x_lo, k), k == 0, k == KT - 1)
                            if k == KT - 1:
                                last.then_inc(weights_used, 1)

            def up_tile(g, s, bank, n_x):
                pe.wait_ge(hi_ready, g + 1)
                pe.wait_ge(lo_ready, g + 1)
                for k in range(KT):
                    pe.wait_ge(x_low, KT * n_x + k + 1)
                    last = three(bank, s, k, ch(x_hi, k), ch(x_lo, k), k == 0, k == KT - 1)
                last.then_inc(weights_used, 1)

            def down_tile(g, s, f, high, low, first, last_one, order=range(KT), banks_read={}):
                pe.wait_ge(hi_ready, g + 1)
                pe.wait_ge(lo_ready, g + 1)
                for d in order:
                    if d in banks_read:
                        pe.wait_ge(*banks_read[d])
                    last = three(ps[d], s, d, high[:, bass.ds(f * SEQ, SEQ)], low[:, bass.ds(f * SEQ, SEQ)],
                                 first, last_one)
                    if last_one and d < KT - 1:
                        last.then_inc(sums_done, 1)
                last.then_inc(weights_used, 1)

            def swiglu(in0, out0, e):
                pe.wait_ge(pairs_free, FT * e + 1)
                up_pair(in0, ps[0], ps[1], 2 * e)
                pe.wait_ge(pairs_free, FT * e + 2)
                for part in range(2):
                    up_tile(in0 + 2 + part, part, ps[2 + part], 2 * e)
                with pe.Fori(1, FT // 2) as i:
                    for s in range(2):
                        pe.wait_ge(pairs_free, i * 2 + (s + 1 + FT * e))
                        for part in range(2):
                            up_tile(i * 4 + (in0 + 2 * s + part), part, ps[2 * s + part], 2 * e)
                pe.wait_ge(h_ready, FT * e + FT - 2)
                down_tile(out0, 0, 0, h_hi, h_lo, True, False, order=(4, 5, 6, 7, 0, 1, 2, 3),
                          banks_read={0: (h_ready, FT * (e + 1) - 1), 2: (h_ready, FT * (e + 1))})
                with pe.Fori(0, FT // 2 - 1) as i:
                    for s in (1, 0):
                        down_tile(i * 2 + (out0 + 2 - s), s, i * 2 + (2 - s), h_hi, h_lo, False, False)
                down_tile(out0 + FT - 1, 1, FT - 1, h_hi, h_lo, False, True)

            def layer_sums(n):
                for k in range(KT):
                    pe.wait_ge(ln_in, KT * n + k + 1)
                    last = pe.matmul(ps[0][:, :], ones[:, :], ch(y_ln, k), start=k == 0, stop=k == KT - 1)
                last.then_inc(ln_sum, 1)
                for k in range(KT):
                    pe.wait_ge(ln_squared, KT * n + k + 1)
                    last = pe.matmul(ps[1][:, :], ones[:, :], ch(sq_ln, k), start=k == 0, stop=k == KT - 1)
                last.then_inc(ln_var, 1)

            swiglu(FFN1_IN, FFN1_OUT, 0)
            pe.wait_ge(ones_set, 1)
            pe.wait_ge(consts_loaded, 80)
            layer_sums(0)

            def kk_sums(j):
                pe.wait_ge(kk_sq, j + 1)
                pe.matmul(ps[4 + j][:, :], head_ones[:, :], ch(tmp, j), start=True, stop=True).then_inc(kk_ss, 1)

            def lora(j):
                if j == 0:
                    pe.wait_ge(lora_loaded, 32)
                    pe.wait_ge(tile_done, 2)
                    pe.wait_ge(act_in, 1)
                for d in range(2):
                    for what in range(2):
                        rows = slice(64 * d, 64 * d + 64)
                        i = 4 * j + 2 * d + what
                        pe.wait_ge(kk_norm, i + 1) if j == 0 else pe.wait_ge(lora_act, i - 3)
                        pe.matmul(ps[4 + i % 4][:, :], lora_s[rows, 512 * what + j * P:512 * what + (j + 1) * P],
                                  wag_t[rows, what * SEQ:(what + 1) * SEQ], start=True, stop=True)\
                            .then_inc(lora_mm, 1)

            pe.wait_ge(proj_free[0], 1)
            pe.wait_ge(proj_free[1], 1)
            up_pair(PROJ_IN, ps[0], ps[1], 1)
            for q in range(2, len(PROJ)):
                b = q % PROJ_BANKS
                pe.wait_ge(proj_free[b], q // PROJ_BANKS + 1)
                up_tile(PROJ_IN + q, q % 2, ps[b], 1)
                if 0 <= q - FIRST_K - 2 < JT:
                    kk_sums(q - FIRST_K - 2)
                if q + 1 in RATES_AT:
                    lora(RATES_AT.index(q + 1))

            pe.wait_ge(diag_set, 2)
            for b in range(PROJ_BANKS):
                pe.wait_ge(proj_free[b], len(PROJ) // PROJ_BANKS + 1)

            def values(j):
                if j == 0:
                    pe.wait_ge(lora_act, 4 * 4)
                    pe.wait_ge(tile_done, 16)
                if j >= 2:
                    pe.wait_ge(vtok_out, j - 1)
                for c in range(NC):
                    last = pe.transpose(ps[6 + j % 2][:, c * P:(c + 1) * P],
                                        v_t[:, j * SEQ + c * CHUNK:j * SEQ + (c + 1) * CHUNK], ident[:, :])
                last.then_inc(vtok_mm, 1)

            def bonus(j):
                pe.wait_ge(vtok_out, j + 3) if j < 2 else pe.wait_ge(bonus_out, j - 1)
                pe.wait_ge(bonus_in, j + 1)
                pe.matmul(ps[6 + j % 2][:, :], head_ones[:, :], ch(k_t, j), start=True, stop=True)\
                    .then_inc(bonus_mm, 1)

            head_rows = [slice(0, 64), slice(64, 128)]

            def ring(*step, k=0):
                b, use = ring_use[(*step, k)]
                if use:
                    pe.wait_ge(ring_free[b], use)
                return ps[b]

            def product(i, p):
                n, half = turns[i]
                if i < 2 and p == 0:
                    pe.wait_ge(prep_done, JT * (i + 1))
                d, u = divmod(p, 4)
                j, rows, c = 2 * half + u // 2, head_rows[u % 2], chunk(n, d)
                bank = ring("product", i, p)
                c0 = ((d * JT + j) * NC + c) * 2 * CHUNK
                t0 = (d * JT + j) * SEQ + c * CHUNK
                q_and_r = qr[rows, c0:c0 + 2 * CHUNK]
                pe.matmul(bank[:, 0:256], b_m[rows, t0:t0 + CHUNK], q_and_r, start=True, stop=True)
                pe.matmul(bank[:, 256:512], k_m[rows, t0:t0 + CHUNK], q_and_r, start=True, stop=True)\
                    .then_inc(prod_mm, 1)

            def rows_of(t, d):
                return t[:, d * 4 * P:(d + 1) * 4 * P]

            def tile_of(t, d, u):
                return t[:, (4 * d + u) * P:(4 * d + u + 1) * P]

            eyes = ident_h[:, :].rearrange("p (a s) -> p a s", a=1).to_broadcast([P, 4, P])

            def ax_stage(i, m):
                for d in range(2):
                    px = ps[2 + d]
                    if m == 0:
                        pe.wait_ge(at_ready[d], i + 1)
                        if i:
                            pe.wait_ge(r_ready[d], i)
                    elif m >= 2:
                        pe.wait_ge(x_ready[d], i * (LEVELS - 1) + m - 1)
                    for u in range(4):
                        x_now = ident_h[:, :] if m == 0 else tile_of(tt_i if m == 1 else x_i, d, u)
                        last = pe.matmul(px[:, u * P:(u + 1) * P], tile_of(at_r, d, u), x_now, start=True, stop=True)
                    last.then_inc(lx_mm[d], 1)

            def xy_stage(i, m):
                for d in range(2):
                    pe.wait_ge(t_ready[d], i * LEVELS + m + 1)
                    px, py = ps[2 + d], ps[4 + d]
                    if m:
                        pe.wait_ge(y_ready[d], i * (LEVELS + 1) + m)
                    elif i:
                        pe.wait_ge(inv_ready[d], i)
                    y_now = [ident_h[:, :] if m == 0 else tile_of(y_i, d, u) for u in range(4)]
                    if m:
                        for u in range(4):
                            last = pe.matmul(px[:, u * P:(u + 1) * P], y_now[u], tile_of(tt_i, d, u),
                                             start=True, stop=True)
                        last.then_inc(xn_mm[d], 1)
                    for u in range(4):
                        last = pe.matmul(py[:, u * P:(u + 1) * P], tile_of(tt_i, d, u), y_now[u],
                                         start=True, stop=True)
                    last.then_inc(yn_mm[d], 1)

            def residual(i):
                n, half = turns[i]
                for d in range(2):
                    px = ps[2 + d]
                    pe.wait_ge(x_ready[d], (i + 1) * (LEVELS - 1))
                    pe.matmul(px[:, :].rearrange("p (u s) -> p u s", u=4), ident_h[:, :], eyes,
                              start=True, stop=True)
                    pe.matmul(px[:, :], minus_h[:, :], rows_of(x_i, d), start=False, stop=True, skip_group_check=True)
                    pe.wait_ge(xf_ready[d], i + 1)
                    for u in range(4):
                        last = pe.matmul(px[:, u * P:(u + 1) * P], prod(half, d, u, "qb"),
                                         tile_of(x_f, d, u), start=False, stop=True,
                                         skip_group_check=True)
                    last.then_inc(nw_mm[d], 1)

            def second(i):
                for d in range(2):
                    py = ps[4 + d]
                    pe.wait_ge(y_ready[d], (i + 1) * LEVELS + i)
                    pe.wait_ge(r_ready[d], i + 1)
                    pe.matmul(py[:, :], ident_h[:, :], rows_of(y_i, d), start=True, stop=True)
                    for u in range(4):
                        last = pe.matmul(py[:, u * P:(u + 1) * P], tile_of(r_i, d, u), tile_of(y_i, d, u),
                                         start=False, stop=True, skip_group_check=True)
                    last.then_inc(z_mm[d], 1)

            def inverse(i):
                for d in range(2):
                    py = ps[4 + d]
                    pe.wait_ge(y_ready[d], (i + 1) * (LEVELS + 1))
                    for u in range(4):
                        o = py[:, u * P:(u + 1) * P]
                        pe.matmul(o, tile_of(x_i, d, u), ident_h[:, :], start=True, stop=False)
                        last = pe.matmul(o, tile_of(r_i, d, u), tile_of(y_i, d, u), start=False, stop=True)
                    last.then_inc(in_mm[d], 1)

            def tokens(i):
                n, half = turns[i]
                if n == NC - 1:
                    return
                for k, t in enumerate((b_m, k_m)):
                    bank = ring("tokens", i, k=k)
                    for d in range(2):
                        for jj in range(2):
                            t0 = (d * JT + 2 * half + jj) * SEQ + chunk(n, d) * CHUNK
                            last = pe.transpose(bank[:, (2 * d + jj) * P:(2 * d + jj + 1) * P],
                                                t[:, t0:t0 + CHUNK], ident[:, :])
                    last.then_inc(tok_mm, 1)

            pairs = [(d, jj) for d in range(2) for jj in range(2)]

            def pair_at(d, jj):
                return slice((2 * d + jj) * P, (2 * d + jj + 1) * P)

            def state_of(half, d, jj):
                return state[:, (4 * half + 2 * d + jj) * P:(4 * half + 2 * d + jj + 1) * P]

            def qr_of(i, d, jj, w):
                n, half = turns[i]
                c0 = (((d * JT + 2 * half + jj) * NC + chunk(n, d)) * 2 + w) * CHUNK
                return qr[:, c0:c0 + CHUNK]

            def head_at(d, u):
                return slice((4 * d + u) * HEAD, (4 * d + u + 1) * HEAD)

            def v_of(i, d, u, n_heads=1):
                n, half = turns[i]
                c0 = chunk(n, d) * WIDTH + (4 * half + u) * HEAD
                return v_tok[:, c0:c0 + n_heads * HEAD]

            def run_w(i):
                n, half = turns[i]
                if i:
                    pe.wait_ge(u_out, i)
                else:
                    pe.wait_ge(vtok_out, JT)
                    pe.wait_ge(bonus_out, JT)
                if i >= 2 and n:
                    pe.wait_ge(s_out, 4 * (i - 1))
                for d, jj in pairs:
                    if n:
                        pe.matmul(ps[6][:, pair_at(d, jj)], qr_of(i, d, jj, 0), state_of(half, d, jj),
                                  start=True, stop=True)
                    for u in (2 * jj, 2 * jj + 1):
                        last = pe.matmul(ps[6][:, head_at(d, u)], prod(half, d, u, "qk"), v_of(i, d, u),
                                         start=n == 0, stop=True, skip_group_check=True)
                last.then_inc(w_mm, 1)

            def run_u(i):
                n, half = turns[i]
                pe.wait_ge(w_out_s, i + 1)
                for d in range(2):
                    pe.wait_ge(inv_ready[d], i + 1)
                for d in range(2):
                    for u in range(4):
                        c0 = unit(half, d, u) * P
                        last = pe.matmul(ps[6][:, head_at(d, u)], inv[:, c0:c0 + P], w_c[:, head_at(d, u)],
                                         start=True, stop=True)
                last.then_inc(u_mm, 1)

            def run_y(i, p):
                n, half = turns[i]
                if p == 0:
                    pe.wait_ge(u_out, i + 1)
                    if i:
                        pe.wait_ge(s_sum, i) if turns[i - 1][0] < NC - 1 else pe.wait_ge(y_out, 2 * i)
                d, jj = pairs[p]
                if n:
                    pe.matmul(ps[7][:, pair_at(d, jj)], state_of(half, d, jj), qr_of(i, d, jj, 1),
                              start=True, stop=True)
                for u in (2 * jj, 2 * jj + 1):
                    o = ps[7][head_rows[u % 2], pair_at(d, jj)]
                    pe.matmul(o, u_c[:, head_at(d, u)], prod(half, d, u, "rb"), start=n == 0, stop=False,
                              skip_group_check=True)
                    last = pe.matmul(o, v_of(i, d, u), prod(half, d, u, "rk"), start=False, stop=True,
                                     skip_group_check=True)
                if p == len(pairs) - 1:
                    last.then_inc(y_mm, 1)

            def run_state(i):
                n, half = turns[i]
                if n == NC - 1:
                    return
                pe.wait_ge(tok_out, 2 * (i + 1))
                pe.wait_ge(y_out, 2 * (i + 1))
                for d, jj in pairs:
                    o, t = ps[7][:, pair_at(d, jj)], pair_at(d, jj)
                    pe.matmul(o, b_tok[:, t], u_c[:, t], start=True, stop=False)
                    last = pe.matmul(o, k_tok[:, t], v_of(i, d, 2 * jj, 2), start=False, stop=True)
                last.then_inc(s_mm, 1)

            def conv_sum():
                bank = ring("conv_sum")
                for j in range(JT):
                    pe.wait_ge(conv_done, j + 1) if j < JT - 1 else pe.wait_ge(pool_taps, 2 * TAPS - 1)
                    last = pe.matmul(bank[:, :], ones[:, :], ch(conv_t, j), start=j == 0, stop=j == JT - 1)
                last.then_inc(cn_sum, 1)

            def conv_var():
                bank = ring("conv_var")
                for j in range(JT):
                    pe.wait_ge(cn_sq, j + 1)
                    last = pe.matmul(bank[:, :], ones[:, :], ch(cn_t, j), start=j == 0, stop=j == JT - 1)
                last.then_inc(cn_var, 1)

            def gate(j):
                bank = ring("gate", j)
                pe.matmul(bank[:, :], lora_s[:, 1024 + j * P:1024 + (j + 1) * P], ch(wag_t, 2), start=True, stop=False)
                pe.matmul(bank[:, :], lora_s[0:32, 1536 + j * P:1536 + (j + 1) * P], wag_t[0:32, 3 * SEQ:4 * SEQ],
                          start=False, stop=True).then_inc(gate_mm, 1)

            def head_sum(j):
                bank = ring("head_sum", j)
                pe.wait_ge(y_out, 2 * (len(turns) - 1 + j // 2))
                pe.matmul(bank[:, :], head_ones[:, :], ch(y_t, j), start=True, stop=True).then_inc(gn_sum, 1)

            def head_var(j):
                bank = ring("head_var", j)
                pe.wait_ge(gn_sq, j + 1)
                pe.matmul(bank[:, :], head_ones[:, :], ch(gn_sq_t, j), start=True, stop=True).then_inc(gn_var, 1)

            steps = {"values": values, "bonus": bonus, "product": product, "ax": ax_stage, "xy": xy_stage,
                     "residual": residual, "second": second, "inverse": inverse, "tokens": tokens, "w": run_w,
                     "u": run_u, "y": run_y, "state": run_state, "conv_sum": conv_sum, "conv_var": conv_var,
                     "gate": gate, "head_sum": head_sum, "head_var": head_var}
            for what, *which in schedule:
                if what in steps:
                    steps[what](*which)

            pe.wait_ge(inv_ready[0], len(turns))
            pe.wait_ge(inv_ready[1], len(turns))
            for i in range(KT):
                if i < JT:
                    pe.wait_ge(mix_low, i + 1)
                    down_tile(MIX_OUT + i, i % 2, i, x_hi[:, JT * SEQ:], conv_lo, i == 0, False,
                              order=(2, 3, 4, 5, 6, 7, 0, 1),
                              banks_read={b: (ring_free[b], (uses + 1 - b) // 2) for b in range(2)} if i == 0 else {})
                else:
                    pe.wait_ge(mix_low, i + 1)
                    down_tile(MIX_OUT + i, i % 2, i - JT, x_hi, x_lo, False, i == KT - 1)
            layer_sums(1)

            swiglu(FFN2_IN, FFN2_OUT, 1)
            layer_sums(2)

        @block.scalar
        def _(act):
            def high(g, s, turn):
                act.wait_ge(raw_landed[s], turn * 16 + 16)
                act.wait_ge(weights_used, g + 1)
                act.activation(w_hi[s][:, :], raw[s][:, :], ACT.Copy).then_inc(hi_ready, 1)

            def swiglu(in0, out0, e, last):
                high(in0 + 2, 0, in0 // 2 + 1)
                with act.Fori(0, FT // 2) as i:
                    for s in range(2):
                        g = i * 4 + (in0 + 2 * s)
                        act.wait_ge(weights_used, g + 3)
                        act.wait_ge(pairs_free, i * 2 + (s + 1 + FT * e))
                        act.activation(ch(sig, s), ps[2 * s][:, :], ACT.Sigmoid).then_inc(sig_ready, 1)
                        high(g + 3, 1, i * 2 + (in0 // 2 + s + 1))
                        high(g + 4, 0, i * 2 + (in0 // 2 + s + 2))
                with act.Fori(0, FT // 2 - last - 1) as i:
                    high(i * 2 + (out0 + 3), 1, i + (out0 // 2 + 1))
                    high(i * 2 + (out0 + 4), 0, i + (out0 // 2 + 2))
                high(out0 + 1 + 2 * (FT // 2 - last), 1, out0 // 2 + FT // 2 - last)

            def norm(n):
                for k in range(KT):
                    act.wait_ge(ln_centered, KT * n + k + 1)
                    act.activation(ch(sq_ln, k), ch(y_ln, k), ACT.Square).then_inc(ln_squared, 1)
                act.wait_ge(ln_var, n + 1)
                act.activation(std[:, :], ps[1][:, :], ACT.Sqrt, scale=1.0 / D_MODEL, bias=eps[n][:, :])\
                    .then_inc(ln_std, 1)
                for k in range(KT):
                    act.wait_ge(ln_norm, KT * n + k + 1)
                    gain = dict(scale=col(f"ln{n + 1}_g", k), bias=col(f"ln{n + 1}_b", k))
                    act.activation(ch(x32, k), ch(y_ln, k), ACT.Identity, **gain).then_inc(ln_out, 1)
                    if n < 2:
                        act.activation(ch(x_hi, k), ch(y_ln, k), ACT.Identity, **gain).then_inc(x_high, 1)

            for k in range(KT):
                if k in (0, 2):
                    high(k // 2, k // 2, 0)
                act.wait_ge(x_loaded[k // 2], 16)
                act.activation(ch(x_hi, k), ch(x32, k), ACT.Copy).then_inc(x_high, 1)
            act.wait_ge(consts_loaded, 80)
            act.wait_ge(eps_set, 4)
            swiglu(FFN1_IN, FFN1_OUT, 0, 0)
            norm(0)

            def decay_tanh():
                act.wait_ge(tile_done, 1)
                act.activation(ch(wag_t, 0), ch(wag_t, 0), ACT.Tanh).then_inc(act_in, 1)

            def kk_square(j):
                act.wait_ge(kk_in, j + 1)
                act.activation(ch(tmp, j), ch(kk_t, j), ACT.Square).then_inc(kk_sq, 1)

            def kk_root(j):
                act.wait_ge(kk_ss, j + 1)
                act.activation(ch(tmp, j), ps[4 + j][:, :], ACT.Sqrt).then_inc(kk_norm, 1)

            def rates(j):
                if j:
                    act.wait_ge(prep_done, 2 * j)
                else:
                    act.wait_ge(kk_ready, JT)
                    act.wait_ge(tile_done, 2 + JT + 2)
                    act.activation(ch(wag_t, 2, 2), ch(wag_t, 2, 2), ACT.Sigmoid).then_inc(act_in, 1)
                for d in range(2):
                    act.wait_ge(lora_mm, 4 * j + 2 * d + 1)
                    act.activation(ch(tmp, 5 * d), ps[4 + 2 * d][:, :], ACT.Sigmoid, bias=col("w0", d * JT + j))\
                        .then_inc(lora_act, 1)
                    act.wait_ge(lora_mm, 4 * j + 2 * d + 2)
                    act.activation(ch(tmp, 5 * d + 1), ps[5 + 2 * d][:, :], ACT.Sigmoid, bias=col("a0", d * JT + j))\
                        .then_inc(lora_act, 1)
                    act.wait_ge(lora_act, 4 * j + 2 * d + 2)
                    act.activation(ch(tmp, 5 * d + 2), ch(tmp, 5 * d + 1), ACT.Identity, scale=col("k_a", j),
                                   bias=own[:, 16 + j:17 + j]).then_inc(mult_ready, 1)

            def decays(j, d):
                act.wait_ge(cum_ready, 2 * j + d + 1)
                past, before = ch(tmp, 5 * d + 4), ch(tmp, 5 * d)
                sources = ((past, 1), (before, -1), (past, -1)) if d == 0 else ((before, -1), (past, 1), (before, 1))
                for w, (src, sign) in enumerate(sources):
                    act.activation(power(3 * d + w), src, ACT.Exp, scale=sign * KAPPA).then_inc(exp_ready, 1)

            between = {}
            for j, q in enumerate(RATES_AT):
                for at_q, part in ((q, (rates, j)), (q + 1, (decays, j, 0)), (q + 2, (decays, j, 1))):
                    between.setdefault(at_q, []).append(part)
            act.wait_ge(own_set, 2)
            parts = 0
            for q, (what, j) in enumerate(PROJ):
                g = PROJ_IN + q
                high(g + 2, q % 2, (g + 2) // 2) if g + 2 < MIX_OUT else None
                act.wait_ge(weights_used, g + 3)
                bank = ps[q % PROJ_BANKS]
                if what == "conv_gate":
                    act.activation(u_t[:, j * ULEN + PAD:j * ULEN + PAD + SEQ], bank[:, :], ACT.Sigmoid)\
                        .then_inc(proj_free[q % PROJ_BANKS], 1)
                elif what != "conv_value":
                    if what == "k" and j == 0:
                        act.wait_ge(spilled, 16)
                    dst = {"wd": (wag_t, 0), "ad": (wag_t, 1), "gd": (wag_t, 2 + j), "k": (k_t, j), "r": (r_t, j),
                           "v": (v_t, j)}[what]
                    m = MU[what, j]
                    act.activation(ch(*dst), bank[:, :], ACT.Identity, scale=own[:, m:m + 1]).then_inc(proj_part, 1)
                if q == 1:
                    decay_tanh()
                if 0 <= q - FIRST_K - 1 < JT:
                    kk_square(q - FIRST_K - 1)
                if 0 <= q - FIRST_K - 2 < JT:
                    kk_root(q - FIRST_K - 2)
                for part, *which in between.get(q, []):
                    part(*which)
            act.wait_ge(fac_in, 2 * JT)
            act.activation(fac[:, :], fac[:, :], ACT.Exp, scale=-KAPPA).then_inc(fac_ready, 1)
            def values(j):
                if j == 0:
                    act.wait_ge(prep_done, 2 * JT)
                act.wait_ge(vtok_mm, j + 1)
                act.activation(v_tok[:, :].rearrange("p (c w) -> p c w", c=NC)[:, :, j * P:(j + 1) * P],
                               ps[6 + j % 2][:, :].rearrange("p (c w) -> p c w", c=NC), ACT.Copy).then_inc(vtok_out, 1)

            def xy_stage(i, m):
                def x_out(d):
                    act.wait_ge(xn_mm[d], i * (LEVELS - 1) + m)
                    act.activation(x_i[:, d * 512:(d + 1) * 512], ps[2 + d][:, :], ACT.Copy).then_inc(x_ready[d], 1)

                def y_part(d):
                    act.wait_ge(yn_mm[d], i * LEVELS + m + 1)
                    act.activation(y_i[:, d * 512:(d + 1) * 512], ps[4 + d][:, :], ACT.Copy).then_inc(y_ready[d], 1)

                if m == LEVELS - 1:
                    for d in range(2):
                        x_out(d)
                        act.wait_ge(x_ready[d], (i + 1) * (LEVELS - 1))
                        act.activation(x_f[:, d * 512:(d + 1) * 512], x_i[:, d * 512:(d + 1) * 512], ACT.Copy)\
                            .then_inc(xf_ready[d], 1)
                    for d in range(2):
                        y_part(d)
                else:
                    for d in range(2):
                        if m:
                            x_out(d)
                        y_part(d)

            def residual(i):
                for d in range(2):
                    act.wait_ge(nw_mm[d], i + 1)
                    act.activation(r_i[:, d * 512:(d + 1) * 512], ps[2 + d][:, :], ACT.Copy).then_inc(r_ready[d], 1)

            def second(i):
                for d in range(2):
                    act.wait_ge(z_mm[d], i + 1)
                    act.activation(y_i[:, d * 512:(d + 1) * 512], ps[4 + d][:, :], ACT.Copy).then_inc(y_ready[d], 1)

            def inverse(i):
                n, half = turns[i]
                for d in range(2):
                    act.wait_ge(in_mm[d], i + 1)
                    c0 = unit(half, d, 0) * P
                    act.activation(inv[:, c0:c0 + 4 * P], ps[4 + d][:, :], ACT.Copy).then_inc(inv_ready[d], 1)

            def tokens(i):
                if turns[i][0] == NC - 1:
                    return
                for t, dst in enumerate((b_tok, k_tok)):
                    act.wait_ge(tok_mm, 2 * i + t + 1)
                    if i:
                        act.wait_ge(s_mm, i)
                    b = ring_use[("tokens", i, t)][0]
                    act.activation(dst[:, :], ps[b][:, :], ACT.Copy).then_inc(tok_out, 1)
                    act.wait_ge(tok_out, 2 * i + t + 1)
                    act.sem_inc(ring_free[b], 1)

            def run_w(i):
                act.wait_ge(w_mm, i + 1)
                act.activation(w_c[:, :], ps[6][:, :], ACT.Copy).then_inc(w_out_s, 1)

            def run_u(i):
                act.wait_ge(u_mm, i + 1)
                act.activation(u_c[:, :], ps[6][:, :], ACT.Copy).then_inc(u_out, 1)

            def conv_sum():
                for j in range(JT):
                    act.wait_ge(cn_cent, j + 1)
                    act.activation(ch(cn_t, j), ch(conv_t, j), ACT.Square).then_inc(cn_sq, 1)

            def conv_var():
                b = ring_use[("conv_var", 0)][0]
                act.wait_ge(cn_var, 1)
                act.activation(ch(cn_std, 0), ps[b][:, :], ACT.Sqrt, scale=1.0 / WIDTH, bias=eps[1][:, :])\
                    .then_inc(cn_root, 1)
                act.wait_ge(cn_root, 1)
                act.sem_inc(ring_free[b], 1)

            def conv_norm(j):
                act.wait_ge(cn_norm, j + 1)
                act.activation(ch(conv_t, j), ch(conv_t, j), ACT.Identity, scale=col("conv_ln_g", j),
                               bias=col("conv_ln_b", j)).then_inc(cn_z, 1)
                act.wait_ge(cn_z, j + 1)
                act.activation(ch(cn_t, j), ch(conv_t, j), ACT.Sigmoid).then_inc(cn_sig, 1)

            def conv_high(j):
                act.wait_ge(conv_out, j + 1)
                act.activation(ch(x_hi, JT + j), ch(conv_t, j), ACT.Copy).then_inc(mix_high, 1)

            def mix_weights(k):
                high(MIX_OUT + k, k % 2, (MIX_OUT + k) // 2)

            def head_gate(j):
                act.wait_ge(gn_norm, j + 1)
                act.activation(ch(y_t, j), ch(y_t, j), ACT.Identity, scale=col("lnx_g", j), bias=col("lnx_b", j))\
                    .then_inc(gn_z, 1)

            def head_split(j):
                act.wait_ge(mix_in, j + 1)
                act.activation(ch(x_hi, j), ch(y_t, j), ACT.Copy).then_inc(mix_high, 1)

            def gate(j):
                b = ring_use[("gate", j, 0)][0]
                if j == 0:
                    act.wait_ge(cn_sum, 1)
                act.wait_ge(gate_mm, j + 1)
                act.activation(ch(gate_t, j), ps[b][:, :], ACT.Copy).then_inc(gate_out, 1)
                act.wait_ge(gate_out, j + 1)
                act.sem_inc(ring_free[b], 1)

            def head_sum(j):
                act.wait_ge(gn_cent, j + 1)
                act.activation(ch(gn_sq_t, j), ch(y_t, j), ACT.Square).then_inc(gn_sq, 1)

            def head_var(j):
                b = ring_use[("head_var", j, 0)][0]
                act.wait_ge(gn_var, j + 1)
                act.activation(ch(gn_std_t, j), ps[b][:, :], ACT.Sqrt, scale=1.0 / HEAD, bias=eps[3][:, :])\
                    .then_inc(gn_std, 1)
                act.wait_ge(gn_std, j + 1)
                act.sem_inc(ring_free[b], 1)

            steps = {"values": values, "xy": xy_stage, "residual": residual, "second": second, "inverse": inverse,
                     "tokens": tokens, "w": run_w, "u": run_u, "conv_sum": conv_sum, "conv_var": conv_var,
                     "conv_norm": conv_norm, "conv_high": conv_high, "gate": gate, "head_sum": head_sum,
                     "head_var": head_var, "head_gate": head_gate, "head_split": head_split,
                     "mix_weights": mix_weights}
            for what, *which in schedule:
                if what in steps:
                    steps[what](*which)

            norm(1)
            swiglu(FFN2_IN, FFN2_OUT, 1, 1)
            norm(2)

        @block.vector
        def _(dve):
            own_steps = [0]

            def step(ins):
                own_steps[0] += 1
                ins.then_inc(vec, 1)
                dve.wait_ge(vec, own_steps[0])

            def low(g, s):
                dve.wait_ge(hi_ready, g + 1)
                dve.tensor_tensor(w_lo[s][:, :], raw[s][:, :], w_hi[s][:, :].bitcast(F32), ALU.subtract)\
                    .then_inc(lo_ready, 1)

            def swiglu(in0, out0, e, last):
                with dve.Fori(0, FT // 2) as i:
                    for s in range(2):
                        g = i * 4 + (in0 + 2 * s)
                        pair = i * 2 + (s + FT * e)
                        low(g + 2, 0)
                        dve.wait_ge(sig_ready, pair + 1)
                        dve.tensor_tensor(ch(h_raw, s), ps[2 * s][:, :], ch(sig, s), ALU.mult).then_inc(gated, 1)
                        low(g + 3, 1)
                        dve.wait_ge(weights_used, g + 4)
                        dve.wait_ge(gated, pair + 1)
                        dve.tensor_tensor(ch(h_raw, s), ps[2 * s + 1][:, :], ch(h_raw, s), ALU.mult)\
                            .then_inc(pairs_free, 1)
                        dve.wait_ge(pairs_free, pair + 3)
                        f = bass.ds(i * (2 * SEQ) + s * SEQ, SEQ)
                        dve.tensor_copy(h_hi[:, f], ch(h_raw, s)).then_inc(h_high, 1)
                        dve.wait_ge(h_high, pair + 1)
                        dve.tensor_tensor(h_lo[:, f], ch(h_raw, s), h_hi[:, f].bitcast(F32), ALU.subtract)\
                            .then_inc(h_ready, 1)
                with dve.Fori(0, FT // 2 - 1) as i:
                    for s in range(2):
                        low(i * 2 + (out0 + 2 + s), s)
                if not last:
                    low(out0 + FT, 0)

            def norm(n, items_done, x, residual):
                for k in range(KT):
                    dve.wait_ge(sums_done, (KT - 1) * n + k + 1) if k < KT - 1 else \
                        dve.wait_ge(weights_used, 2 + items_done)
                    dve.scalar_tensor_tensor(ch(y_ln, k), ch(x, k), residual, ps[k][:, :], ALU.mult, ALU.add)\
                        .then_inc(ln_in, 1)
                if n < 2:
                    low(items_done + 1, 1)
                dve.wait_ge(ln_sum, n + 1)
                for k in range(KT):
                    dve.scalar_tensor_tensor(ch(y_ln, k), ps[0][:, :], -1.0 / D_MODEL, ch(y_ln, k), ALU.mult, ALU.add)\
                        .then_inc(ln_centered, 1)
                dve.wait_ge(ln_std, n + 1)
                dve.reciprocal(rstd[:, :], std[:, :]).then_inc(ln_rstd, 1)
                dve.wait_ge(ln_rstd, n + 1)
                for k in range(KT + 2):
                    if k < KT:
                        dve.tensor_tensor(ch(y_ln, k), ch(y_ln, k), rstd[:, :], ALU.mult).then_inc(ln_norm, 1)
                    if n < 2 and k >= 2:
                        dve.wait_ge(x_high, KT * (n + 1) + k - 1)
                        dve.tensor_tensor(ch(x_lo, k - 2), ch(x32, k - 2), ch(x_hi, k - 2).bitcast(F32), ALU.subtract)\
                            .then_inc(x_low, 1)

            for n, value in enumerate((4 * LN_EPS, LN_EPS, 4 * LN_EPS, GN_EPS)):
                dve.memset(eps[n][:, :], value).then_inc(eps_set, 1)
            step(dve.memset(h_reset[:, :], 1.0))
            step(dve.memset(h_reset[:, :].rearrange("p (c t) -> p c t", c=NC)[:, :, 0:1], 0.0))
            for k in range(KT):
                if k in (0, 2):
                    low(k // 2, k // 2)
                dve.wait_ge(x_high, k + 1)
                dve.tensor_tensor(ch(x_lo, k), ch(x32, k), ch(x_hi, k).bitcast(F32), ALU.subtract).then_inc(x_low, 1)
            dve.wait_ge(consts_loaded, 80)
            step(dve.tensor_copy(level[:, :], level_f[:, :]))
            dve.tensor_copy(ident_h[:, :], ident[:, :]).then_inc(diag_set, 1)
            dve.tensor_scalar(minus_h[:, :], ident[:, :], -1.0, None, ALU.mult).then_inc(diag_set, 1)
            p0, n0 = PAR["mu_prev"], PAR["mu_next"]
            step(dve.tensor_tensor(own[:, 0:16], par[:, p0:p0 + 16], par[:, n0:n0 + 16], ALU.add))
            dve.tensor_scalar(own[:, 0:16], own[:, 0:16], -1.0, 1.0, ALU.mult, ALU.add).then_inc(own_set, 1)
            dve.tensor_scalar(own[:, 16:16 + JT], par[:, PAR["k_a"]:PAR["k_a"] + JT], -1.0, 1.0, ALU.mult, ALU.add)\
                .then_inc(own_set, 1)

            swiglu(FFN1_IN, FFN1_OUT, 0, 0)
            norm(0, PROJ_IN, x32, 2 * ALPHA)

            taps = [(j, k) for j in range(JT - 1) for k in range(TAPS)]

            def tap(j, k):
                window = u_t[:, j * ULEN + k:j * ULEN + k + SEQ]
                weight = tap_weight(j, k)
                if k == 0:
                    step(dve.tensor_scalar(ch(conv_t, j), window, weight, col("conv_b", j), ALU.mult, ALU.add))
                elif k < TAPS - 1:
                    step(dve.scalar_tensor_tensor(ch(conv_t, j), window, weight, ch(conv_t, j), ALU.mult, ALU.add))
                else:
                    dve.scalar_tensor_tensor(ch(conv_t, j), window, weight, ch(conv_t, j), ALU.mult, ALU.add)\
                        .then_inc(conv_done, 1)

            def kk_normalized(j):
                dve.wait_ge(kk_norm, j + 1)
                step(dve.tensor_scalar(ch(tmp, j), ch(tmp, j), NORM_EPS, None, ALU.max))
                step(dve.reciprocal(ch(tmp, j), ch(tmp, j)))
                dve.tensor_tensor(ch(kk_t, j), ch(kk_t, j), ch(tmp, j), ALU.mult).then_inc(kk_ready, 1)

            def sums(j, directions):
                for d in directions:
                    if j == 0 and d == 0:
                        dve.wait_ge(kk_ready, JT)
                    rate, cum, past = (ch(tmp, 5 * d + i) for i in (0, 3, 4))
                    c_view = cum.rearrange("p (c t) -> p c t", c=NC)
                    p_view = past.rearrange("p (c t) -> p c t", c=NC)
                    dve.wait_ge(mult_ready, 2 * j + d + 1)
                    step(dve.tensor_tensor_scan(cum, h_reset[:, :], rate, 0.0, ALU.mult, ALU.add))
                    step(dve.tensor_tensor(p_view, c_view, c_view[:, :, MID:MID + 1].to_broadcast([P, NC, CHUNK]),
                                           ALU.subtract))
                    f0 = (d * JT + j) * (NC - 1)
                    dve.tensor_tensor(fac[:, f0:f0 + NC - 1].rearrange("p (c a) -> p c a", a=1),
                                      p_view[:, 0:NC - 1, CHUNK - 1:CHUNK], c_view[:, 1:NC, MID:MID + 1],
                                      ALU.add).then_inc(fac_in, 1)
                    dve.tensor_tensor(rate, past, rate, ALU.subtract).then_inc(cum_ready, 1)

            def operands(j, directions):
                for d in directions:
                    a, kd = ch(tmp, 5 * d + 1), ch(tmp, 5 * d + 2)
                    slot = (d * JT + j) * SEQ
                    q_view = qr[:, 2 * slot:2 * slot + 2 * SEQ].rearrange("p (c w t) -> p c w t", c=NC, w=2)
                    i, w = 6 * j + 3 * d, 3 * d
                    dve.wait_ge(rated, 2 * (2 * j + d + 1))
                    dve.wait_ge(exp_ready, i + 1)
                    dve.tensor_tensor(b_m[:, slot:slot + SEQ], a, power(w), ALU.mult)
                    dve.tensor_tensor(k_m[:, slot:slot + SEQ], kd, power(w), ALU.mult)
                    dve.wait_ge(exp_ready, i + 2)
                    dve.scalar_tensor_tensor(q_view[:, :, 0, :], ch(kk_t, j).rearrange("p (c t) -> p c t", c=NC), -1.0,
                                             power(w + 1).rearrange("p (c t) -> p c t", c=NC), ALU.mult, ALU.mult)
                    dve.wait_ge(exp_ready, i + 3)
                    step(dve.tensor_tensor(q_view[:, :, 1, :], ch(r_t, j).rearrange("p (c t) -> p c t", c=NC),
                                           power(w + 2).rearrange("p (c t) -> p c t", c=NC), ALU.mult))
                    if d:
                        step(dve.tensor_tensor(ch(k_t, j), ch(tmp, 2), kd, ALU.add))
                        dve.scalar_tensor_tensor(ch(k_t, j), ch(k_t, j), col("r_k", j), ch(r_t, j),
                                                 ALU.mult, ALU.mult).then_inc(bonus_in, 1)
                        dve.wait_ge(bonus_in, j + 1)
                    dve.sem_inc(prep_done, 1)

            between = {FIRST_K + 3 + j: [(kk_normalized, j)] for j in range(JT)}
            for j, q in enumerate(RATES_AT):
                for at_q, part in ((q, (sums, j, (0,))), (q + 1, (sums, j, (1,))), (q + 2, (operands, j, (0,))),
                                   (LAST_PART_AT[j], (operands, j, (1,)))):
                    between.setdefault(at_q, []).append(part)
            parts = 0
            dve.wait_ge(pads_set, 2 * JT)
            for q, (what, j) in enumerate(PROJ):
                g = PROJ_IN + q
                low(g + 2, q % 2) if g + 2 < MIX_OUT else None
                bank, free = ps[q % PROJ_BANKS], proj_free[q % PROJ_BANKS]
                if what == "conv_value":
                    dve.wait_ge(weights_used, g + 3)
                    dve.wait_ge(proj_free[(q - 1) % PROJ_BANKS], 2 + q // PROJ_BANKS)
                    u = u_t[:, j * ULEN + PAD:j * ULEN + PAD + SEQ]
                    step(dve.tensor_tensor(u, bank[:, :], u, ALU.mult))
                    dve.sem_inc(free, 1)
                    dve.sem_inc(tile_done, 1)
                elif what != "conv_gate":
                    parts += 1
                    dst, i = {"wd": (wag_t, 0), "ad": (wag_t, 1), "gd": (wag_t, 2 + j), "k": (k_t, j), "r": (r_t, j),
                              "v": (v_t, j)}[what]
                    m, c0 = MU[what, j], i * SEQ
                    dve.wait_ge(proj_part, parts)
                    later, earlier = dst[:, c0 + 1:c0 + SEQ], dst[:, c0:c0 + SEQ - 1]
                    step(dve.scalar_tensor_tensor(later, bank[:, 0:SEQ - 1], col("mu_prev", m), later,
                                                  ALU.mult, ALU.add))
                    step(dve.scalar_tensor_tensor(earlier, bank[:, 1:SEQ], col("mu_next", m), earlier,
                                                  ALU.mult, ALU.add))
                    dve.sem_inc(free, 1)
                    dve.sem_inc(tile_done, 1)
                    if what == "k":
                        dve.tensor_scalar(ch(kk_t, j), ch(k_t, j), col("k_k", j), None, ALU.mult).then_inc(kk_in, 1)
                for part, *which in between.get(q, []):
                    part(*which)

            def bonus(j):
                dve.wait_ge(bonus_mm, j + 1)
                dve.tensor_tensor(ch(v_t, j), ps[6 + j % 2][:, :], ch(v_t, j), ALU.mult).then_inc(bonus_out, 1)

            def product(i, p):
                n, half = turns[i]
                d, u = divmod(p, 4)
                b = ring_use[("product", i, p, 0)][0]
                dve.wait_ge(prod_mm, 8 * i + p + 1)
                if i >= 2 and p == 0:
                    dve.wait_ge(y_mm, i - 1)
                c0 = unit(half, d, u) * 512
                dve.tensor_tensor(a_t[:, c0:c0 + 512], ps[b][:, :], tri[:, d * 512:(d + 1) * 512], ALU.mult)\
                    .then_inc(prod_out, 1)
                dve.wait_ge(prod_out, 8 * i + p + 1)
                dve.sem_inc(ring_free[b], 1)

            def operand(i, d):
                half = turns[i][1]
                c0 = unit(half, d, 0) * 512
                dve.tensor_tensor(at_r[:, d * 512:(d + 1) * 512].rearrange("p (u s) -> p u s", u=4),
                                  a_t[:, c0:c0 + 4 * 512].rearrange("p (u w) -> p u w", u=4)[:, :, 0:P],
                                  ident[:, :].rearrange("p (a s) -> p a s", a=1).to_broadcast([P, 4, P]),
                                  ALU.add).then_inc(at_ready[d], 1)

            def some_taps(count):
                for _ in range(count):
                    if taps:
                        tap(*taps.pop(0))

            def ax_stage(i, m):
                for d in range(2):
                    dve.wait_ge(lx_mm[d], i * LEVELS + m + 1)
                    l0 = (d * LEVELS + m) * P
                    dve.tensor_tensor(tt_i[:, d * 512:(d + 1) * 512].rearrange("p (u s) -> p u s", u=4),
                                      ps[2 + d][:, :].rearrange("p (u s) -> p u s", u=4),
                                      level[:, l0:l0 + P].rearrange("p (a s) -> p a s", a=1).to_broadcast([P, 4, P]),
                                      ALU.mult).then_inc(t_ready[d], 1)

            def xy_stage(i, m):
                some_taps((2, 2, 2, 1, 0, 0, 1)[m])

            def residual(i):
                some_taps(2)

            def second(i):
                some_taps(2)

            def inverse(i):
                some_taps(2)

            def run_y(i, p):
                n, half = turns[i]
                if p < 3:
                    return
                dve.wait_ge(y_mm, i + 1)
                for d in range(2):
                    dst = y_t[:, 2 * half * SEQ:(2 * half + 2) * SEQ].rearrange("p (j c t) -> p j c t", j=2, c=NC)[
                        :, :, chunk(n, d), :]
                    src = ps[7][:, 2 * d * CHUNK:(2 * d + 2) * CHUNK].rearrange("p (j t) -> p j t", j=2)
                    if n < NC // 2:
                        dve.tensor_copy(dst, src).then_inc(y_out, 1)
                    else:
                        dve.tensor_tensor(dst, src, dst, ALU.add).then_inc(y_out, 1)

            def run_state(i):
                n, half = turns[i]
                if n == NC - 1:
                    return
                if i == 0:
                    dve.wait_ge(fac_ready, 1)
                dve.wait_ge(s_mm, i + 1)
                now = state[:, half * 4 * P:(half + 1) * 4 * P]
                if n:
                    dve.tensor_tensor(s_new[:, :], ps[7][:, :], now, ALU.add).then_inc(s_sum, 1)
                else:
                    dve.tensor_copy(s_new[:, :], ps[7][:, :]).then_inc(s_sum, 1)
                dve.wait_ge(s_sum, i + 1)
                for d in range(2):
                    for jj in range(2):
                        f = (d * JT + 2 * half + jj) * (NC - 1) + (n if d == 0 else NC - 2 - n)
                        c0 = (2 * d + jj) * P
                        dve.scalar_tensor_tensor(now[:, c0:c0 + P], s_new[:, c0:c0 + P], fac[:, f:f + 1],
                                                 head_ones[:, :], ALU.mult, ALU.mult).then_inc(s_out, 1)

            def conv_sum():
                b = ring_use[("conv_sum", 0)][0]
                dve.wait_ge(cn_sum, 1)
                for j in range(JT):
                    dve.scalar_tensor_tensor(ch(conv_t, j), ps[b][:, :], -1.0 / WIDTH, ch(conv_t, j),
                                             ALU.mult, ALU.add).then_inc(cn_cent, 1)
                dve.wait_ge(cn_cent, JT)
                dve.sem_inc(ring_free[b], 1)

            def conv_root(p):
                if p == 0:
                    dve.wait_ge(cn_root, 1)
                part = slice(p * P, (p + 1) * P)
                step(dve.reciprocal(ch(cn_std, 1)[:, part], ch(cn_std, 0)[:, part]))

            def conv_norm(j):
                dve.tensor_tensor(ch(conv_t, j), ch(conv_t, j), ch(cn_std, 1), ALU.mult).then_inc(cn_norm, 1)

            def conv_swish():
                for j in range(JT):
                    dve.wait_ge(cn_sig, j + 1)
                    dve.tensor_tensor(ch(conv_t, j), ch(conv_t, j), ch(cn_t, j), ALU.mult).then_inc(conv_out, 1)

            def conv_low():
                for j in range(JT):
                    dve.wait_ge(mix_high, j + 1)
                    dve.tensor_tensor(ch(conv_lo, j), ch(conv_t, j), ch(x_hi, JT + j).bitcast(F32), ALU.subtract)\
                        .then_inc(mix_low, 1)

            def mix_weights(k):
                if k <= KT:
                    low(MIX_OUT + k, k % 2)

            def head_sum(j):
                b = ring_use[("head_sum", j, 0)][0]
                dve.wait_ge(gn_sum, j + 1)
                dve.scalar_tensor_tensor(ch(y_t, j), ps[b][:, :], -1.0 / HEAD, ch(y_t, j), ALU.mult, ALU.add)\
                    .then_inc(gn_cent, 1)
                dve.wait_ge(gn_cent, j + 1)
                dve.sem_inc(ring_free[b], 1)

            def head_root(j):
                dve.wait_ge(gn_std, j + 1)
                step(dve.reciprocal(ch(gn_std_t, j), ch(gn_std_t, j)))
                dve.tensor_tensor(ch(y_t, j), ch(y_t, j), ch(gn_std_t, j), ALU.mult).then_inc(gn_norm, 1)

            def head_gate(j):
                dve.wait_ge(gn_z, j + 1)
                step(dve.tensor_tensor(ch(y_t, j), ch(y_t, j), ch(v_t, j), ALU.add))
                dve.tensor_tensor(ch(y_t, j), ch(y_t, j), ch(gate_t, j), ALU.mult).then_inc(mix_in, 1)

            def head_split(j):
                dve.wait_ge(mix_high, JT + j + 1)
                dve.tensor_tensor(ch(x_lo, j), ch(y_t, j), ch(x_hi, j).bitcast(F32), ALU.subtract)\
                    .then_inc(mix_low, 1)

            steps = {"bonus": bonus, "product": product, "operand": operand, "ax": ax_stage, "xy": xy_stage,
                     "residual": residual, "second": second, "inverse": inverse, "y": run_y, "state": run_state,
                     "conv_sum": conv_sum, "conv_root": conv_root, "conv_norm": conv_norm, "conv_swish": conv_swish,
                     "conv_low": conv_low, "head_sum": head_sum, "head_root": head_root, "head_gate": head_gate,
                     "head_split": head_split, "mix_weights": mix_weights}
            for what, *which in schedule:
                if what in steps:
                    steps[what](*which)

            dve.wait_ge(reloaded, 16)
            norm(1, FFN2_IN, x_back, ALPHA)
            swiglu(FFN2_IN, FFN2_OUT, 1, 1)
            norm(2, N_ITEMS, x32, 2 * ALPHA)


def kernel(**inputs):
    import numpy as np
    import concourse.bacc as bacc
    from concourse.bass_utils import run_bass_kernel_spmd

    a = {k: np.ascontiguousarray(v) for k, v in inputs.items()}
    f32 = np.float32

    def columns(v):
        v = v.reshape(-1)
        n = -(-v.size // P)
        out = np.zeros((n * P,), v.dtype)
        out[:v.size] = v
        return out.reshape(n, P).T

    def in_tile(w):
        full = np.zeros((D_MODEL, P), w.dtype)
        full[:, :w.shape[1]] = w
        return full.reshape(KT, P, P).transpose(1, 0, 2).reshape(P, KT * P)

    w_in = a["w_in"][0]
    shift = 3 * WIDTH + 4 * 64 + 160
    starts = {"r": 0, "k": WIDTH, "v": 2 * WIDTH, "wd": 3 * WIDTH, "ad": 3 * WIDTH + 128, "gd": 3 * WIDTH + 256,
              "conv_value": shift, "conv_gate": shift + WIDTH}
    tiles = []

    def ffn(w1, w2):
        for f in range(FT):
            tiles.append(in_tile(w1[:, f * P:(f + 1) * P]))
            tiles.append(in_tile(w1[:, D_FF + f * P:D_FF + (f + 1) * P]))
        for f in range(FT):
            tiles.append(w2[f * P:(f + 1) * P, :])

    ffn(a["ffn1_w_in"][0], a["ffn1_w_out"][0])
    for what, j in PROJ:
        c0 = starts[what] + j * P
        c1 = min(c0 + P, shift) if what == "gd" else c0 + P
        tiles.append(in_tile(w_in[:, c0:c1]))
    for i in range(KT):
        k = (i + JT) % KT
        tiles.append(a["w_out"][0][k * P:(k + 1) * P, :])
    ffn(a["ffn2_w_in"][0], a["ffn2_w_out"][0])
    weights = np.stack(tiles)

    order = sorted(PAR, key=PAR.get)
    params = np.ascontiguousarray(np.concatenate([columns(a[name][0]) for name in order], axis=1))
    lora = np.ascontiguousarray(np.concatenate(
        [a["w2"][0].reshape(128, WIDTH), a["a2"][0].reshape(128, WIDTH), a["g2"][0, :128]], axis=1))
    gate_tail = np.ascontiguousarray(a["g2"][0, 128:])
    x_t = np.ascontiguousarray(a["x"][0].T.reshape(KT, P, SEQ).transpose(1, 0, 2).reshape(P, KT * SEQ))

    src, dst = np.arange(CHUNK)[:, None], np.arange(CHUNK)[None, :]
    tri = []
    for strict, whole in ((dst > src, dst >= src), (dst < src, dst <= src)):
        tri += [strict, whole, strict, whole]
    tri = np.concatenate(tri, axis=1).astype(f32)
    level = []
    for d in range(2):
        for m in range(LEVELS):
            row, colm = (src, dst) if d == 0 else (dst, src)
            same = row >> (m + 1) == colm >> (m + 1)
            level.append((src == dst) | same & ((row >> m) % 2 == 1) & ((colm >> m) % 2 == 0))
    level = np.concatenate(level, axis=1).astype(f32)
    arrays = {
        "x_t": x_t, "weights": weights, "params": params, "lora": lora, "gate_tail": gate_tail,
        "ident_c": np.eye(P, dtype=f32), "head_ones_c": np.kron(np.eye(2, dtype=f32), np.ones((64, 64), f32)),
        "tri_c": tri, "level_c": level,
    }
    nc = bacc.Bacc("TRN2", target_bir_lowering=False, num_devices=1)
    aps = {n: nc.dram_tensor(n + "_in", v.shape, mybir.dt.from_np(v.dtype), kind="ExternalInput").ap()
           for n, v in arrays.items()}
    out_t = nc.dram_tensor("out_t", (P, KT * SEQ), F32, kind="ExternalOutput").ap()
    encoder_block(nc, out_t=out_t, **aps)
    got = run_bass_kernel_spmd(nc, [{n + "_in": v for n, v in arrays.items()}], core_ids=[0])
    y = got.results[0]["out_t"].reshape(P, KT, SEQ)
    return y.transpose(1, 0, 2).reshape(D_MODEL, SEQ).T[None]
```
